# Optimizing a Trainium2 kernel written in Bass

```python
import jax, jax.numpy as jnp
from jax import lax
import numpy as np

D_MODEL = 2048
BATCH = 1
SEQ = 256
DEPTH = 2

GRID_W = 64
N_MEM = 256
EPS = 1e-6
RW_HEADS = 16
RW_HEAD = 64
RW_WIDTH = RW_HEADS * RW_HEAD
W_LORA = 64
A_LORA = 64
V_LORA = 32
G_LORA = 160
RW_GN_EPS = 64e-5
AT_HEADS = 16
AT_KV_HEADS = 4
AT_HEAD = 64
AT_Q = AT_HEADS * AT_HEAD
AT_KV = AT_KV_HEADS * AT_HEAD
Q_BLOCK = 128
ROPE_THETA = 10000.0
X_HEADS = 4
X_HEAD = 128
X_WIDTH = X_HEADS * X_HEAD
D_FF = -(-8 * D_MODEL // (3 * 256)) * 256
RW_COLS = 3 * RW_WIDTH + 2 * W_LORA + 2 * A_LORA + G_LORA
AT_COLS = AT_Q + 2 * AT_KV
GATE_COLS = 2 * D_MODEL
IN_COLS = RW_COLS + AT_COLS + GATE_COLS

kernel_name = "bidir_rwkv7_axial_gqa_hybrid"

def rmsnorm(x, g):
    xf = x.astype(jnp.float32)
    y = xf * lax.rsqrt(jnp.mean(xf * xf, axis=-1, keepdims=True) + EPS)
    return (y * g.astype(jnp.float32)).astype(x.dtype)

def centred_shift(z, mu_prev, mu_next):
    zp = jnp.pad(z, ((0, 0), (1, 0), (0, 0)))[:, :-1]
    zn = jnp.pad(z, ((0, 0), (0, 1), (0, 0)))[:, 1:]
    return z + mu_prev * (zp - z) + mu_next * (zn - z)

def rwkv7_step(state, inp):
    r_t, w_t, k_t, v_t, a_t, b_t = inp
    sa = jnp.einsum('dbhij,dbhj->dbhi', state, a_t)
    state = (state * w_t[..., None, :] + sa[..., :, None] * b_t[..., None, :]
             + v_t[..., :, None] * k_t[..., None, :])
    y = jnp.einsum('dbhij,dbhj->dbhi', state, r_t)
    return state, y

def rwkv7_branch(z, mu_prev, mu_next, w0, w_up, a0, a_up, g_up, k_k, k_a, r_k,
                 ln_w, ln_b, v_first, v_mix):
    B, S, _ = z.shape
    f32 = jnp.float32
    z = centred_shift(z, mu_prev, mu_next)
    o = 0
    r = z[..., o:o + RW_WIDTH]; o += RW_WIDTH
    k = z[..., o:o + RW_WIDTH]; o += RW_WIDTH
    v = z[..., o:o + RW_WIDTH]; o += RW_WIDTH
    wd = z[..., o:o + 2 * W_LORA].reshape(B, S, 2, W_LORA); o += 2 * W_LORA
    ad = z[..., o:o + 2 * A_LORA].reshape(B, S, 2, A_LORA); o += 2 * A_LORA
    gd = z[..., o:o + G_LORA]
    if v_mix is None:
        v_first = v
    else:
        v0, v_down, v_up = v_mix
        v = v + (v_first - v) * jax.nn.sigmoid(v0 + (v @ v_down) @ v_up)
    w_log = -jax.nn.softplus(-(w0 + jnp.einsum('bsdr,drc->bsdc', jnp.tanh(wd), w_up)).astype(f32)) - 0.5
    decay = jnp.exp(-jnp.exp(w_log))
    a = jax.nn.sigmoid((a0 + jnp.einsum('bsdr,drc->bsdc', ad, a_up)).astype(f32))
    g = jax.nn.sigmoid(gd) @ g_up
    kf = k.astype(f32)
    kk = (kf * k_k).reshape(B, S, RW_HEADS, RW_HEAD)
    kk = kk / jnp.maximum(jnp.linalg.norm(kk, axis=-1, keepdims=True), 1e-12)
    kd = kf[:, :, None, :] * (1.0 + (a - 1.0) * k_a)

    hv = lambda t: t.reshape(B, S, 2, RW_HEADS, RW_HEAD)
    two = lambda t: jnp.broadcast_to(t.reshape(B, S, 1, RW_HEADS, RW_HEAD), (B, S, 2, RW_HEADS, RW_HEAD))

    def time_major(t):
        fwd = t[:, :, 0]
        bwd = jnp.flip(t[:, :, 1], axis=1)
        return jnp.transpose(jnp.stack([fwd, bwd], 0), (2, 0, 1, 3, 4))

    rr = two(r.astype(f32))
    vv = two(v.astype(f32))
    kk2 = two(kk)
    kd_h = hv(kd)
    seqs = (time_major(rr), time_major(hv(decay)), time_major(kd_h), time_major(vv),
            time_major(-kk2), time_major(kk2 * hv(a)))
    state0 = jnp.zeros((2, B, RW_HEADS, RW_HEAD, RW_HEAD), f32)
    _, y = lax.scan(rwkv7_step, state0, seqs)
    y = y[:, 0] + jnp.flip(y[:, 1], axis=0)
    y = jnp.transpose(y, (1, 0, 2, 3))
    mu = jnp.mean(y, axis=-1, keepdims=True)
    var = jnp.mean(jnp.square(y - mu), axis=-1, keepdims=True)
    y = ((y - mu) * lax.rsqrt(var + RW_GN_EPS)).reshape(B, S, RW_WIDTH) * ln_w + ln_b
    bonus = jnp.sum(rr * kd_h * r_k, axis=-1, keepdims=True) * vv
    y = y + jnp.sum(bonus, axis=2).reshape(B, S, RW_WIDTH)
    y = y * g
    return y.astype(z.dtype), v_first

def axial_rope(S):
    rows = S // GRID_W
    row = jnp.repeat(jnp.arange(rows), GRID_W)
    col = jnp.tile(jnp.arange(GRID_W), rows)
    n_freq = AT_HEAD // 4
    inv = ROPE_THETA ** (-jnp.arange(n_freq, dtype=jnp.float32) / n_freq)
    ang = jnp.stack([row, col], -1).astype(jnp.float32)[..., None] * inv
    return jnp.cos(ang), jnp.sin(ang)

def apply_rope(t, cos, sin):
    B, S, H, _ = t.shape
    tf = t.astype(jnp.float32).reshape(B, S, H, 2, 2, AT_HEAD // 4)
    t1, t2 = tf[..., 0, :], tf[..., 1, :]
    c = cos[None, :, None]
    s = sin[None, :, None]
    out = jnp.stack([t1 * c - t2 * s, t2 * c + t1 * s], axis=-2)
    return out.reshape(B, S, H, AT_HEAD).astype(t.dtype)

def axial_gqa_branch(z, q_norm, k_norm):
    B, S, _ = z.shape
    q = z[..., :AT_Q].reshape(B, S, AT_HEADS, AT_HEAD)
    k = z[..., AT_Q:AT_Q + AT_KV].reshape(B, S, AT_KV_HEADS, AT_HEAD)
    v = z[..., AT_Q + AT_KV:].reshape(B, S, AT_KV_HEADS, AT_HEAD)
    cos, sin = axial_rope(S)
    q = apply_rope(rmsnorm(q, q_norm), cos, sin)
    k = apply_rope(rmsnorm(k, k_norm), cos, sin)
    G = AT_HEADS // AT_KV_HEADS
    nb = S // Q_BLOCK
    qb = q.reshape(B, nb, Q_BLOCK, AT_KV_HEADS, G, AT_HEAD).transpose(1, 0, 2, 3, 4, 5)
    scale = AT_HEAD ** -0.5

    def block(qi):
        s = jnp.einsum('bqkgd,bskd->bkgqs', qi, k, preferred_element_type=jnp.float32) * scale
        p = jax.nn.softmax(s, axis=-1).astype(v.dtype)
        return jnp.einsum('bkgqs,bskd->bqkgd', p, v)

    o = lax.map(block, qb)
    return o.transpose(1, 0, 2, 3, 4, 5).reshape(B, S, AT_Q)

def memory_cross_attention(h, mem_n, wq, wkv, wo):
    B, S, _ = h.shape
    M = mem_n.shape[1]
    q = (h @ wq).reshape(B, S, X_HEADS, X_HEAD)
    kv = (mem_n @ wkv).reshape(B, M, 2, X_HEADS, X_HEAD)
    s = jnp.einsum('bshd,bmhd->bhsm', q, kv[:, :, 0], preferred_element_type=jnp.float32) * (X_HEAD ** -0.5)
    p = jax.nn.softmax(s, axis=-1).astype(h.dtype)
    o = jnp.einsum('bhsm,bmhd->bshd', p, kv[:, :, 1]).reshape(B, S, X_WIDTH)
    return o @ wo

def swiglu(h, wg, wu, wd):
    return (jax.nn.silu(h @ wg) * (h @ wu)) @ wd

def setup_inputs(seed: int = 0) -> dict:
    key = jax.random.key(seed)
    keys = list(jax.random.split(key, 64))
    idx = [0]

    def nk():
        k = keys[idx[0]]
        idx[0] += 1
        return k

    f32 = jnp.float32
    nrm = lambda shape, scale: jax.random.normal(nk(), shape, f32) * scale
    gain = lambda shape: 1.0 + nrm(shape, 0.02)
    unif = lambda shape, lo, hi: jax.random.uniform(nk(), shape, f32, lo, hi)
    L, D = DEPTH, D_MODEL
    return {
        "x": nrm((BATCH, SEQ, D), 1.0),
        "mem": nrm((BATCH, N_MEM, D), 1.0),
        "n_mix_pre": gain((L, D)),
        "n_mix_post": gain((L, D)),
        "n_x_pre": gain((L, D)),
        "n_x_post": gain((L, D)),
        "n_ffn_pre": gain((L, D)),
        "n_ffn_post": gain((L, D)),
        "n_mem": gain((L, D)),
        "w_in": nrm((L, D, IN_COLS), D ** -0.5),
        "rw_mu_prev": unif((L, RW_COLS), 0.0, 0.5),
        "rw_mu_next": unif((L, RW_COLS), 0.0, 0.5),
        "rw_w0": unif((L, 2, RW_WIDTH), -6.5, -1.5),
        "rw_w_up": nrm((L, 2, W_LORA, RW_WIDTH), 0.1 * W_LORA ** -0.5),
        "rw_a0": nrm((L, 2, RW_WIDTH), 0.1),
        "rw_a_up": nrm((L, 2, A_LORA, RW_WIDTH), 0.1 * A_LORA ** -0.5),
        "rw_g_up": nrm((L, G_LORA, RW_WIDTH), G_LORA ** -0.5),
        "rw_v0": 1.0 + nrm((L - 1, RW_WIDTH), 0.1),
        "rw_v_down": nrm((L - 1, RW_WIDTH, V_LORA), RW_WIDTH ** -0.5),
        "rw_v_up": nrm((L - 1, V_LORA, RW_WIDTH), 0.1 * V_LORA ** -0.5),
        "rw_k_k": 0.85 + nrm((L, RW_WIDTH), 0.02),
        "rw_k_a": 1.0 + nrm((L, RW_WIDTH), 0.02),
        "rw_r_k": nrm((L, RW_HEADS, RW_HEAD), 0.1),
        "rw_ln_w": gain((L, RW_WIDTH)),
        "rw_ln_b": nrm((L, RW_WIDTH), 0.02),
        "w_rw_out": nrm((L, RW_WIDTH, D), RW_WIDTH ** -0.5),
        "at_q_norm": gain((L, AT_HEAD)),
        "at_k_norm": gain((L, AT_HEAD)),
        "w_at_out": nrm((L, AT_Q, D), AT_Q ** -0.5),
        "w_o": nrm((L, D, D), D ** -0.5),
        "x_wq": nrm((L, D, X_WIDTH), D ** -0.5),
        "x_wkv": nrm((L, D, 2 * X_WIDTH), D ** -0.5),
        "x_wo": nrm((L, X_WIDTH, D), X_WIDTH ** -0.5),
        "ffn_wg": nrm((L, D, D_FF), D ** -0.5),
        "ffn_wu": nrm((L, D, D_FF), D ** -0.5),
        "ffn_wd": nrm((L, D_FF, D), D_FF ** -0.5),
    }

def reference(x, mem, n_mix_pre, n_mix_post, n_x_pre, n_x_post, n_ffn_pre, n_ffn_post,
              n_mem, w_in, rw_mu_prev, rw_mu_next, rw_w0, rw_w_up, rw_a0, rw_a_up,
              rw_g_up, rw_v0, rw_v_down, rw_v_up, rw_k_k, rw_k_a, rw_r_k, rw_ln_w,
              rw_ln_b, w_rw_out, at_q_norm, at_k_norm, w_at_out, w_o, x_wq, x_wkv,
              x_wo, ffn_wg, ffn_wu, ffn_wd):
    v_first = None
    for l in range(DEPTH):
        h = rmsnorm(x, n_mix_pre[l])
        z = h @ w_in[l]
        z_rw = z[..., :RW_COLS]
        z_at = z[..., RW_COLS:RW_COLS + AT_COLS]
        z_g = z[..., RW_COLS + AT_COLS:]
        v_mix = None if l == 0 else (rw_v0[l - 1], rw_v_down[l - 1], rw_v_up[l - 1])
        y_rw, v_first = rwkv7_branch(z_rw, rw_mu_prev[l], rw_mu_next[l], rw_w0[l], rw_w_up[l],
                                     rw_a0[l], rw_a_up[l], rw_g_up[l], rw_k_k[l], rw_k_a[l],
                                     rw_r_k[l], rw_ln_w[l], rw_ln_b[l], v_first, v_mix)
        y_at = axial_gqa_branch(z_at, at_q_norm[l], at_k_norm[l])
        gate = jax.nn.sigmoid(z_g.astype(jnp.float32)).astype(x.dtype)
        merged = (gate[..., :D_MODEL] * (y_rw @ w_rw_out[l])
                  + gate[..., D_MODEL:] * (y_at @ w_at_out[l]))
        x = x + rmsnorm(merged @ w_o[l], n_mix_post[l])
        h = rmsnorm(x, n_x_pre[l])
        c = memory_cross_attention(h, rmsnorm(mem, n_mem[l]), x_wq[l], x_wkv[l], x_wo[l])
        x = x + rmsnorm(c, n_x_post[l])
        h = rmsnorm(x, n_ffn_pre[l])
        x = x + rmsnorm(swiglu(h, ffn_wg[l], ffn_wu[l], ffn_wd[l]), n_ffn_post[l])
    return x


_drawn_inputs = setup_inputs


def setup_inputs(seed=0):
    import zlib

    import numpy as np

    out = dict(_drawn_inputs(seed))
    spreads = {}
    factors = {'n_mix_post': 2.73,
     'n_x_pre': 3.366,
     'n_x_post': 2.975,
     'n_ffn_pre': 2.812,
     'n_ffn_post': 4.078,
     'rw_w_up': 8.0,
     'rw_v0': 3.665,
     'rw_v_down': 5.097,
     'rw_v_up': 5.215,
     'rw_k_k': 2.706,
     'rw_ln_w': 2.915,
     'rw_ln_b': 2.767,
     'at_q_norm': 8.0,
     'at_k_norm': 8.0}
    for name, (base, spread) in spreads.items():
        noise = np.random.default_rng([zlib.crc32(name.encode()), seed]).standard_normal(out[name].shape)
        drawn = base * np.exp(spread * noise) if base else spread * noise
        out[name] = __import__('jax').numpy.asarray(drawn.astype(out[name].dtype))
    for name, factor in factors.items():
        out[name] = (out[name] * factor).astype(out[name].dtype)
    return out
```

```python
from contextlib import ExitStack, contextmanager

import numpy as np

import concourse.bass as bass
from concourse import mybir

F32 = mybir.dt.float32
ALU = mybir.AluOpType
ACT = mybir.ActivationFunctionType
AX_X = mybir.AxisListType.X

P = 128
D_MODEL, SEQ, DEPTH, N_MEM = 2048, 256, 2, 256
GRID_W = 64
EPS = 1e-6
RW_HEADS, HEAD = 16, 64
RW_WIDTH = RW_HEADS * HEAD
W_LORA = A_LORA = 64
V_LORA, G_LORA = 32, 160
GN_EPS = 64e-5
AT_HEADS, AT_KV_HEADS = 16, 4
AT_Q, AT_KV = AT_HEADS * HEAD, AT_KV_HEADS * HEAD
ROPE_THETA = 10000.0
X_HEADS, X_HEAD = 4, 128
X_WIDTH = X_HEADS * X_HEAD
D_FF = -(-8 * D_MODEL // (3 * 256)) * 256
LORA_COLS = 2 * W_LORA + 2 * A_LORA + G_LORA
RW_COLS = 3 * RW_WIDTH + LORA_COLS
AT_COLS = AT_Q + 2 * AT_KV
DECAY = float(np.exp(-0.5))

TOK = SEQ // P
KD = D_MODEL // P
UNIT = 512
SLAB_K = 2
RING = 4
PAIRS = RW_HEADS // 2
CHUNK = 64
NCH = SEQ // CHUNK
FF_PARTS = (16, 16, 12)
LORA_W = (P, P, P, LORA_COLS - 3 * P)

PARAM_ROWS = [
    [("n_mix_pre", KD), ("n_x_pre", KD), ("n_ffn_pre", KD), ("n_mem", KD), ("rw_mu_prev", 28), ("rw_mu_next", 28)],
    [("rw_w0", 2 * PAIRS), ("rw_a0", 2 * PAIRS), ("rw_k_k", PAIRS), ("rw_k_a", PAIRS), ("rw_r_k", PAIRS),
     ("rw_ln_w", PAIRS), ("rw_ln_b", PAIRS), ("rw_v0", PAIRS), ("qk_norm", 5)],
]
PCOL = {}
_n = 0
for _g in PARAM_ROWS:
    for _name, _rows in _g:
        PCOL[_name] = _n
        _n += _rows
GROUP_ROWS = [sum(r for _, r in g) for g in PARAM_ROWS]
N_COLS = sum(GROUP_ROWS)

CONST = {}
_n = 0
for _name, _w in (("ident", P), ("head_ones", P), ("rot", P), ("mask", 2 * 2 * P), ("in16", P), ("in32", P),
                  ("in64", P), ("cos", SEQ), ("sin", SEQ), ("carry", SEQ)):
    CONST[_name] = (_n, _w)
    _n += _w
N_CONST = _n


def shape_constants():
    out = np.zeros((P, N_CONST), np.float32)

    def put(name, a):
        o, w = CONST[name]
        out[:, o:o + w] = a.reshape(P, w)

    r = np.arange(P)
    put("ident", np.eye(P))
    head = r[:, None] // HEAD == r[None, :] // HEAD
    put("head_ones", head)
    rot = np.zeros((P, P))
    for m in range(P):
        if m % 32 < 16:
            rot[m + 16, m] = -1.0
        else:
            rot[m - 16, m] = 1.0
    put("rot", rot)
    s, t = r[:, None] % HEAD, r[None, :] % HEAD
    mask = np.stack([head & (s < t), head & (s <= t), head & (s > t), head & (s >= t)], axis=1)
    put("mask", mask)
    put("in16", r[:, None] // 16 == r[None, :] // 16)
    for n in (32, 64):
        put(f"in{n}", (r[:, None] // n == r[None, :] // n) & (r[:, None] // (n // 2) != r[None, :] // (n // 2)))
    n_freq = HEAD // 4
    inv = np.float32(ROPE_THETA) ** (-np.arange(n_freq, dtype=np.float32) / np.float32(n_freq))
    tok = np.arange(SEQ)
    pos = np.stack([tok // GRID_W, tok % GRID_W]).astype(np.float32)
    ang = pos[(r % HEAD) // 32] * inv[r % 16][:, None]
    put("cos", np.cos(ang))
    put("sin", np.sin(ang))
    put("carry", np.broadcast_to((tok % CHUNK != 0).astype(np.float32), (P, SEQ)))
    return out


class Tally:

    def __init__(self, sem, scale=1):
        self.sem, self.count, self.loop, self.scale = sem, 0, None, scale

    def at(self, back=0):
        n = (self.count - back) * self.scale
        return n if self.loop is None else self.loop[0] * (self.loop[1] * self.scale) + n

    def next(self, n=1):
        self.count += n
        return self.at()


@contextmanager
def repeat(eng, times, per):
    start = {t: t.count for t in per}
    with eng.Fori(0, times) as i:
        for t, n in per.items():
            t.loop = (i, n)
        yield i
        for t, n in per.items():
            assert t.count - start[t] == n, (t.sem, t.count - start[t], n)
    for t, n in per.items():
        t.loop = None
        t.count = start[t] + times * n


def encoder_kernel(nc, a, out):
    with ExitStack() as ctx:
        def sb(name, shape):
            return ctx.enter_context(nc.sbuf_tensor("sb_" + name, shape, F32))

        def sem(name):
            return ctx.enter_context(nc.semaphore(name))

        x = sb("x", [P, TOK, D_MODEL])
        tok_buf = sb("tok_buf", [P, TOK, D_MODEL])
        opT = sb("opT", [P, KD, SEQ])
        ring = sb("ring", [P, RING, SLAB_K, UNIT])
        rows = sb("rows", [P, 2, TOK, UNIT])
        zs = sb("zs", [P, 28, SEQ])
        y_rw = zs[:, 0:PAIRS, :]
        v_first = sb("v_first", [P, PAIRS, SEQ])
        y_at = sb("y_at", [P, PAIRS, SEQ])
        memk = sb("memk", [P, X_HEADS, N_MEM])
        memv = sb("memv", [P, TOK, X_WIDTH])
        const = sb("const", [P, N_CONST])
        cols = sb("cols", [P, DEPTH, N_COLS])
        cols_mix = sb("cols_mix", [P, DEPTH, 28])
        cols_ka = sb("cols_ka", [P, DEPTH, PAIRS])
        vdown = sb("vdown", [P, PAIRS, V_LORA])
        stat = sb("stat", [P, 64])
        lora_w = sb("lora_w", [P, 4, P])
        lora_in = sb("lora_in", [P, 3, 2, SEQ])
        v_low = lora_in[32:32 + V_LORA, 2, 1, :]
        arena = sb("arena", [P, 14336])

        def view(off, *shape):
            n = int(np.prod(shape))
            names = "abcd"[:len(shape)]
            v = arena[:, off:off + n]
            if len(shape) == 1:
                return v
            return v.rearrange(f"p ({' '.join(names)}) -> p {' '.join(names)}", **dict(zip(names, shape)))

        qk = view(0, 5, 2, SEQ)
        k_both = view(2560, AT_KV_HEADS, SEQ)
        v_at = view(3584, TOK, AT_KV)
        prob = view(4096, 8, SEQ)
        probT = view(6144, 4, 2 * SEQ)
        q_now = view(8192, 2, SEQ)
        k_now = view(8704, SEQ)
        v_now = view(8960, TOK, HEAD)
        sq_tmp = view(9216, 2, SEQ)
        rt_tmp = view(9728, 2, SEQ)
        qn_tmp = view(10240, 2, SEQ)
        x_q = view(10752, X_HEADS, SEQ)
        x_y = view(11776, X_HEADS, SEQ)
        AR = view(0, 2, NCH, 2, P)
        KB = view(2048, 2, NCH, 2, P)
        KBt = rows[:, :, :, :].rearrange("p a b c -> p (a b c)").rearrange("p (d c w n) -> p d c w n", d=2, c=NCH, w=2)
        GT = view(4096, 2, NCH, 4, P)
        XA = view(8192, 2, NCH, P)
        XTA = view(9216, 2, NCH, P)
        XB = view(10240, 2, NCH, P)
        XTB = view(11264, 2, NCH, P)
        EE = view(12288, 2, NCH, P)
        OFF = {32: view(13312, 2, NCH, P),
               64: zs[:, 24:28, :].rearrange("p a b -> p (a b)").rearrange("p (d c n) -> p d c n", d=2, c=NCH)}
        tb = tok_buf[:, :, :].rearrange("p a b -> p (a b)")

        def tview(off, *shape):
            n = int(np.prod(shape))
            names = "abcd"[:len(shape)]
            v = tb[:, off:off + n]
            if len(shape) == 1:
                return v
            return v.rearrange(f"p ({' '.join(names)}) -> p {' '.join(names)}", **dict(zip(names, shape)))

        sig = tview(0, 4, SEQ)
        inc = tview(1024, 2, SEQ)
        exc = tview(1536, 2, SEQ)
        p_inc = tview(2048, 2, SEQ)
        p_inv = tview(2560, 2, SEQ)
        p_exc = tview(3072, 2, SEQ)
        kd = tview(3584, 2, SEQ)
        v_cur = sb("v_cur", [P, SEQ])
        tmp = sb("tmp", [P, SEQ])
        tmp2 = sb("tmp2", [P, SEQ])
        g_cur = sb("g_cur", [P, SEQ])
        Vc = sb("Vc", [P, NCH, HEAD])
        Yc = sb("Yc", [P, NCH, HEAD])
        Wc = sb("Wc", [P, 2, HEAD])
        Uc = sb("Uc", [P, 2, HEAD])
        St = sb("St", [P, 2, HEAD])
        prow = view(0, DEPTH, 2, P)
        junk = view(0, D_MODEL)
        gain_row = view(2048, D_MODEL)
        gate_a = view(4096, TOK, UNIT)
        gate_b = view(5120, TOK, UNIT)
        hidT = view(4096, 16, SEQ)

        acc = ctx.enter_context(nc.psum_tensor("acc", [P, 2, TOK, UNIT], F32))
        work = ctx.enter_context(nc.psum_tensor("work", [P, 4, 512], F32))

        def cst(name):
            o, w = CONST[name]
            return const[:, o:o + w]

        ident, head_ones, rot = cst("ident"), cst("head_ones"), cst("rot")
        mask = cst("mask").rearrange("p (d n) -> p d n", d=2)

        def col(l, name, j=0, n=1):
            return cols[:, l, PCOL[name] + j:PCOL[name] + j + n]

        def colv(l, name, n):
            return cols[:, l, PCOL[name]:PCOL[name] + n]

        s_const = sem("constants_landed")
        s_rows_zero = sem("param_rows_zeroed")
        s_rows = sem("param_rows_landed")
        s_x = sem("x_landed")
        s_mem = sem("mem_landed")
        s_mem_free = sem("tok_buf_free_for_mem")
        s_gain = sem("gain_row_landed")
        s_gain_free = sem("gain_row_free")
        s_lw = sem("lora_weights_landed")
        s_lw_free = sem("lora_weights_free")
        s_land = [sem(f"slab_landed{i}") for i in range(RING)]
        s_used = sem("slab_used")
        s_asked = sem("branch_weights_asked_for")
        s_emptied = sem("unit_emptied")
        s_branch = sem("branch_unit_emptied")
        s_rows_free = sem("unit_rows_transposed")
        s_full = sem("work_bank_full")
        s_drained = sem("work_bank_drained")
        s_dve = sem("vector_step")
        s_for_pe = sem("vector_result_for_tensor")
        s_for_act = sem("vector_result_for_scalar")
        s_from_act = sem("scalar_result_for_vector")
        s_out = sem("output_stored")

        w_in = a["w_in"]
        C_LORA, C_Q = 3 * RW_WIDTH, RW_COLS
        C_KV, C_G = RW_COLS + AT_Q, RW_COLS + AT_COLS

        def slabs_of(w2d, ncols):
            return w2d.rearrange("(s t p) (u n) -> u s p t n", t=SLAB_K, p=P, n=ncols)

        rows_landed = Tally(s_rows, 16)

        block = ctx.enter_context(nc.Block())

        @block.sync
        def _(sp):
            slab = Tally(s_used)
            sp.dma_start(const[:, :], a["shape_constants"]).then_inc(s_const, 16)
            sp.dma_start(x[:, :, :], a["x"].rearrange("b (t p) d -> p (b t) d", p=P)).then_inc(s_x, 16)

            def load(src, note=False):
                slot = slab.count % RING
                if slab.count >= RING:
                    sp.wait_ge(s_used, slab.at(RING - 1))
                    if note:
                        sp.sem_inc(s_asked, 1)
                slab.next()
                for dst, part in src(ring[:, slot]):
                    sp.dma_start(dst, part).then_inc(s_land[slot], 32 // len(src(ring[:, slot])))

            def whole(part):
                w = part.shape[-1]
                return lambda r: [(r[:, :, 0:w], part)]

            for l in range(DEPTH):
                mem_w = slabs_of(a["x_wkv"][l], UNIT)
                for u in range(2):
                    for s in range(8):
                        load(whole(mem_w[u, s]))
                rkv = slabs_of(w_in[l][:, 0:3 * RW_WIDTH], UNIT)
                with repeat(sp, 3, {slab: 16}) as i:
                    for j in range(2):
                        v = rkv.rearrange("(i j) s p t n -> j i s p t n", j=2)[j]
                        for s in range(8):
                            load(whole(v[i, s]))
                lora = slabs_of(w_in[l][:, C_LORA:C_LORA + LORA_COLS], LORA_COLS)
                for s in range(8):
                    load(whole(lora[0, s]))
                qkv = slabs_of(w_in[l][:, C_Q:C_Q + AT_COLS], UNIT)
                for u in range(3):
                    for s in range(8):
                        load(whole(qkv[u, s]))
                gates = slabs_of(w_in[l][:, C_G:C_G + 2 * D_MODEL], UNIT)
                wr, wa = slabs_of(a["w_rw_out"][l], UNIT), slabs_of(a["w_at_out"][l], UNIT)
                with repeat(sp, 4, {slab: 24}) as i:
                    for s in range(8):
                        load(whole(gates[0:4][i, s]))
                    for s in range(8):
                        load(whole(gates[4:8][i, s]))
                    for s in range(4):
                        load(whole(wr[i, s]), note=s == 0)
                    for s in range(4):
                        load(whole(wa[i, s]))
                wo = slabs_of(a["w_o"][l], UNIT)
                with repeat(sp, 4, {slab: 8}) as i:
                    for s in range(8):
                        load(whole(wo[i, s]))
                xq = slabs_of(a["x_wq"][l], UNIT)
                for s in range(8):
                    load(whole(xq[0, s]))
                xo = slabs_of(a["x_wo"][l], UNIT)
                for u in range(4):
                    for s in range(2):
                        load(whole(xo[u, s]))
                wg, wu = slabs_of(a["ffn_wg"][l], 256), slabs_of(a["ffn_wu"][l], 256)
                t0 = 0
                for tiles in FF_PARTS:
                    n = tiles // 2
                    g_v = wg[t0 // 2:t0 // 2 + n].rearrange("(i j) s p t n -> j i s p t n", j=2)
                    u_v = wu[t0 // 2:t0 // 2 + n].rearrange("(i j) s p t n -> j i s p t n", j=2)
                    with repeat(sp, n // 2, {slab: 16}) as i:
                        for j in range(2):
                            for s in range(8):
                                load(lambda r, j=j, s=s: [(r[:, :, 0:256], g_v[j][i, s]), (r[:, :, 256:512], u_v[j][i, s])])
                    wd = slabs_of(a["ffn_wd"][l][t0 * P:(t0 + tiles) * P, :], UNIT)
                    wd_v = wd.rearrange("(i j) s p t n -> j i s p t n", j=2)
                    with repeat(sp, 2, {slab: tiles}) as i:
                        for j in range(2):
                            for s in range(tiles // 2):
                                load(whole(wd_v[j][i, s]))
                    t0 += tiles
            sp.wait_ge(s_out, 1)
            sp.dma_start(out.rearrange("b (t p) d -> p (b t) d", p=P), x[:, :, :]).then_inc(s_x, 16)
            sp.wait_ge(s_x, 32)

        @block.gpsimd
        def _(pool):
            pool.wait_ge(s_rows_zero, 1)
            for l in range(DEPTH):
                for g, group in enumerate(PARAM_ROWS):
                    r0 = 0
                    for name, n in group:
                        if name == "qk_norm":
                            srcs = []
                            for j in range(n):
                                g_src = a["at_q_norm" if j < 4 else "at_k_norm"][l:l + 1, :]
                                for h in range(2):
                                    pool.dma_start(prow[r0 + j:r0 + j + 1, l, g, h * HEAD:(h + 1) * HEAD],
                                                   g_src).then_inc(s_rows, 16)
                                    rows_landed.next()
                            r0 += n
                            continue
                        if name == "rw_v0":
                            if l == 0:
                                r0 += n
                                continue
                            src = a[name][l - 1]
                        elif name in ("rw_w0", "rw_a0"):
                            src = a[name][l].rearrange("d c -> (d c)")
                        elif name == "rw_r_k":
                            src = a[name][l].rearrange("h c -> (h c)")
                        else:
                            src = a[name][l]
                        full = src.shape[0] // P
                        pool.dma_start(prow[r0:r0 + full, l, g, :],
                                       src[0:full * P].rearrange("(r c) -> r c", c=P)).then_inc(s_rows, 16)
                        rows_landed.next()
                        rest = src.shape[0] - full * P
                        if rest:
                            pool.dma_start(prow[r0 + full:r0 + full + 1, l, g, 0:rest],
                                           src[full * P:].rearrange("(r c) -> r c", r=1)).then_inc(s_rows, 16)
                            rows_landed.next()
                        r0 += n
            pool.dma_start(vdown[:, :, :], a["rw_v_down"][0].rearrange("(t p) n -> p t n", p=P)).then_inc(s_rows, 16)
            rows_landed.next()
            landed = Tally(s_lw, 16)
            gain = Tally(s_gain_free)
            for l in range(DEPTH):
                pool.wait_ge(s_mem_free, l + 1)
                pool.dma_start(tok_buf[:, :, :], a["mem"].rearrange("b (t p) d -> p (b t) d", p=P)).then_inc(s_mem, 16)
                n_lw = 7 if l else 6
                with repeat(pool, PAIRS, {landed: n_lw}) as i:
                    pool.wait_ge(s_lw_free, i + (l * (PAIRS + 1) + 1))
                    for d in range(2):
                        w_v = a["rw_w_up"][l, d].rearrange("r (i c) -> i r c", c=P)
                        a_v = a["rw_a_up"][l, d].rearrange("r (i c) -> i r c", c=P)
                        pool.dma_start(lora_w[d * 64:(d + 1) * 64, 0, :], w_v[i]).then_inc(s_lw, 16)
                        pool.dma_start(lora_w[d * 64:(d + 1) * 64, 1, :], a_v[i]).then_inc(s_lw, 16)
                        landed.next(2)
                    g_v = a["rw_g_up"][l].rearrange("r (i c) -> i r c", c=P)
                    pool.dma_start(lora_w[:, 2, :], g_v[i, 0:P]).then_inc(s_lw, 16)
                    pool.dma_start(lora_w[0:32, 3, :], g_v[i, P:G_LORA]).then_inc(s_lw, 16)
                    landed.next(2)
                    if l:
                        v_v = a["rw_v_up"][l - 1].rearrange("r (i c) -> i r c", c=P)
                        pool.dma_start(lora_w[32:32 + V_LORA, 3, :], v_v[i]).then_inc(s_lw, 16)
                        landed.next()
                for name in ("n_mix_post", "n_x_post", "n_ffn_post"):
                    pool.wait_ge(s_gain_free, gain.next())
                    pool.dma_start(gain_row, a[name][l].partition_broadcast(P)).then_inc(s_gain, 16)

        @block.tensor
        def _(pe):
            slab = Tally(s_used)
            emptied = Tally(s_emptied)
            branch = Tally(s_branch)
            full = Tally(s_full)
            for_pe = Tally(s_for_pe)
            lw = Tally(s_lw, 16)

            def unit(ub, nslab, operand, k0=0, width=UNIT, wait=True, between=None):
                if wait:
                    if emptied.count >= 2:
                        pe.wait_ge(s_emptied, emptied.at(1))
                    emptied.next()
                for s in range(nslab):
                    slot, use = slab.count % RING, slab.count // RING + 1
                    val = 32 * use if slab.loop is None else slab.loop[0] * (slab.loop[1] // RING * 32) + 32 * use
                    slab.next()
                    pe.wait_ge(s_land[slot], val)
                    for t in range(SLAB_K):
                        for tok in range(TOK):
                            k = SLAB_K * s + t
                            last = nc.tensor.matmul(acc[:, ub, tok, 0:width], operand[:, k0 + k, tok * P:(tok + 1) * P],
                                                    ring[:, slot, t, 0:width], start=k == 0, stop=k == SLAB_K * nslab - 1)
                    last.then_inc(s_used, 1)
                    if between and s == nslab // 2 - 1:
                        between()

            def settle():
                if emptied.count:
                    pe.wait_ge(s_emptied, emptied.at())

            def fill(products, aligned=False):
                b = full.count % 4
                if full.count >= 4:
                    pe.wait_ge(s_drained, full.at(3))
                last = products(work[:, b, :])
                n = 1 + (-(full.count + 1) % 4 if aligned else 0)
                last.then_inc(s_full, n)
                full.next(n)
                return full.at()

            def have(n):
                pe.wait_ge(s_drained, n)

            def transpose_unit(ub, tiles, lag, aligned=False):
                pe.wait_ge(s_emptied, emptied.at(lag))
                for b0 in range(0, len(tiles), 2):
                    def go(bank):
                        for j, w in enumerate(tiles[b0:b0 + 2]):
                            for tok in range(TOK):
                                c0 = (b0 + j) * P
                                last = nc.tensor.transpose(bank[0:w, j * SEQ + tok * P:j * SEQ + (tok + 1) * P],
                                                           rows[:, ub, tok, c0:c0 + w], ident)
                        return last
                    fill(go, aligned and b0 + 2 >= len(tiles))

            def transpose_tok(n_src=TOK):
                for tok in range(TOK):
                    pe.wait_ge(s_for_pe, for_pe.next())
                    for g in range(KD // 4):
                        def go(bank):
                            for j in range(4):
                                k = 4 * g + j
                                last = nc.tensor.transpose(bank[:, j * P:(j + 1) * P], tok_buf[:, tok, k * P:(k + 1) * P], ident)
                            return last
                        n = fill(go)
                have(n)
                settle()

            def softmax_turn():
                for b in range(4):
                    def go(bank):
                        for st in range(2):
                            for qt in range(2):
                                last = nc.tensor.transpose(bank[:, st * SEQ + qt * P:st * SEQ + (qt + 1) * P],
                                                           prob[:, 2 * b + qt, st * P:(st + 1) * P], ident)
                        return last
                    if b == 0:
                        have(full.at())
                    n = fill(go)
                have(n)

            pe.wait_ge(s_const, 16)
            pe.wait_ge(s_rows, rows_landed.at())
            for l in range(DEPTH):
                for g in range(2):
                    n = GROUP_ROWS[g]
                    fill(lambda bank: nc.tensor.transpose(bank[:, 0:n], prow[0:n, l, g, :], ident[0:n, 0:n]))
            for l in range(DEPTH):
                transpose_tok()
                unit(0, 8, opT)
                unit(1, 8, opT)
                transpose_unit(0, [P] * 4, 1)
                transpose_tok()
                with repeat(pe, 3, {slab: 16, emptied: 2, full: 4}):
                    unit(0, 8, opT)
                    unit(1, 8, opT, between=lambda: transpose_unit(0, [P] * 4, 1))
                    transpose_unit(1, [P] * 4, 0)
                unit(0, 8, opT, width=LORA_COLS)
                unit(1, 8, opT, between=lambda: transpose_unit(0, LORA_W, 1))
                unit(0, 8, opT, between=lambda: transpose_unit(1, [P] * 4, 1))
                unit(1, 8, opT, between=lambda: transpose_unit(0, [P] * 4, 1))
                transpose_unit(1, [P] * 2, 0, aligned=True)
                with repeat(pe, 5, {full: 4, for_pe: 2}):
                    pe.wait_ge(s_for_pe, for_pe.next())
                    fill(lambda bank: nc.tensor.matmul(bank, head_ones, sq_tmp, start=True, stop=True))
                    pe.wait_ge(s_for_pe, for_pe.next())
                    fill(lambda bank: nc.tensor.matmul(bank, rot, qn_tmp, start=True, stop=True), aligned=True)
                with repeat(pe, AT_KV_HEADS, {full: 12, for_pe: 1}):
                    pe.wait_ge(s_for_pe, for_pe.next())
                    for tile in range(2):
                        for h in range(2):
                            def go(bank):
                                for qt in range(2):
                                    last = nc.tensor.matmul(bank[:, qt * SEQ:(qt + 1) * SEQ],
                                                            q_now[h * HEAD:(h + 1) * HEAD, tile, qt * P:(qt + 1) * P],
                                                            k_now[h * HEAD:(h + 1) * HEAD, :], start=True, stop=True)
                                return last
                            fill(go)
                    softmax_turn()

                    def values(bank):
                        for tile in range(2):
                            for h in range(2):
                                for st in range(2):
                                    last = nc.tensor.matmul(bank[h * HEAD:(h + 1) * HEAD, tile * SEQ:(tile + 1) * SEQ],
                                                            v_now[:, st, :], probT[:, 2 * tile + h, st * SEQ:(st + 1) * SEQ],
                                                            start=st == 0, stop=st == 1)
                        return last
                    fill(values, aligned=True)
                if l:
                    pe.wait_ge(s_for_pe, for_pe.next())
                    def low(bank):
                        for j in range(PAIRS):
                            last = nc.tensor.matmul(bank[0:V_LORA, 0:SEQ], vdown[:, j, :], zs[:, 2 * PAIRS + j, :],
                                                    start=j == 0, stop=j == PAIRS - 1)
                        return last
                    fill(low, aligned=True)
                pe.wait_ge(s_for_pe, for_pe.next())
                with repeat(pe, PAIRS, {full: 68 if l else 64, for_pe: 6, lw: 7 if l else 6}):
                    pe.wait_ge(s_lw, lw.next(7 if l else 6))
                    fill(lambda bank: nc.tensor.matmul(bank, lora_w[:, 0, :], lora_in[:, 0], start=True, stop=True))
                    fill(lambda bank: nc.tensor.matmul(bank, lora_w[:, 1, :], lora_in[:, 1], start=True, stop=True))
                    if l:
                        fill(lambda bank: nc.tensor.matmul(bank[:, 0:SEQ], lora_w[32:32 + V_LORA, 3, :], v_low, start=True, stop=True))

                    def gate(bank):
                        nc.tensor.matmul(bank[:, 0:SEQ], lora_w[:, 2, :], lora_in[:, 2, 0, :], start=True, stop=False)
                        return nc.tensor.matmul(bank[:, 0:SEQ], lora_w[0:32, 3, :], lora_in[0:32, 2, 1, :], start=False, stop=True)
                    fill(gate)
                    pe.wait_ge(s_for_pe, for_pe.next())
                    fill(lambda bank: nc.tensor.matmul(bank[:, 0:SEQ], head_ones, tmp2[:, :], start=True, stop=True))

                    pe.wait_ge(s_for_pe, for_pe.next())
                    fill(lambda bank: nc.tensor.matmul(bank[:, 0:SEQ], head_ones, tmp[:, :], start=True, stop=True))

                    def v_turn(bank):
                        for c2 in range(NCH // 2):
                            last = nc.tensor.transpose(bank[:, c2 * P:(c2 + 1) * P], v_cur[:, c2 * P:(c2 + 1) * P], ident)
                        return last
                    fill(v_turn)
                    pe.wait_ge(s_for_pe, for_pe.next())
                    for d in range(2):
                        for c2 in range(0, NCH, 2):
                            def go(bank):
                                for j in range(4):
                                    last = nc.tensor.transpose(bank[:, j * P:(j + 1) * P], KB[:, d, c2 + j // 2, j % 2, :], ident)
                                return last
                            fill(go)
                    for d in range(2):
                        for c in range(NCH):
                            def go(bank):
                                ar = AR[:, d, c].rearrange("p w n -> p (w n)")
                                nc.tensor.matmul(bank[:, 0:256], KB[:, d, c, 0, :], ar, start=True, stop=True)
                                return nc.tensor.matmul(bank[:, 256:512], KB[:, d, c, 1, :], ar, start=True, stop=True)
                            n = fill(go)
                    nat = {}
                    for d in range(2):
                        def go(bank):
                            for c in range(NCH):
                                last = nc.tensor.transpose(bank[:, c * P:(c + 1) * P], GT[:, d, c, 0, :], ident)
                            return last
                        have(full.at((1 - d) * 4 + d))
                        nat[d] = fill(go)

                    def four(lhs, rhs):
                        def go(bank):
                            for c in range(NCH):
                                last = nc.tensor.matmul(bank[:, c * P:(c + 1) * P], lhs[:, c, :], rhs[:, c, :], start=True, stop=True)
                            return last
                        return go

                    def turned(src):
                        def go(bank):
                            for c in range(NCH):
                                last = nc.tensor.transpose(bank[:, c * P:(c + 1) * P], src[:, c, :], ident)
                            return last
                        return go

                    done = {}
                    for d in range(2):
                        pe.wait_ge(s_for_pe, for_pe.next())
                        fill(four(XTA[:, d], XA[:, d]))
                        done[d] = fill(four(XA[:, d], XTA[:, d]))
                    for d in range(2):
                        have(done[d])
                        fill(four(XB[:, d], EE[:, d]))
                        fill(four(XTB[:, d], XB[:, d]))
                        done[d] = fill(four(XB[:, d], XTB[:, d]))
                    for d in range(2):
                        have(done[d])
                        fill(four(XA[:, d], EE[:, d]))
                        done[d] = fill(four(XTA[:, d], XA[:, d]))
                    for d in range(2):
                        have(done[d])
                        done[d] = fill(four(XB[:, d], EE[:, d]))
                    for n in (32, 64):
                        for d in range(2):
                            have(done[d])
                            fill(four(OFF[n][:, d], EE[:, d]))
                            done[d] = fill(turned(EE[:, d]))
                        for d in range(2):
                            have(done[d])
                            done[d] = fill(four(XA[:, d], XTB[:, d]))
                    have(done[1])
                    for n in range(NCH):
                        at = (n, NCH - 1 - n)

                        def go_w(bank):
                            for d, c in enumerate(at):
                                o = bank[:, d * HEAD:(d + 1) * HEAD]
                                if n:
                                    nc.tensor.matmul(o, AR[:, d, c, 0, :], St[:, d, :], start=True, stop=False)
                                last = nc.tensor.matmul(o, GT[:, d, c, 2, :], Vc[:, c, :], start=n == 0, stop=True)
                            return last

                        def go_u(bank):
                            for d, c in enumerate(at):
                                last = nc.tensor.matmul(bank[:, d * HEAD:(d + 1) * HEAD], EE[:, d, c, :], Wc[:, d, :], start=True, stop=True)
                            return last

                        def go_y(bank):
                            for d, c in enumerate(at):
                                o = bank[:, d * HEAD:(d + 1) * HEAD]
                                if n:
                                    nc.tensor.matmul(o, AR[:, d, c, 1, :], St[:, d, :], start=True, stop=False)
                                nc.tensor.matmul(o, GT[:, d, c, 1, :], Uc[:, d, :], start=n == 0, stop=False)
                                last = nc.tensor.matmul(o, GT[:, d, c, 3, :], Vc[:, c, :], start=False, stop=True)
                            return last

                        def go_s(bank):
                            for d, c in enumerate(at):
                                o = bank[:, d * HEAD:(d + 1) * HEAD]
                                nc.tensor.matmul(o, KBt[:, d, c, 0, :], Uc[:, d, :], start=True, stop=False)
                                last = nc.tensor.matmul(o, KBt[:, d, c, 1, :], Vc[:, c, :], start=False, stop=True)
                            return last
                        have(fill(go_w))
                        have(fill(go_u))
                        if n < NCH - 1:
                            fill(go_s)
                            n_s = fill(go_y)
                            have(n_s)
                        else:
                            fill(go_y)
                    pe.wait_ge(s_for_pe, for_pe.next())

                    def y_turn(bank):
                        for c2 in range(NCH // 2):
                            two_chunks = Yc[:, 2 * c2:2 * c2 + 2, :].rearrange("p c n -> p (c n)")
                            last = nc.tensor.transpose(bank[:, c2 * P:(c2 + 1) * P], two_chunks, ident)
                        return last
                    fill(y_turn, aligned=True)
                have(full.at())
                pe.wait_ge(s_for_pe, for_pe.next())
                with repeat(pe, 4, {slab: 24, emptied: 2, branch: 2}):
                    pe.wait_ge(s_branch, branch.at())
                    unit(0, 8, opT)
                    unit(1, 8, opT)
                    pe.wait_ge(s_emptied, emptied.at(1))
                    unit(0, 4, y_rw, wait=False)
                    pe.wait_ge(s_emptied, emptied.at())
                    unit(1, 4, y_at, wait=False)
                    branch.next(2)
                pe.wait_ge(s_branch, branch.at())
                transpose_tok()
                with repeat(pe, 2, {slab: 16, emptied: 2}):
                    unit(0, 8, opT)
                    unit(1, 8, opT)
                transpose_tok()
                unit(0, 8, opT)
                transpose_unit(0, [P] * 4, 0, aligned=True)
                have(full.at())
                for b in range(X_HEADS):
                    def go(bank):
                        for qt in range(2):
                            last = nc.tensor.matmul(bank[:, qt * SEQ:(qt + 1) * SEQ], x_q[:, b, qt * P:(qt + 1) * P], memk[:, b, :],
                                                    start=True, stop=True)
                        return last
                    fill(go)
                softmax_turn()
                for b2 in range(2):
                    def go(bank):
                        for j in range(2):
                            for st in range(2):
                                b = 2 * b2 + j
                                last = nc.tensor.matmul(bank[:, j * SEQ:(j + 1) * SEQ], memv[:, st, b * X_HEAD:(b + 1) * X_HEAD],
                                                        probT[:, b, st * SEQ:(st + 1) * SEQ], start=st == 0, stop=st == 1)
                        return last
                    n = fill(go, aligned=b2 == 1)
                have(n)
                unit(1, 2, x_y)
                for u in range(1, 4):
                    unit((u + 1) % 2, 2, x_y)
                transpose_tok()
                ub = 1
                for tiles in FF_PARTS:
                    settle()
                    with repeat(pe, tiles // 4, {slab: 16, emptied: 2, full: 4}):
                        unit(1, 8, opT)
                        unit(0, 8, opT, between=lambda: transpose_unit(1, [P] * 2, 1))
                        transpose_unit(0, [P] * 2, 0, aligned=True)
                    have(full.at())
                    with repeat(pe, 2, {slab: tiles, emptied: 2}):
                        unit(1, tiles // 2, hidT)
                        unit(0, tiles // 2, hidT)

        @block.scalar
        def _(act):
            slab = Tally(s_used)
            for_act = Tally(s_for_act)
            rows_free = Tally(s_rows_free)

            def unit_rows(ub, nslab, width=UNIT, turned=True):
                if rows_free.count >= 2:
                    act.wait_ge(s_rows_free, rows_free.at(1))
                if turned:
                    rows_free.next()
                act.wait_ge(s_used, slab.next(nslab))
                nc.scalar.activation(rows[:, ub, :, 0:width], acc[:, ub, :, 0:width], ACT.Copy).then_inc(s_emptied, 1)

            def rms(src):
                for tok in range(TOK):
                    nc.scalar.activation(junk, src[:, tok, :], ACT.Square, accum_out=stat[:, tok:tok + 1]).then_inc(s_from_act, 1)
                    if tok == 0:
                        act.wait_ge(s_from_act, from_act.next())
                    else:
                        from_act.next()
                root(stat[:, 2:4])

            def root(v):
                act.wait_ge(s_for_act, for_act.next())
                nc.scalar.activation(v, v, ACT.Sqrt).then_inc(s_from_act, 1)
                from_act.next()

            def exps(scale):
                act.wait_ge(s_for_act, for_act.next())
                for k in range(8):
                    last = nc.scalar.activation(prob[:, k, :], work[:, k // 2, (k % 2) * SEQ:(k % 2 + 1) * SEQ], ACT.Exp,
                                                bias=stat[:, 16 + k:17 + k], scale=scale, accum_out=stat[:, 24 + k:25 + k])
                last.then_inc(s_from_act, 1)
                from_act.next()

            from_act = Tally(s_from_act)
            for l in range(DEPTH):
                act.wait_ge(s_mem, 16 * (l + 1))
                if l == 0:
                    act.wait_ge(s_x, 16)
                act.wait_ge(s_for_act, for_act.next())
                rms(tok_buf)
                unit_rows(0, 8)
                unit_rows(1, 8, turned=False)
                act.wait_ge(s_for_act, for_act.next())
                rms(x)
                with repeat(act, 3, {slab: 16, rows_free: 2}):
                    unit_rows(0, 8)
                    unit_rows(1, 8)
                unit_rows(0, 8, LORA_COLS)
                unit_rows(1, 8)
                unit_rows(0, 8)
                unit_rows(1, 8)
                with repeat(act, 5, {for_act: 1, from_act: 1}):
                    root(rt_tmp)
                with repeat(act, AT_KV_HEADS, {for_act: 1, from_act: 1}):
                    exps(HEAD ** -0.5)
                act.wait_ge(s_for_act, for_act.next())
                for d in range(2):
                    r = slice(d * 64, (d + 1) * 64)
                    nc.scalar.activation(lora_in[r, 0, d, :], zs[r, 24, :], ACT.Tanh)
                nc.scalar.activation(lora_in[:, 2, 0, :], zs[:, 26, :], ACT.Sigmoid)
                nc.scalar.activation(lora_in[0:32, 2, 1, :], zs[0:32, 27, :], ACT.Sigmoid).then_inc(s_from_act, 1)
                from_act.next()
                with repeat(act, PAIRS, {for_act: 4, from_act: 4}):
                    act.wait_ge(s_for_act, for_act.next())
                    if l:
                        nc.scalar.activation(tmp2[:, :], tmp2[:, :], ACT.Sigmoid)
                    nc.scalar.activation(sig, sig, ACT.Sigmoid).then_inc(s_from_act, 1)
                    from_act.next()
                    root(tmp[:, :])
                    act.wait_ge(s_for_act, for_act.next())
                    nc.scalar.activation(p_inc, inc, ACT.Exp, scale=-DECAY)
                    nc.scalar.activation(p_inv, inc, ACT.Exp, scale=DECAY)
                    nc.scalar.activation(p_exc, exc, ACT.Exp, scale=-DECAY).then_inc(s_from_act, 1)
                    from_act.next()
                    root(stat[:, 8:12])
                with repeat(act, 4, {slab: 24, for_act: 1}):
                    for ub, gate in enumerate((gate_a, gate_b)):
                        act.wait_ge(s_used, slab.next(8))
                        if ub == 0:
                            act.wait_ge(s_for_act, for_act.next())
                        nc.scalar.activation(gate, acc[:, ub], ACT.Sigmoid).then_inc(s_emptied, 1)
                    slab.next(8)

                def product(n, nslab, ubs):
                    for j in range(n):
                        act.wait_ge(s_used, slab.next(nslab))
                        nc.scalar.activation(tok_buf[:, :, j * UNIT:(j + 1) * UNIT], acc[:, ubs[j]], ACT.Copy).then_inc(s_emptied, 1)
                product(4, 8, (0, 1, 0, 1))
                act.wait_ge(s_emptied, emptied_now(l, "wo"))
                rms(tok_buf)
                act.wait_ge(s_for_act, for_act.next())
                rms(x)
                unit_rows(0, 8)
                exps(X_HEAD ** -0.5)
                product(4, 2, (1, 0, 1, 0))
                act.wait_ge(s_emptied, emptied_now(l, "xo"))
                rms(tok_buf)
                act.wait_ge(s_for_act, for_act.next())
                rms(x)
                for tiles in FF_PARTS:
                    with repeat(act, tiles // 4, {slab: 16, rows_free: 2, from_act: 2}):
                        for ub in (1, 0):
                            act.wait_ge(s_rows_free, rows_free.at(1))
                            rows_free.next()
                            act.wait_ge(s_used, slab.next(8))
                            nc.scalar.activation(rows[:, ub, :, 0:256], acc[:, ub, :, 0:256], ACT.Silu).then_inc(s_from_act, 1)
                            from_act.next()
                    slab.next(2 * tiles)
                act.wait_ge(s_for_act, for_act.next())
                rms(tok_buf)

        @block.vector
        def _(dve):
            V = nc.vector
            slab = Tally(s_used)
            full = Tally(s_full)
            drained = Tally(s_drained)
            step = Tally(s_dve)
            for_pe = Tally(s_for_pe)
            for_act = Tally(s_for_act)
            from_act = Tally(s_from_act)
            gain = Tally(s_gain, 16)

            def own(ins):
                ins.then_inc(s_dve, 1)
                dve.wait_ge(s_dve, step.next())

            def to_pe(ins):
                ins.then_inc(s_for_pe, 1)
                for_pe.next()

            def to_act(ins):
                ins.then_inc(s_for_act, 1)
                for_act.next()

            def act_result():
                dve.wait_ge(s_from_act, from_act.next())

            def bank():
                b = full.count % 4
                dve.wait_ge(s_full, full.next())
                return work[:, b, :]

            def drain(ins, n=1, wait=False, aligned=False):
                if aligned:
                    pad = -full.count % 4
                    full.next(pad)
                    n += pad
                ins.then_inc(s_drained, n)
                drained.next(n)
                if wait:
                    dve.wait_ge(s_drained, drained.at())

            def bc(ap, n):
                return ap.unsqueeze(2).to_broadcast([ap.shape[0], ap.shape[1], n])

            def rms_scale():
                act_result()
                act_result()
                to_act(V.tensor_scalar(stat[:, 2:4], stat[:, 0:2], 1.0 / D_MODEL, EPS, ALU.mult, ALU.add))
                act_result()
                own(V.reciprocal(stat[:, 4:6], stat[:, 2:4]))

            def norm_rows(src):
                rms_scale()
                for tok in range(TOK):
                    to_pe(V.tensor_scalar(tok_buf[:, tok, :], src[:, tok, :], stat[:, 4 + tok:5 + tok], None, ALU.mult))

            def turned_rows(gains=None):
                for tok in range(TOK):
                    for g in range(KD // 4):
                        src = bank().rearrange("p (j n) -> p j n", j=4)
                        dst = opT[:, 4 * g:4 * g + 4, tok * P:(tok + 1) * P]
                        if gains is None:
                            drain(V.tensor_copy(dst, src))
                        else:
                            drain(V.tensor_tensor(dst, src, bc(gains[:, 4 * g:4 * g + 4], P), ALU.mult))

            def post_norm(name):
                rms_scale()
                dve.wait_ge(s_gain, gain.next())
                for tok in range(TOK):
                    own(V.scalar_tensor_tensor(tok_buf[:, tok, :], tok_buf[:, tok, :], stat[:, 4 + tok:5 + tok], gain_row, ALU.mult, ALU.mult))
                    own(V.tensor_tensor(x[:, tok, :], x[:, tok, :], tok_buf[:, tok, :], ALU.add))

            def nudge_act():
                dve.sem_inc(s_for_act, 1)
                for_act.next()

            def softmax(scale):
                for _ in range(4):
                    bank()
                scores = work[:, :, :].rearrange("p b (q s) -> p (b q) s", q=2)
                own(V.reduce_max(stat[:, 32:40], scores, AX_X))
                to_act(V.tensor_scalar(stat[:, 16:24], stat[:, 32:40], -scale, None, ALU.mult))
                act_result()
                own(V.reciprocal(stat[:, 40:48], stat[:, 24:32]))
                drain(V.tensor_tensor(prob, prob, bc(stat[:, 40:48], SEQ), ALU.mult), 4)
                for _ in range(4):
                    bank()
                drain(V.tensor_copy(probT, work[:, :, :]), 4)

            own(V.memset(prow, 0.0))
            dve.sem_inc(s_rows_zero, 1)
            own(V.memset(lora_in[:, :, :, :], 0.0))
            dve.wait_ge(s_const, 16)
            for l in range(DEPTH):
                for g in range(2):
                    n, o = GROUP_ROWS[g], GROUP_ROWS[0] * g
                    drain(V.tensor_copy(cols[:, l, o:o + n], bank()[:, 0:n]), wait=True)
                own(V.tensor_tensor(cols_mix[:, l, :], colv(l, "rw_mu_prev", 28), colv(l, "rw_mu_next", 28), ALU.add))
                own(V.tensor_scalar(cols_mix[:, l, :], cols_mix[:, l, :], -1.0, 1.0, ALU.mult, ALU.add))
                own(V.tensor_scalar(cols_ka[:, l, :], colv(l, "rw_k_a", PAIRS), -1.0, 1.0, ALU.mult, ALU.add))
            carry = cst("carry")
            for l in range(DEPTH):
                dve.sem_inc(s_mem_free, 1)
                dve.wait_ge(s_mem, 16 * (l + 1))
                if l == 0:
                    dve.wait_ge(s_x, 16)
                nudge_act()
                norm_rows(tok_buf)
                turned_rows(colv(l, "n_mem", KD))
                for b in range(2):
                    src = bank().rearrange("p (j n) -> p j n", j=2)
                    if b:
                        V.tensor_copy(memk[:, 2 * b:2 * b + 1, :], src[:, 0:1, :]).then_inc(s_rows_free, 1)
                        drain(V.tensor_copy(memk[:, 2 * b + 1:2 * b + 2, :], src[:, 1:2, :]))
                    else:
                        drain(V.tensor_copy(memk[:, 0:2, :], src))
                dve.wait_ge(s_emptied, emptied_now(l, "memv"))
                to_act(V.tensor_copy(memv[:, :, :], rows[:, 1, :, :]))

                norm_rows(x)
                turned_rows(colv(l, "n_mix_pre", KD))

                def shifted(src, t, w, mix, prev, nxt):
                    dst = t
                    own(V.tensor_scalar(dst, src, mix, None, ALU.mult))
                    own(V.scalar_tensor_tensor(dst[:, 1:SEQ], src[:, 0:SEQ - 1], prev, dst[:, 1:SEQ], ALU.mult, ALU.add))
                    return V.scalar_tensor_tensor(dst[:, 0:SEQ - 1], src[:, 1:SEQ], nxt, dst[:, 0:SEQ - 1], ALU.mult, ALU.add)

                with repeat(dve, 3, {full: 4, drained: 4, step: 16}) as i:
                    for u in range(2):
                        for b in range(2):
                            src = bank()
                            for j in range(2):
                                k = u * 4 + b * 2 + j
                                zt = zs[:, 0:24, :].rearrange("p (i k) n -> p k i n", k=8)[:, k]
                                pv = colv(l, "rw_mu_prev", 24).rearrange("p (i k) -> p k i", k=8)[:, k]
                                nx = colv(l, "rw_mu_next", 24).rearrange("p (i k) -> p k i", k=8)[:, k]
                                mx = cols_mix[:, l, 0:24].rearrange("p (i k) -> p k i", k=8)[:, k]
                                ins = shifted(src[:, j * SEQ:(j + 1) * SEQ], zt[:, i, :], P, mx[:, bass.ts(i, 1)], pv[:, bass.ts(i, 1)], nx[:, bass.ts(i, 1)])
                                if j:
                                    drain(ins)
                                elif b:
                                    ins.then_inc(s_rows_free, 1)
                for b in range(2):
                    src = bank()
                    for j in range(2):
                        k = 24 + 2 * b + j
                        w = LORA_W[2 * b + j]
                        ins = shifted(src[0:w, j * SEQ:(j + 1) * SEQ], zs[0:w, k, :], w, cols_mix[0:w, l, k:k + 1],
                                      col(l, "rw_mu_prev", k)[0:w], col(l, "rw_mu_next", k)[0:w])
                        if j:
                            drain(ins, wait=True)
                        elif b:
                            ins.then_inc(s_rows_free, 1)
                for u in range(3):
                    for b in range(2 if u < 2 else 1):
                        src = bank()
                        dst = qk[:, 2 * u + b]
                        if b or u == 2:
                            V.tensor_copy(dst[:, 0:1, :], src[:, 0:SEQ].rearrange("p (j n) -> p j n", j=1)).then_inc(s_rows_free, 1)
                            drain(V.tensor_copy(dst[:, 1:2, :], src[:, SEQ:2 * SEQ].rearrange("p (j n) -> p j n", j=1)), wait=True, aligned=u == 2)
                        else:
                            drain(V.tensor_copy(dst, src.rearrange("p (j n) -> p j n", j=2)), wait=True)
                own(V.tensor_copy(v_at, rows[:, 1, :, AT_KV:2 * AT_KV]))
                with repeat(dve, 5, {full: 4, drained: 4, for_pe: 2, for_act: 1, from_act: 1, step: 3}) as i:
                    qi = qk[:, i].rearrange("p a b -> p (a b)")
                    flat = lambda t: t.rearrange("p a b -> p (a b)")
                    to_pe(V.tensor_tensor(flat(sq_tmp), qi, qi, ALU.mult))
                    src = bank()
                    ins = V.tensor_scalar(flat(rt_tmp), src, 1.0 / HEAD, EPS, ALU.mult, ALU.add)
                    to_act(ins)
                    act_result()
                    own(V.reciprocal(flat(rt_tmp), flat(rt_tmp)))
                    dve.sem_inc(s_drained, 1)
                    drained.next()
                    gcol = colv(l, "qk_norm", 5)[:, bass.ts(i, 1)]
                    to_pe(V.scalar_tensor_tensor(flat(qn_tmp), qi, gcol, flat(rt_tmp), ALU.mult, ALU.mult))
                    dve.wait_ge(s_for_pe, for_pe.at())
                    b2 = lambda t: t.unsqueeze(1).to_broadcast([P, 2, SEQ])
                    own(V.tensor_tensor(qk[:, i], qn_tmp, b2(cst("cos")), ALU.mult))
                    src = bank().rearrange("p (j n) -> p j n", j=2)
                    drain(V.tensor_tensor(sq_tmp, src, b2(cst("sin")), ALU.mult), wait=True, aligned=True)
                    own(V.tensor_tensor(qk[:, i], qk[:, i], sq_tmp, ALU.add))
                for g in range(AT_KV_HEADS):
                    for half in range(2):
                        s0 = (g % 2) * HEAD
                        ins = V.tensor_copy(k_both[half * HEAD:(half + 1) * HEAD, g, :], qk[s0:s0 + HEAD, 4, g // 2, :])
                own(ins)
                with repeat(dve, AT_KV_HEADS, {full: 12, drained: 12, for_pe: 1, for_act: 1, from_act: 1, step: 2}) as g:
                    V.tensor_copy(q_now, qk[:, g])
                    V.tensor_copy(k_now, k_both[:, g, :])
                    to_pe(V.tensor_copy(v_now, v_at.rearrange("p t (g d) -> p g t d", g=AT_KV_HEADS)[:, g]))
                    softmax(HEAD ** -0.5)
                    drain(V.tensor_copy(y_at[:, :, :].rearrange("p (g t) n -> p g (t n)", t=2)[:, g], bank()), aligned=True)
                if l:
                    dve.sem_inc(s_for_pe, 1)
                    for_pe.next()
                    drain(V.tensor_copy(v_low, bank()[0:V_LORA, 0:SEQ]), aligned=True)
                nudge_act()
                for d in range(2):
                    r = slice(d * 64, (d + 1) * 64)
                    own(V.tensor_copy(lora_in[r, 1, d, :], zs[r, 25, :]))
                own(V.memset(view(0, 4096), 0.0))
                act_result()
                dve.sem_inc(s_for_pe, 1)
                for_pe.next()
                dve.sem_inc(s_lw_free, 1)
                with repeat(dve, PAIRS, {full: 68 if l else 64, drained: 68 if l else 64, for_pe: 6, for_act: 4, from_act: 4, step: N_STEP[l]}) as i:
                    rT, kT, vT = zs[:, 0:8, :][:, i, :], zs[:, 8:16, :][:, i, :], zs[:, 16:24, :][:, i, :]

                    def pcol(name, d=None):
                        v = colv(l, name, PAIRS) if d is None else cols[:, l, PCOL[name] + d * PAIRS:PCOL[name] + (d + 1) * PAIRS]
                        return v[:, bass.ts(i, 1)]
                    flat = lambda t: t.rearrange("p a b -> p (a b)")
                    for kind, name in enumerate(("rw_w0", "rw_a0")):
                        src = bank()
                        for d in range(2):
                            ins = V.tensor_scalar(sig[:, 2 * kind + d, :], src[:, d * SEQ:(d + 1) * SEQ], pcol(name, d), None, ALU.add)
                        drain(ins)
                    if l:
                        drain(V.tensor_scalar(tmp2[:, :], bank()[:, 0:SEQ], pcol("rw_v0"), None, ALU.add))
                    drain(V.tensor_copy(g_cur[:, :], bank()[:, 0:SEQ]), wait=True)
                    nudge_act()
                    dve.sem_inc(s_lw_free, 1)
                    act_result()
                    if l:
                        own(V.tensor_tensor(v_cur[:, :], v_first[:, :, :][:, i, :], vT, ALU.subtract))
                        own(V.tensor_tensor(v_cur[:, :], v_cur[:, :], tmp2[:, :], ALU.mult))
                        own(V.tensor_tensor(v_cur[:, :], v_cur[:, :], vT, ALU.add))
                    else:
                        own(V.tensor_copy(v_cur[:, :], vT))
                        own(V.tensor_copy(v_first[:, :, :][:, i, :], vT))
                    own(V.tensor_scalar(flat(kd), flat(sig[:, 2:4, :]), pcol("rw_k_a"), cols_ka[:, l, :][:, bass.ts(i, 1)], ALU.mult, ALU.add))
                    two = lambda t: t.unsqueeze(1).to_broadcast([P, 2, SEQ])
                    own(V.tensor_tensor(kd, kd, two(kT), ALU.mult))
                    own(V.tensor_tensor(tmp[:, :], kd[:, 0, :], kd[:, 1, :], ALU.add))
                    own(V.scalar_tensor_tensor(tmp2[:, :], rT, pcol("rw_r_k"), tmp[:, :], ALU.mult, ALU.mult))
                    dve.sem_inc(s_for_pe, 1)
                    for_pe.next()
                    own(V.tensor_scalar(p_exc[:, 0, :], kT, pcol("rw_k_k"), None, ALU.mult))
                    to_pe(V.tensor_tensor(tmp[:, :], p_exc[:, 0, :], p_exc[:, 0, :], ALU.mult))
                    drain(V.tensor_tensor(kT, bank()[:, 0:SEQ], v_cur[:, :], ALU.mult))
                    drain(V.tensor_copy(tmp[:, :], bank()[:, 0:SEQ]), wait=True)
                    nudge_act()
                    own(V.tensor_tensor_scan(inc[:, 0, :], carry, sig[:, 0, :], 0.0, ALU.mult, ALU.add))
                    own(V.tensor_tensor_scan(p_inc[:, 0, :], carry, sig[:, 1, :], 0.0, ALU.mult, ALU.add))
                    own(V.tensor_tensor(exc[:, 0, :], inc[:, 0, :], sig[:, 0, :], ALU.subtract))
                    ch = lambda t: t.rearrange("p (c n) -> p c n", c=NCH)
                    total = ch(p_inc[:, 0, :])[:, :, CHUNK - 1:CHUNK].to_broadcast([P, NCH, CHUNK])
                    own(V.tensor_tensor(ch(exc[:, 1, :]), total, ch(p_inc[:, 0, :]), ALU.subtract))
                    own(V.tensor_tensor(inc[:, 1, :], exc[:, 1, :], sig[:, 1, :], ALU.add))
                    act_result()
                    own(V.tensor_scalar(tmp[:, :], tmp[:, :], 1e-12, None, ALU.max))
                    own(V.reciprocal(tmp[:, :], tmp[:, :]))
                    own(V.scalar_tensor_tensor(tmp[:, :], p_exc[:, 0, :], -1.0, tmp[:, :], ALU.mult, ALU.mult))
                    nudge_act()
                    own(V.scalar_tensor_tensor(sig[:, 2:4, :], two(tmp[:, :]), -1.0, sig[:, 2:4, :], ALU.mult, ALU.mult))
                    src = bank()[:, 0:2 * P].rearrange("p (c n) -> p c n", c=2)
                    by_two = Vc[:, :, :].rearrange("p (c k) n -> p c k n", k=2)
                    for h in range(2):
                        for odd in range(2):
                            ins = V.tensor_copy(by_two[h * HEAD:(h + 1) * HEAD, :, odd, :],
                                                src[odd * CHUNK:(odd + 1) * CHUNK, :, h * HEAD:(h + 1) * HEAD])
                    drain(ins)
                    act_result()
                    for h in range(2):
                        r = slice(h * HEAD, (h + 1) * HEAD)
                        for buf, which, p, q in ((AR, 0, two(tmp[:, :]), p_exc), (AR, 1, two(rT), p_inc),
                                                 (KB, 0, sig[:, 2:4, :], p_inv), (KB, 1, kd, p_inv)):
                            cv = lambda t: t.rearrange("p d (c n) -> p d c n", c=NCH)
                            ins = V.tensor_tensor(buf[r, :, :, which, h * HEAD:(h + 1) * HEAD], cv(p)[r], cv(q)[r], ALU.mult)
                    to_pe(ins)
                    for d in range(2):
                        for c2 in range(0, NCH, 2):
                            drain(V.tensor_copy(KBt[:, d, c2:c2 + 2].rearrange("p c w n -> p (c w n)"), bank()))
                    for d in range(2):
                        for c in range(NCH):
                            drain(V.tensor_tensor(GT[:, d, c].rearrange("p (w v) n -> p w (v n)", w=2), bank().rearrange("p (w n) -> p w n", w=2),
                                                  mask[:, d].unsqueeze(1).to_broadcast([P, 2, 2 * P]), ALU.mult))
                    m4 = lambda name: cst(name).unsqueeze(1).to_broadcast([P, NCH, P])
                    four = lambda t: t.rearrange("p (c n) -> p c n", c=NCH)
                    for d in range(2):
                        src = four(bank())
                        V.tensor_tensor(XA[:, d], src, m4("in16"), ALU.mult)
                        V.tensor_tensor(OFF[32][:, d], src, m4("in32"), ALU.mult)
                        drain(V.tensor_tensor(OFF[64][:, d], src, m4("in64"), ALU.mult))
                        own(V.tensor_tensor(XTA[:, d], GT[:, d, :, 0, :], m4("in16"), ALU.mult))
                        to_pe(V.tensor_tensor(EE[:, d], XTA[:, d], m4("ident"), ALU.add))
                    for d in range(2):
                        drain(V.tensor_copy(XB[:, d], four(bank())))
                        drain(V.tensor_copy(XTB[:, d], four(bank())))
                    for d in range(2):
                        drain(V.tensor_tensor(EE[:, d], EE[:, d], four(bank()), ALU.add), wait=True)
                        drain(V.tensor_copy(XA[:, d], four(bank())))
                        drain(V.tensor_copy(XTA[:, d], four(bank())))
                    for d in range(2):
                        drain(V.tensor_tensor(EE[:, d], EE[:, d], four(bank()), ALU.add), wait=True)
                        drain(V.tensor_copy(XB[:, d], four(bank())))
                    for d in range(2):
                        drain(V.tensor_tensor(EE[:, d], EE[:, d], four(bank()), ALU.add), wait=True)
                    for n in (32, 64):
                        for d in range(2):
                            drain(V.tensor_copy(XTB[:, d], four(bank())))
                            drain(V.tensor_copy(XA[:, d], four(bank())))
                        for d in range(2):
                            drain(V.tensor_tensor(EE[:, d], EE[:, d], four(bank()), ALU.add), wait=True)
                    for n in range(NCH):
                        at = (n, NCH - 1 - n)
                        drain(V.tensor_copy(flat(Wc[:, :, :]), bank()[:, 0:P]))
                        drain(V.tensor_copy(flat(Uc[:, :, :]), bank()[:, 0:P]))
                        if n < NCH - 1:
                            src_s = bank()
                        src = bank()
                        if n < NCH - 1:
                            for d, c in enumerate(at):
                                end = c * CHUNK + (CHUNK - 1 if d == 0 else 0)
                                s_d = src_s[:, d * HEAD:(d + 1) * HEAD]
                                if n:
                                    own(V.tensor_tensor(St[:, d, :], St[:, d, :], s_d, ALU.add))
                                    s_d = St[:, d, :]
                                own(V.tensor_scalar(St[:, d, :], s_d, p_inc[:, d, end:end + 1], None, ALU.mult))
                            dve.sem_inc(s_drained, 1)
                            drained.next()
                        for d, c in enumerate(at):
                            y = src[:, d * HEAD:(d + 1) * HEAD]
                            if n < NCH // 2:
                                ins = V.tensor_copy(Yc[:, c, :], y)
                            else:
                                ins = V.tensor_tensor(Yc[:, c, :], Yc[:, c, :], y, ALU.add)
                        drain(ins, wait=True)
                    own(V.reduce_sum(stat[:, 12:16], Yc[:, :, :], AX_X))
                    own(V.tensor_scalar(stat[:, 12:16], stat[:, 12:16], 1.0 / HEAD, None, ALU.mult))
                    own(V.tensor_tensor(Yc[:, :, :], Yc[:, :, :], bc(stat[:, 12:16], HEAD), ALU.subtract))
                    own(V.tensor_tensor(ch(p_inv[:, 0, :]), Yc[:, :, :], Yc[:, :, :], ALU.mult))
                    own(V.reduce_sum(stat[:, 12:16], ch(p_inv[:, 0, :]), AX_X))
                    to_act(V.tensor_scalar(stat[:, 8:12], stat[:, 12:16], 1.0 / HEAD, GN_EPS, ALU.mult, ALU.add))
                    act_result()
                    own(V.reciprocal(stat[:, 12:16], stat[:, 8:12]))
                    to_pe(V.tensor_tensor(Yc[:, :, :], Yc[:, :, :], bc(stat[:, 12:16], HEAD), ALU.mult))
                    src = bank()[:, 0:2 * P].rearrange("p (c n) -> p c n", c=2)
                    by_two = tmp[:, :].rearrange("p (c k n) -> p c k n", k=2, n=CHUNK)
                    for h in range(2):
                        for odd in range(2):
                            ins = V.tensor_copy(by_two[h * HEAD:(h + 1) * HEAD, :, odd, :],
                                                src[odd * HEAD:(odd + 1) * HEAD, :, h * HEAD:(h + 1) * HEAD])
                    drain(ins, wait=True, aligned=True)
                    own(V.tensor_scalar(tmp[:, :], tmp[:, :], pcol("rw_ln_w"), pcol("rw_ln_b"), ALU.mult, ALU.add))
                    own(V.tensor_tensor(tmp[:, :], tmp[:, :], kT, ALU.add))
                    own(V.tensor_tensor(y_rw[:, :, :][:, i, :], tmp[:, :], g_cur[:, :], ALU.mult))
                dve.sem_inc(s_for_pe, 1)
                for_pe.next()
                dve.sem_inc(s_gain_free, 1)
                slab.count = slab_now(l, "gates")
                with repeat(dve, 4, {slab: 24, for_act: 1, step: 2}) as i:
                    nudge_act()
                    tb_i = tok_buf[:, :, :].rearrange("p t (i n) -> p i t n", i=4)[:, i]
                    dve.wait_ge(s_used, slab.next(20))
                    own(V.tensor_tensor(tb_i, acc[:, 0], gate_a, ALU.mult))
                    dve.sem_inc(s_branch, 1)
                    dve.wait_ge(s_used, slab.next(4))
                    V.tensor_tensor(gate_b, acc[:, 1], gate_b, ALU.mult).then_inc(s_branch, 1)
                    dve.wait_ge(s_branch, branch_now(l, i))
                    own(V.tensor_tensor(tb_i, tb_i, gate_b, ALU.add))
                for tok in range(TOK):
                    dve.sem_inc(s_for_pe, 1)
                    for_pe.next()
                turned_rows()
                post_norm("n_mix_post")
                nudge_act()
                norm_rows(x)
                turned_rows(colv(l, "n_x_pre", KD))
                for b in range(2):
                    src = bank().rearrange("p (j n) -> p j n", j=2)
                    if b:
                        V.tensor_copy(x_q[:, 2:3, :], src[:, 0:1, :]).then_inc(s_rows_free, 1)
                        drain(V.tensor_copy(x_q[:, 3:4, :], src[:, 1:2, :]), aligned=True)
                    else:
                        drain(V.tensor_copy(x_q[:, 0:2, :], src))
                dve.sem_inc(s_gain_free, 1)
                softmax(X_HEAD ** -0.5)
                for b2 in range(2):
                    drain(V.tensor_copy(x_y[:, 2 * b2:2 * b2 + 2, :], bank().rearrange("p (j n) -> p j n", j=2)), aligned=b2 == 1)
                post_norm("n_x_post")
                nudge_act()
                norm_rows(x)
                turned_rows(colv(l, "n_ffn_pre", KD))
                dve.sem_inc(s_gain_free, 1)
                slab.count = slab_now(l, "ffn")
                for part, tiles in enumerate(FF_PARTS):
                    with repeat(dve, tiles // 4, {slab: 16, full: 4, drained: 4, from_act: 2, step: 0}) as i:
                        for j, ub in enumerate((1, 0)):
                            act_result()
                            slab.next(8)
                            V.tensor_tensor(rows[:, ub, :, 0:256], acc[:, ub, :, 256:512], rows[:, ub, :, 0:256], ALU.mult).then_inc(s_emptied, 1)
                            src = bank().rearrange("p (t n) -> p t n", t=2)
                            dst = hidT.rearrange("p (i j t) n -> p j i t n", j=2, t=2)[:, j]
                            V.tensor_copy(dst[:, i, 0:1, :], src[:, 0:1, :]).then_inc(s_rows_free, 1)
                            drain(V.tensor_copy(dst[:, i, 1:2, :], src[:, 1:2, :]), aligned=j == 1)
                    with repeat(dve, 2, {slab: tiles, step: 0}) as i:
                        for j, ub in enumerate((1, 0)):
                            dve.wait_ge(s_used, slab.next(tiles // 2))
                            c = tok_buf[:, :, :].rearrange("p t (i j n) -> p j i t n", i=2, j=2)[:, j][:, i]
                            if part == 0:
                                V.tensor_copy(c, acc[:, ub]).then_inc(s_emptied, 1)
                            else:
                                V.tensor_tensor(c, c, acc[:, ub], ALU.add).then_inc(s_emptied, 1)
                dve.wait_ge(s_emptied, emptied_now(l, "end"))
                nudge_act()
                post_norm("n_ffn_post")
            dve.sem_inc(s_out, 1)


N_STEP = {0: 37, 1: 38}


def slab_now(l, where):
    before = {"gates": 16 + 48 + 8 + 24, "ffn": 16 + 48 + 8 + 24 + 96 + 32 + 8 + 8}[where]
    return l * SLABS + before


SLABS = 16 + 48 + 8 + 24 + 96 + 32 + 8 + 8 + 8 * 22 + 2 * sum(FF_PARTS)
UNITS = 2 + 10 + 8 + 4 + 1 + 4 + 22 + 4 * len(FF_PARTS)


def emptied_now(l, where):
    n = {"memv": 2, "wo": 24, "xo": 29, "end": UNITS}[where]
    return l * UNITS + n


def branch_now(l, i):
    return i * 2 + (l * 8 + 2)


_INS = ["x", "mem", "n_mix_pre", "n_mix_post", "n_x_pre", "n_x_post", "n_ffn_pre", "n_ffn_post", "n_mem", "w_in",
        "rw_mu_prev", "rw_mu_next", "rw_w0", "rw_w_up", "rw_a0", "rw_a_up", "rw_g_up", "rw_v0", "rw_v_down", "rw_v_up",
        "rw_k_k", "rw_k_a", "rw_r_k", "rw_ln_w", "rw_ln_b", "w_rw_out", "at_q_norm", "at_k_norm", "w_at_out", "w_o",
        "x_wq", "x_wkv", "x_wo", "ffn_wg", "ffn_wu", "ffn_wd"]


def kernel(**inputs):
    import numpy as _np
    import concourse.bacc as _bacc
    from concourse import mybir as _mybir
    from concourse.bass_utils import run_bass_kernel_spmd as _run

    nc = _bacc.Bacc("TRN2", target_bir_lowering=False, num_devices=1)
    given = {name: _np.ascontiguousarray(inputs[name]) for name in _INS}
    given["shape_constants"] = shape_constants()
    arrays, aps = {}, {}
    for name, v in given.items():
        arrays[f"in_{name}_dram"] = v
        aps[name] = nc.dram_tensor(f"in_{name}_dram", v.shape, _mybir.dt.from_np(v.dtype), kind="ExternalInput").ap()
    out = nc.dram_tensor("out_0_dram", (1, SEQ, D_MODEL), _mybir.dt.float32, kind="ExternalOutput").ap()
    encoder_kernel(nc, aps, out)
    r = _run(nc, [arrays], core_ids=[0])
    return r.results[0]["out_0_dram"]
```

```python
from contextlib import ExitStack, contextmanager

import numpy as np

import concourse.bass as bass
from concourse import mybir

F32 = mybir.dt.float32
ALU = mybir.AluOpType
ACT = mybir.ActivationFunctionType
AX_X = mybir.AxisListType.X

P = 128
D_MODEL, SEQ, DEPTH, N_MEM = 2048, 256, 2, 256
GRID_W = 64
EPS = 1e-6
RW_HEADS, HEAD = 16, 64
RW_WIDTH = RW_HEADS * HEAD
W_LORA = A_LORA = 64
V_LORA, G_LORA = 32, 160
GN_EPS = 64e-5
AT_HEADS, AT_KV_HEADS = 16, 4
AT_Q, AT_KV = AT_HEADS * HEAD, AT_KV_HEADS * HEAD
ROPE_THETA = 10000.0
X_HEADS, X_HEAD = 4, 128
X_WIDTH = X_HEADS * X_HEAD
D_FF = -(-8 * D_MODEL // (3 * 256)) * 256
LORA_COLS = 2 * W_LORA + 2 * A_LORA + G_LORA
RW_COLS = 3 * RW_WIDTH + LORA_COLS
AT_COLS = AT_Q + 2 * AT_KV
DECAY = float(np.exp(-0.5))

TOK = SEQ // P
KD = D_MODEL // P
UNIT = 512
SLAB_K = 2
RING = 4
PAIRS = RW_HEADS // 2
SCAN_BANKS = 6
PER_PAIR = 54
CHUNK = 64
NCH = SEQ // CHUNK
FF_PARTS = (16, 16, 12)
LORA_W = (P, P, P, LORA_COLS - 3 * P)

PARAM_ROWS = [
    [("n_mix_pre", KD), ("n_x_pre", KD), ("n_ffn_pre", KD), ("n_mem", KD), ("rw_mu_prev", 28), ("rw_mu_next", 28)],
    [("rw_w0", 2 * PAIRS), ("rw_a0", 2 * PAIRS), ("rw_k_k", PAIRS), ("rw_k_a", PAIRS), ("rw_r_k", PAIRS),
     ("rw_ln_w", PAIRS), ("rw_ln_b", PAIRS), ("rw_v0", PAIRS), ("qk_norm", 5)],
]
PCOL = {}
_n = 0
for _g in PARAM_ROWS:
    for _name, _rows in _g:
        PCOL[_name] = _n
        _n += _rows
GROUP_ROWS = [sum(r for _, r in g) for g in PARAM_ROWS]
N_COLS = sum(GROUP_ROWS)

CONST = {}
_n = 0
for _name, _w in (("ident", P), ("head_ones", P), ("rot", P), ("mask", 2 * 2 * P), ("in16", P), ("in32", P),
                  ("in64", P), ("cos", SEQ), ("sin", SEQ), ("carry", SEQ), ("before", 2 * HEAD),
                  ("in16_head", HEAD), ("ident_head", HEAD)):
    CONST[_name] = (_n, _w)
    _n += _w
N_CONST = _n


def shape_constants():
    out = np.zeros((P, N_CONST), np.float32)

    def put(name, a):
        o, w = CONST[name]
        out[:, o:o + w] = a.reshape(P, w)

    r = np.arange(P)
    put("ident", np.eye(P))
    head = r[:, None] // HEAD == r[None, :] // HEAD
    put("head_ones", head)
    rot = np.zeros((P, P))
    for m in range(P):
        if m % 32 < 16:
            rot[m + 16, m] = -1.0
        else:
            rot[m - 16, m] = 1.0
    put("rot", rot)
    s, t = r[:, None] % HEAD, r[None, :] % HEAD
    mask = np.stack([head & (s < t), head & (s <= t), head & (s > t), head & (s >= t)], axis=1)
    put("mask", mask)
    put("in16", r[:, None] // 16 == r[None, :] // 16)
    for n in (32, 64):
        put(f"in{n}", (r[:, None] // n == r[None, :] // n) & (r[:, None] // (n // 2) != r[None, :] // (n // 2)))
    row, c64 = r[:, None] % HEAD, np.arange(HEAD)[None, :]
    put("before", np.stack([row < c64, row > c64], axis=1))
    put("in16_head", row // 16 == c64 // 16)
    put("ident_head", row == c64)
    n_freq = HEAD // 4
    inv = np.float32(ROPE_THETA) ** (-np.arange(n_freq, dtype=np.float32) / np.float32(n_freq))
    tok = np.arange(SEQ)
    pos = np.stack([tok // GRID_W, tok % GRID_W]).astype(np.float32)
    ang = pos[(r % HEAD) // 32] * inv[r % 16][:, None]
    put("cos", np.cos(ang))
    put("sin", np.sin(ang))
    put("carry", np.broadcast_to((tok % CHUNK != 0).astype(np.float32), (P, SEQ)))
    return out


class Tally:

    def __init__(self, sem, scale=1):
        self.sem, self.count, self.loop, self.scale = sem, 0, None, scale

    def at(self, back=0):
        n = (self.count - back) * self.scale
        return n if self.loop is None else self.loop[0] * (self.loop[1] * self.scale) + n

    def next(self, n=1):
        self.count += n
        return self.at()


class Banks:

    def __init__(self, tally, drained):
        self.tally, self.drained = tally, drained

    def now(self):
        t = self.tally
        uses = t.count // SCAN_BANKS + 1
        if t.loop is not None:
            assert t.loop[1] % SCAN_BANKS == 0
            return t.count % SCAN_BANKS, t.loop[0] * (2 * (t.loop[1] // SCAN_BANKS)) + 2 * uses
        return t.count % SCAN_BANKS, 2 * uses


@contextmanager
def repeat(eng, times, per):
    start = {t: t.count for t in per}
    with eng.Fori(0, times) as i:
        for t, n in per.items():
            t.loop = (i, n)
        yield i
        for t, n in per.items():
            assert t.count - start[t] == n, (t.sem, t.count - start[t], n)
    for t, n in per.items():
        t.loop = None
        t.count = start[t] + times * n


def encoder_kernel(nc, a, out):
    with ExitStack() as ctx:
        def sb(name, shape):
            return ctx.enter_context(nc.sbuf_tensor("sb_" + name, shape, F32))

        def sem(name):
            return ctx.enter_context(nc.semaphore(name))

        streams = sb("streams", [P, 5, D_MODEL])
        x = streams[:, 1:5:2, :]
        tok_buf = sb("tok_buf", [P, TOK, D_MODEL])
        opT = sb("opT", [P, KD, SEQ])
        ring = sb("ring", [P, RING, SLAB_K, UNIT])
        rows = sb("rows", [P, 2, TOK, UNIT])
        r_all, k_all, v_all = (streams[:, b, :].rearrange("p (i n) -> p i n", i=PAIRS) for b in (0, 2, 4))
        y_rw = r_all
        low_in = sb("low_in", [P, 4, SEQ])
        v_first = sb("v_first", [P, PAIRS, SEQ])
        y_at = sb("y_at", [P, PAIRS, SEQ])
        memk = sb("memk", [P, X_HEADS, N_MEM])
        memv = sb("memv", [P, TOK, X_WIDTH])
        const = sb("const", [P, N_CONST])
        cols = sb("cols", [P, DEPTH, N_COLS])
        cols_mix = sb("cols_mix", [P, DEPTH, 28])
        cols_ka = sb("cols_ka", [P, DEPTH, PAIRS])
        vdown = sb("vdown", [P, PAIRS, V_LORA])
        stat = sb("stat", [P, 64])
        lora_w = sb("lora_w", [P, 4, P])
        lora_in = sb("lora_in", [P, 3, 2, SEQ])
        v_low = lora_in[32:32 + V_LORA, 2, 1, :]
        arena = sb("arena", [P, 14336])

        def view(off, *shape):
            n = int(np.prod(shape))
            names = "abcd"[:len(shape)]
            v = arena[:, off:off + n]
            if len(shape) == 1:
                return v
            return v.rearrange(f"p ({' '.join(names)}) -> p {' '.join(names)}", **dict(zip(names, shape)))

        qk = view(0, 5, 2, SEQ)
        k_both = view(2560, AT_KV_HEADS, SEQ)
        v_at = view(3584, TOK, AT_KV)
        prob = view(4096, 8, SEQ)
        probT = view(6144, 4, 2 * SEQ)
        q_now = view(8192, 2, SEQ)
        k_now = view(8704, SEQ)
        v_now = view(8960, TOK, HEAD)
        sq_tmp = view(9216, 2, SEQ)
        rt_tmp = view(9728, 2, SEQ)
        qn_tmp = view(10240, 2, SEQ)
        x_q = view(10752, X_HEADS, SEQ)
        x_y = view(11776, X_HEADS, SEQ)
        AR = view(0, 2, NCH, 2, P)
        KB = view(2048, 2, NCH, 2, P)
        KBt = rows[:, :, :, :].rearrange("p a b c -> p (a b c)").rearrange("p (d c w n) -> p d c w n", d=2, c=NCH, w=2)
        GT = view(4096, 2, NCH, 3, P)
        XA = view(7168, 2, NCH, P)
        XTA = view(8192, 2, NCH, P)
        XB = view(9216, 2, NCH, P)
        XTB = view(10240, 2, NCH, P)
        ET = view(11264, 2, NCH, P)
        EE = view(12288, 2, NCH, P)
        OFF = {32: view(13312, 2, NCH, P),
               64: low_in[:, :, :].rearrange("p a b -> p (a b)").rearrange("p (d c n) -> p d c n", d=2, c=NCH)}
        tb = tok_buf[:, :, :].rearrange("p a b -> p (a b)")

        def tview(off, *shape):
            n = int(np.prod(shape))
            names = "abcd"[:len(shape)]
            v = tb[:, off:off + n]
            if len(shape) == 1:
                return v
            return v.rearrange(f"p ({' '.join(names)}) -> p {' '.join(names)}", **dict(zip(names, shape)))

        sig = tview(0, 4, SEQ)
        inc = tview(1024, 2, SEQ)
        exc = tview(1536, 2, SEQ)
        p_inc = tview(2048, 2, SEQ)
        p_inv = tview(2560, 2, SEQ)
        p_exc = tview(3072, 2, SEQ)
        kd = tview(3584, 2, SEQ)
        ar_side = tb[:, 1024:1024 + 4096 - 1024].rearrange("p (x d c n) -> p x d c n", x=6, d=2, c=NCH)[:, 0:5:4]
        b_side = tview(512, 2, NCH, HEAD)
        AT_c = tview(0, 2, NCH, HEAD)
        A_c = tview(1536, 2, NCH, HEAD)
        XT_c = tview(2560, 2, NCH, HEAD)
        X_c = tview(512, 2, NCH, HEAD)
        E_c = tview(3584, 2, NCH, HEAD)
        X2_c = tb[:, 1024:4096].rearrange("p (x d c n) -> p x d c n", x=6, d=2, c=NCH)[:, 0:5:4]
        P_c = X_c
        v_cur = sb("v_cur", [P, SEQ])
        tmp = sb("tmp", [P, SEQ])
        tmp2 = sb("tmp2", [P, SEQ])
        g_cur = sb("g_cur", [P, SEQ])
        Vc = sb("Vc", [P, NCH, HEAD])
        Yc = sb("Yc", [P, NCH, HEAD])
        Wc = sb("Wc", [P, 2, HEAD])
        Uc = sb("Uc", [P, 2, HEAD])
        St = sb("St", [P, 2, HEAD])
        prow = view(0, DEPTH, 2, P)
        junk = view(0, D_MODEL)
        gain_row = view(2048, D_MODEL)
        hidT = view(4096, 16, SEQ)

        psum = ctx.enter_context(nc.psum_tensor("psum", [P, 8, 512], F32))
        gates = streams[:, 1:5, :].rearrange("p (t b) d -> p t (b d)", t=TOK).rearrange("p t (u n) -> p u t n", n=UNIT)
        acc = psum[:, 0:4, :].rearrange("p (u t) n -> p u t n", t=TOK)
        work = psum[:, 4:8, :]
        gate_acc = psum[:, 6:8, :]
        x_saved = nc.dram_tensor("x_saved", [P, TOK, D_MODEL], F32, kind="Internal").ap()

        def cst(name):
            o, w = CONST[name]
            return const[:, o:o + w]

        ident, head_ones, rot = cst("ident"), cst("head_ones"), cst("rot")
        mask = cst("mask").rearrange("p (d n) -> p d n", d=2)

        def col(l, name, j=0, n=1):
            return cols[:, l, PCOL[name] + j:PCOL[name] + j + n]

        def colv(l, name, n):
            return cols[:, l, PCOL[name]:PCOL[name] + n]

        s_const = sem("constants_landed")
        s_rows_zero = sem("param_rows_zeroed")
        s_rows = sem("param_rows_landed")
        s_x = sem("x_landed")
        s_mem = sem("mem_landed")
        s_mem_free = sem("tok_buf_free_for_mem")
        s_gain = sem("gain_row_landed")
        s_gain_free = sem("gain_row_free")
        s_lw = sem("lora_weights_landed")
        s_lw_free = sem("lora_weights_free")
        s_land = [sem(f"slab_landed{i}") for i in range(RING)]
        s_used = sem("slab_used")
        s_asked = sem("branch_weights_asked_for")
        s_emptied = sem("unit_emptied")
        s_branch = sem("branch_unit_emptied")
        s_gate = sem("gate_unit_emptied")
        s_x_idle = sem("x_idle_from_vector")
        s_x_saved = sem("x_saved_in_dram")
        s_x_back = sem("x_back_in_place")
        s_rows_free = sem("unit_rows_transposed")
        s_full = sem("work_bank_full")
        s_drained = sem("work_bank_drained")
        s_sfull = sem("scan_bank_full")
        s_sdrained = [sem(f"scan_bank{b}_drained") for b in range(SCAN_BANKS)]
        s_pool = sem("pool_result")
        s_for_pool = sem("vector_result_for_pool")
        s_act_pe = sem("scalar_result_for_tensor")
        s_act = sem("scalar_step")
        s_dve = sem("vector_step")
        s_for_pe = sem("vector_result_for_tensor")
        s_for_act = sem("vector_result_for_scalar")
        s_from_act = sem("scalar_result_for_vector")
        s_out = sem("output_stored")

        w_in = a["w_in"]
        C_LORA, C_Q = 3 * RW_WIDTH, RW_COLS
        C_KV, C_G = RW_COLS + AT_Q, RW_COLS + AT_COLS

        def slabs_of(w2d, ncols):
            return w2d.rearrange("(s t p) (u n) -> u s p t n", t=SLAB_K, p=P, n=ncols)

        rows_landed = Tally(s_rows, 16)

        block = ctx.enter_context(nc.Block())

        @block.sync
        def _(sp):
            slab = Tally(s_used)
            sp.dma_start(const[:, :], a["shape_constants"]).then_inc(s_const, 16)
            sp.dma_start(x, a["x"].rearrange("b (t p) d -> p (b t) d", p=P)).then_inc(s_x, 16)

            def load(src, note=False):
                slot = slab.count % RING
                if slab.count >= RING:
                    sp.wait_ge(s_used, slab.at(RING - 1))
                    if note:
                        sp.sem_inc(s_asked, 1)
                slab.next()
                for dst, part in src(ring[:, slot]):
                    sp.dma_start(dst, part).then_inc(s_land[slot], 32 // len(src(ring[:, slot])))

            def whole(part):
                w = part.shape[-1]
                return lambda r: [(r[:, :, 0:w], part)]

            for l in range(DEPTH):
                mem_w = slabs_of(a["x_wkv"][l], UNIT)
                for u in range(2):
                    for s in range(8):
                        load(whole(mem_w[u, s]))
                rkv = slabs_of(w_in[l][:, 0:3 * RW_WIDTH], UNIT)
                with repeat(sp, 3, {slab: 16}) as i:
                    for j in range(2):
                        v = rkv.rearrange("(i j) s p t n -> j i s p t n", j=2)[j]
                        for s in range(8):
                            load(whole(v[i, s]))
                lora = slabs_of(w_in[l][:, C_LORA:C_LORA + LORA_COLS], LORA_COLS)
                for s in range(8):
                    load(whole(lora[0, s]))
                qkv = slabs_of(w_in[l][:, C_Q:C_Q + AT_COLS], UNIT)
                for u in range(3):
                    for s in range(8):
                        load(whole(qkv[u, s]))
                gate_w = slabs_of(w_in[l][:, C_G:C_G + 2 * D_MODEL], UNIT)
                wr, wa = slabs_of(a["w_rw_out"][l], UNIT), slabs_of(a["w_at_out"][l], UNIT)
                with repeat(sp, PAIRS, {slab: 8}) as i:
                    for s in range(8):
                        load(whole(gate_w[i, s]))
                with repeat(sp, 4, {slab: 8}) as i:
                    for s in range(4):
                        load(whole(wr[i, s]), note=s == 0)
                    for s in range(4):
                        load(whole(wa[i, s]))
                wo = slabs_of(a["w_o"][l], UNIT)
                with repeat(sp, 4, {slab: 8}) as i:
                    for s in range(8):
                        load(whole(wo[i, s]))
                xq = slabs_of(a["x_wq"][l], UNIT)
                for s in range(8):
                    load(whole(xq[0, s]))
                xo = slabs_of(a["x_wo"][l], UNIT)
                for u in range(4):
                    for s in range(2):
                        load(whole(xo[u, s]))
                wg, wu = slabs_of(a["ffn_wg"][l], 256), slabs_of(a["ffn_wu"][l], 256)
                t0 = 0
                for tiles in FF_PARTS:
                    n = tiles // 2
                    g_v = wg[t0 // 2:t0 // 2 + n].rearrange("(i j) s p t n -> j i s p t n", j=2)
                    u_v = wu[t0 // 2:t0 // 2 + n].rearrange("(i j) s p t n -> j i s p t n", j=2)
                    with repeat(sp, n // 2, {slab: 16}) as i:
                        for j in range(2):
                            for s in range(8):
                                load(lambda r, j=j, s=s: [(r[:, :, 0:256], g_v[j][i, s]), (r[:, :, 256:512], u_v[j][i, s])])
                    wd = slabs_of(a["ffn_wd"][l][t0 * P:(t0 + tiles) * P, :], UNIT)
                    wd_v = wd.rearrange("(i j) s p t n -> j i s p t n", j=2)
                    with repeat(sp, 2, {slab: tiles}) as i:
                        for j in range(2):
                            for s in range(tiles // 2):
                                load(whole(wd_v[j][i, s]))
                    t0 += tiles
            sp.wait_ge(s_out, 1)
            sp.dma_start(out.rearrange("b (t p) d -> p (b t) d", p=P), x).then_inc(s_x, 16)
            sp.wait_ge(s_x, 32)

        @block.gpsimd
        def _(pool):
            pool.wait_ge(s_rows_zero, 1)
            for l in range(DEPTH):
                for g, group in enumerate(PARAM_ROWS):
                    r0 = 0
                    for name, n in group:
                        if name == "qk_norm":
                            srcs = []
                            for j in range(n):
                                g_src = a["at_q_norm" if j < 4 else "at_k_norm"][l:l + 1, :]
                                for h in range(2):
                                    pool.dma_start(prow[r0 + j:r0 + j + 1, l, g, h * HEAD:(h + 1) * HEAD],
                                                   g_src).then_inc(s_rows, 16)
                                    rows_landed.next()
                            r0 += n
                            continue
                        if name == "rw_v0":
                            if l == 0:
                                r0 += n
                                continue
                            src = a[name][l - 1]
                        elif name in ("rw_w0", "rw_a0"):
                            src = a[name][l].rearrange("d c -> (d c)")
                        elif name == "rw_r_k":
                            src = a[name][l].rearrange("h c -> (h c)")
                        else:
                            src = a[name][l]
                        full = src.shape[0] // P
                        pool.dma_start(prow[r0:r0 + full, l, g, :],
                                       src[0:full * P].rearrange("(r c) -> r c", c=P)).then_inc(s_rows, 16)
                        rows_landed.next()
                        rest = src.shape[0] - full * P
                        if rest:
                            pool.dma_start(prow[r0 + full:r0 + full + 1, l, g, 0:rest],
                                           src[full * P:].rearrange("(r c) -> r c", r=1)).then_inc(s_rows, 16)
                            rows_landed.next()
                        r0 += n
            pool.dma_start(vdown[:, :, :], a["rw_v_down"][0].rearrange("(t p) n -> p t n", p=P)).then_inc(s_rows, 16)
            rows_landed.next()
            landed = Tally(s_lw, 16)
            for_pool = Tally(s_for_pool)
            gain = Tally(s_gain_free)
            for l in range(DEPTH):
                pool.wait_ge(s_mem_free, l + 1)
                pool.dma_start(tok_buf[:, :, :], a["mem"].rearrange("b (t p) d -> p (b t) d", p=P)).then_inc(s_mem, 16)
                n_lw = 7 if l else 6
                if l:
                    pool.wait_ge(s_x_idle, 2 * l + 1)
                    pool.dma_start(x_saved, x).then_inc(s_x_saved, 16)
                with repeat(pool, PAIRS, {landed: n_lw, for_pool: 1}) as i:
                    pool.wait_ge(s_lw_free, i + (l * (PAIRS + 1) + 1))
                    for d in range(2):
                        w_v = a["rw_w_up"][l, d].rearrange("r (i c) -> i r c", c=P)
                        a_v = a["rw_a_up"][l, d].rearrange("r (i c) -> i r c", c=P)
                        pool.dma_start(lora_w[d * 64:(d + 1) * 64, 0, :], w_v[i]).then_inc(s_lw, 16)
                        pool.dma_start(lora_w[d * 64:(d + 1) * 64, 1, :], a_v[i]).then_inc(s_lw, 16)
                        landed.next(2)
                    g_v = a["rw_g_up"][l].rearrange("r (i c) -> i r c", c=P)
                    pool.dma_start(lora_w[:, 2, :], g_v[i, 0:P]).then_inc(s_lw, 16)
                    pool.dma_start(lora_w[0:32, 3, :], g_v[i, P:G_LORA]).then_inc(s_lw, 16)
                    landed.next(2)
                    if l:
                        v_v = a["rw_v_up"][l - 1].rearrange("r (i c) -> i r c", c=P)
                        pool.dma_start(lora_w[32:32 + V_LORA, 3, :], v_v[i]).then_inc(s_lw, 16)
                        landed.next()
                    pool.wait_ge(s_for_pool, for_pool.next())
                    for d in range(2):
                        for n in (32, 64):
                            in_n = cst(f"in{n}").rearrange("p (h n) -> p h n", h=2).unsqueeze(1).to_broadcast([P, NCH, 2, HEAD])
                            ins = nc.gpsimd.tensor_tensor(OFF[n][:, d].rearrange("p c (h n) -> p c h n", h=2),
                                                          A_c[:, d].unsqueeze(2).to_broadcast([P, NCH, 2, HEAD]), in_n, ALU.mult)
                    ins.then_inc(s_pool, 1)
                for name in ("n_mix_post", "n_x_post", "n_ffn_post"):
                    if name == "n_x_post":
                        if l:
                            pool.wait_ge(s_x_saved, 16 * l)
                        pool.wait_ge(s_x_idle, 2 * l + 2)
                        pool.dma_start(x, x_saved if l else a["x"].rearrange("b (t p) d -> p (b t) d", p=P)).then_inc(s_x_back, 16)
                    pool.wait_ge(s_gain_free, gain.next())
                    pool.dma_start(gain_row, a[name][l].partition_broadcast(P)).then_inc(s_gain, 16)

        @block.tensor
        def _(pe):
            slab = Tally(s_used)
            emptied = Tally(s_emptied)
            branch = Tally(s_branch)
            branch.next(2)
            gate = Tally(s_gate)
            gate.next()
            full = Tally(s_full)
            for_pe = Tally(s_for_pe)
            lw = Tally(s_lw, 16)
            scan = Banks(Tally(s_sfull), s_sdrained)
            scan_before, scan_last, scan_start = None, [None], [0]
            from_act = Tally(s_act_pe)
            from_pool = Tally(s_pool)

            def unit(ub, nslab, operand, k0=0, width=UNIT, wait=True, between=None):
                if wait:
                    if emptied.count >= 2:
                        pe.wait_ge(s_emptied, emptied.at(1))
                    emptied.next()
                for s in range(nslab):
                    slot, use = slab.count % RING, slab.count // RING + 1
                    val = 32 * use if slab.loop is None else slab.loop[0] * (slab.loop[1] // RING * 32) + 32 * use
                    slab.next()
                    pe.wait_ge(s_land[slot], val)
                    for t in range(SLAB_K):
                        for tok in range(TOK):
                            k = SLAB_K * s + t
                            last = nc.tensor.matmul(acc[:, ub, tok, 0:width], operand[:, k0 + k, tok * P:(tok + 1) * P],
                                                    ring[:, slot, t, 0:width], start=k == 0, stop=k == SLAB_K * nslab - 1)
                    last.then_inc(s_used, 1)
                    if between and s == nslab // 2 - 1:
                        between()

            def gate_unit():
                pe.wait_ge(s_gate, gate.at())
                gate.next()
                for s in range(8):
                    slot, use = slab.count % RING, slab.count // RING + 1
                    pe.wait_ge(s_land[slot], slab.loop[0] * (slab.loop[1] // RING * 32) + 32 * use)
                    slab.next()
                    for t in range(SLAB_K):
                        for tok in range(TOK):
                            k = SLAB_K * s + t
                            last = nc.tensor.matmul(gate_acc[:, tok, :], opT[:, k, tok * P:(tok + 1) * P], ring[:, slot, t, :],
                                                    start=k == 0, stop=k == KD - 1)
                            if (t, tok) == (SLAB_K - 1, TOK - 1):
                                last.then_inc(s_used, 1)
                            yield

            def settle():
                if emptied.count:
                    pe.wait_ge(s_emptied, emptied.at())

            def fill(products, aligned=False):
                b = full.count % 4
                if full.count >= 4:
                    pe.wait_ge(s_drained, full.at(3))
                last = products(work[:, b, :])
                n = 1 + (-(full.count + 1) % 4 if aligned else 0)
                last.then_inc(s_full, n)
                full.next(n)
                return full.at()

            def have(n):
                pe.wait_ge(s_drained, n)

            def transpose_unit(ub, tiles, lag, aligned=False):
                pe.wait_ge(s_emptied, emptied.at(lag))
                for b0 in range(0, len(tiles), 2):
                    def go(bank):
                        for j, w in enumerate(tiles[b0:b0 + 2]):
                            for tok in range(TOK):
                                c0 = (b0 + j) * P
                                last = nc.tensor.transpose(bank[0:w, j * SEQ + tok * P:j * SEQ + (tok + 1) * P],
                                                           rows[:, ub, tok, c0:c0 + w], ident)
                        return last
                    fill(go, aligned and b0 + 2 >= len(tiles))

            def transpose_tok(n_src=TOK):
                for tok in range(TOK):
                    pe.wait_ge(s_for_pe, for_pe.next())
                    for g in range(KD // 4):
                        def go(bank):
                            for j in range(4):
                                k = 4 * g + j
                                last = nc.tensor.transpose(bank[:, j * P:(j + 1) * P], tok_buf[:, tok, k * P:(k + 1) * P], ident)
                            return last
                        n = fill(go)
                have(n)
                settle()

            def sfill(products, pad=0):
                nonlocal scan_before
                b, free = scan.now()
                pe.wait_ge(s_sdrained[b], free)
                scan_before = scan_last[0]
                last = products(psum[:, b, :])
                n = 1 if not pad else pad - (scan.tally.count - scan_start[0])
                last.then_inc(s_sfull, n)
                scan.tally.next(n)
                scan_last[0] = (b, free + 2)
                return scan_last[0]

            def shave(q):
                pe.wait_ge(s_sdrained[q[0]], q[1])

            def softmax_turn():
                for b in range(4):
                    def go(bank):
                        for st in range(2):
                            for qt in range(2):
                                last = nc.tensor.transpose(bank[:, st * SEQ + qt * P:st * SEQ + (qt + 1) * P],
                                                           prob[:, 2 * b + qt, st * P:(st + 1) * P], ident)
                        return last
                    if b == 0:
                        have(full.at())
                    n = fill(go)
                have(n)

            pe.wait_ge(s_const, 16)
            pe.wait_ge(s_rows, rows_landed.at())
            for l in range(DEPTH):
                for g in range(2):
                    n = GROUP_ROWS[g]
                    fill(lambda bank: nc.tensor.transpose(bank[:, 0:n], prow[0:n, l, g, :], ident[0:n, 0:n]))
            for l in range(DEPTH):
                transpose_tok()
                unit(0, 8, opT)
                unit(1, 8, opT)
                transpose_unit(0, [P] * 4, 1)
                transpose_tok()
                with repeat(pe, 3, {slab: 16, emptied: 2, full: 4}):
                    unit(0, 8, opT)
                    unit(1, 8, opT, between=lambda: transpose_unit(0, [P] * 4, 1))
                    transpose_unit(1, [P] * 4, 0)
                unit(0, 8, opT, width=LORA_COLS)
                unit(1, 8, opT, between=lambda: transpose_unit(0, LORA_W, 1))
                unit(0, 8, opT, between=lambda: transpose_unit(1, [P] * 4, 1))
                unit(1, 8, opT, between=lambda: transpose_unit(0, [P] * 4, 1))
                transpose_unit(1, [P] * 2, 0, aligned=True)
                with repeat(pe, 5, {full: 4, for_pe: 2}):
                    pe.wait_ge(s_for_pe, for_pe.next())
                    fill(lambda bank: nc.tensor.matmul(bank, head_ones, sq_tmp, start=True, stop=True))
                    pe.wait_ge(s_for_pe, for_pe.next())
                    fill(lambda bank: nc.tensor.matmul(bank, rot, qn_tmp, start=True, stop=True), aligned=True)
                with repeat(pe, AT_KV_HEADS, {full: 12, for_pe: 1}):
                    pe.wait_ge(s_for_pe, for_pe.next())
                    for tile in range(2):
                        for h in range(2):
                            def go(bank):
                                for qt in range(2):
                                    last = nc.tensor.matmul(bank[:, qt * SEQ:(qt + 1) * SEQ],
                                                            q_now[h * HEAD:(h + 1) * HEAD, tile, qt * P:(qt + 1) * P],
                                                            k_now[h * HEAD:(h + 1) * HEAD, :], start=True, stop=True)
                                return last
                            fill(go)
                    softmax_turn()

                    def values(bank):
                        for tile in range(2):
                            for h in range(2):
                                for st in range(2):
                                    last = nc.tensor.matmul(bank[h * HEAD:(h + 1) * HEAD, tile * SEQ:(tile + 1) * SEQ],
                                                            v_now[:, st, :], probT[:, 2 * tile + h, st * SEQ:(st + 1) * SEQ],
                                                            start=st == 0, stop=st == 1)
                        return last
                    fill(values, aligned=True)
                if l:
                    pe.wait_ge(s_for_pe, for_pe.next())
                    def low(bank):
                        for j in range(PAIRS):
                            last = nc.tensor.matmul(bank[0:V_LORA, 0:SEQ], vdown[:, j, :], v_all[:, j, :],
                                                    start=j == 0, stop=j == PAIRS - 1)
                        return last
                    fill(low, aligned=True)
                pe.wait_ge(s_for_pe, for_pe.next())
                settle()
                with repeat(pe, PAIRS, {scan.tally: PER_PAIR, for_pe: 4, from_act: 1, from_pool: 1, slab: 8, gate: 1, lw: 7 if l else 6}):
                    scan_start[0] = scan.tally.count
                    beside = gate_unit()

                    def step(n=1):
                        for _ in range(n):
                            next(beside, None)
                    pe.wait_ge(s_lw, lw.next(7 if l else 6))
                    sfill(lambda bank: nc.tensor.matmul(bank, lora_w[:, 0, :], lora_in[:, 0], start=True, stop=True))
                    sfill(lambda bank: nc.tensor.matmul(bank, lora_w[:, 1, :], lora_in[:, 1], start=True, stop=True))
                    if l:
                        sfill(lambda bank: nc.tensor.matmul(bank[:, 0:SEQ], lora_w[32:32 + V_LORA, 3, :], v_low, start=True, stop=True))

                    def gate_low(bank):
                        nc.tensor.matmul(bank[:, 0:SEQ], lora_w[:, 2, :], lora_in[:, 2, 0, :], start=True, stop=False)
                        return nc.tensor.matmul(bank[:, 0:SEQ], lora_w[0:32, 3, :], lora_in[0:32, 2, 1, :], start=False, stop=True)
                    sfill(gate_low)
                    step(6)
                    pe.wait_ge(s_for_pe, for_pe.next())
                    sfill(lambda bank: nc.tensor.matmul(bank[:, 0:SEQ], head_ones, tmp[:, :], start=True, stop=True))
                    sfill(lambda bank: nc.tensor.matmul(bank[:, 0:SEQ], head_ones, tmp2[:, :], start=True, stop=True))

                    def v_turn(bank):
                        for c2 in range(NCH // 2):
                            last = nc.tensor.transpose(bank[:, c2 * P:(c2 + 1) * P], v_cur[:, c2 * P:(c2 + 1) * P], ident)
                        return last
                    sfill(v_turn)
                    step(8)
                    pe.wait_ge(s_act_pe, from_act.next())
                    for d in range(2):
                        for c2 in range(0, NCH, 2):
                            def go(bank):
                                for j in range(2):
                                    for w in range(2):
                                        o = bank[:, (2 * j + w) * P:(2 * j + w + 1) * P].rearrange("p (x n) -> p x n", x=2)
                                        last = nc.tensor.matmul(o, KB[:, d, c2 + j, w, :], ar_side[:, :, d, c2 + j, :], start=True, stop=True)
                                return last
                            sfill(go)

                    def natural(bank):
                        for d in range(2):
                            for c in range(NCH):
                                o = bank[:, (d * NCH + c) * HEAD:(d * NCH + c + 1) * HEAD]
                                last = nc.tensor.matmul(o, AR[:, d, c, 0, :], b_side[:, d, c, :], start=True, stop=True)
                        return last
                    sfill(natural)
                    for d in range(2):
                        for c2 in range(0, NCH, 2):
                            def go(bank):
                                for j in range(4):
                                    last = nc.tensor.transpose(bank[:, j * P:(j + 1) * P], KB[:, d, c2 + j // 2, j % 2, :], ident)
                                return last
                            sfill(go)

                    def blocks(*products):
                        def go(bank):
                            for k, (lhs, rhs) in enumerate(products):
                                for c in range(NCH):
                                    o = bank[:, (k * NCH + c) * HEAD:(k * NCH + c + 1) * HEAD]
                                    last = nc.tensor.matmul(o, lhs[:, c, :], rhs[:, c, :], start=True, stop=True)
                            return last
                        return go

                    def turned(src):
                        def go(bank):
                            for c in range(NCH):
                                last = nc.tensor.transpose(bank[:, c * P:(c + 1) * P], src[:, c, :], ident)
                            return last
                        return go

                    step(3)
                    done = {}
                    for d in range(2):
                        pe.wait_ge(s_for_pe, for_pe.next())
                        done[d] = sfill(blocks((XTA[:, d], X_c[:, d]), (XA[:, d], XT_c[:, d])))
                    for d in range(2):
                        shave(done[d])
                        sfill(blocks((XB[:, d], E_c[:, d]), (XTB[:, d], X2_c[:, 0, d])))
                        done[d] = sfill(blocks((XB[:, d], X2_c[:, 1, d])))
                        done[d, 1] = scan_before
                    for d in range(2):
                        shave(done[d, 1])
                        shave(done[d])
                        done[d] = sfill(blocks((XA[:, d], E_c[:, d]), (XTA[:, d], X_c[:, d])))
                    for d in range(2):
                        shave(done[d])
                        done[d] = sfill(blocks((XB[:, d], E_c[:, d])))
                    pe.wait_ge(s_pool, from_pool.next())
                    for n in (32, 64):
                        for d in range(2):
                            shave(done[d])
                            done[d, 1] = sfill(blocks((OFF[n][:, d], E_c[:, d])))
                            done[d] = sfill(turned(EE[:, d]))
                        for d in range(2):
                            shave(done[d, 1])
                            shave(done[d])
                            done[d] = sfill(blocks((ET[:, d], P_c[:, d])))
                    shave(done[0])
                    shave(done[1])
                    for n in range(NCH):
                        at = (n, NCH - 1 - n)

                        def go_w(bank):
                            for d, c in enumerate(at):
                                o = bank[:, d * HEAD:(d + 1) * HEAD]
                                if n:
                                    nc.tensor.matmul(o, AR[:, d, c, 0, :], St[:, d, :], start=True, stop=False)
                                last = nc.tensor.matmul(o, GT[:, d, c, 2, :], Vc[:, c, :], start=n == 0, stop=True)
                            return last

                        def go_u(bank):
                            for d, c in enumerate(at):
                                last = nc.tensor.matmul(bank[:, d * HEAD:(d + 1) * HEAD], EE[:, d, c, :], Wc[:, d, :], start=True, stop=True)
                            return last

                        def go_y(bank):
                            for d, c in enumerate(at):
                                o = bank[:, d * HEAD:(d + 1) * HEAD]
                                if n:
                                    nc.tensor.matmul(o, AR[:, d, c, 1, :], St[:, d, :], start=True, stop=False)
                                nc.tensor.matmul(o, GT[:, d, c, 0, :], Uc[:, d, :], start=n == 0, stop=False)
                                last = nc.tensor.matmul(o, GT[:, d, c, 1, :], Vc[:, c, :], start=False, stop=True)
                            return last

                        def go_s(bank):
                            for d, c in enumerate(at):
                                o = bank[:, d * HEAD:(d + 1) * HEAD]
                                nc.tensor.matmul(o, KBt[:, d, c, 0, :], Uc[:, d, :], start=True, stop=False)
                                last = nc.tensor.matmul(o, KBt[:, d, c, 1, :], Vc[:, c, :], start=False, stop=True)
                            return last
                        n_w = sfill(go_w)
                        step()
                        shave(n_w)
                        n_u = sfill(go_u)
                        step()
                        shave(n_u)
                        if n < NCH - 1:
                            n_s = sfill(go_s)
                            sfill(go_y)
                            step()
                            shave(n_s)
                        else:
                            sfill(go_y)
                    step(KD * TOK)
                    pe.wait_ge(s_for_pe, for_pe.next())

                    def y_turn(bank):
                        for c2 in range(NCH // 2):
                            two_chunks = Yc[:, 2 * c2:2 * c2 + 2, :].rearrange("p c n -> p (c n)")
                            last = nc.tensor.transpose(bank[:, c2 * P:(c2 + 1) * P], two_chunks, ident)
                        return last
                    sfill(y_turn, pad=PER_PAIR)
                pe.wait_ge(s_gate, gate.at())
                pe.wait_ge(s_for_pe, for_pe.next())
                with repeat(pe, 4, {slab: 8, branch: 2}):
                    pe.wait_ge(s_branch, branch.at(1))
                    unit(0, 4, y_rw, wait=False)
                    pe.wait_ge(s_branch, branch.at())
                    unit(1, 4, y_at, wait=False)
                    branch.next(2)
                pe.wait_ge(s_branch, branch.at())
                transpose_tok()
                with repeat(pe, 2, {slab: 16, emptied: 2}):
                    unit(0, 8, opT)
                    unit(1, 8, opT)
                transpose_tok()
                unit(0, 8, opT)
                transpose_unit(0, [P] * 4, 0, aligned=True)
                have(full.at())
                for b in range(X_HEADS):
                    def go(bank):
                        for qt in range(2):
                            last = nc.tensor.matmul(bank[:, qt * SEQ:(qt + 1) * SEQ], x_q[:, b, qt * P:(qt + 1) * P], memk[:, b, :],
                                                    start=True, stop=True)
                        return last
                    fill(go)
                softmax_turn()
                for b2 in range(2):
                    def go(bank):
                        for j in range(2):
                            for st in range(2):
                                b = 2 * b2 + j
                                last = nc.tensor.matmul(bank[:, j * SEQ:(j + 1) * SEQ], memv[:, st, b * X_HEAD:(b + 1) * X_HEAD],
                                                        probT[:, b, st * SEQ:(st + 1) * SEQ], start=st == 0, stop=st == 1)
                        return last
                    n = fill(go, aligned=b2 == 1)
                have(n)
                unit(1, 2, x_y)
                for u in range(1, 4):
                    unit((u + 1) % 2, 2, x_y)
                transpose_tok()
                ub = 1
                for tiles in FF_PARTS:
                    settle()
                    with repeat(pe, tiles // 4, {slab: 16, emptied: 2, full: 4}):
                        unit(1, 8, opT)
                        unit(0, 8, opT, between=lambda: transpose_unit(1, [P] * 2, 1))
                        transpose_unit(0, [P] * 2, 0, aligned=True)
                    have(full.at())
                    with repeat(pe, 2, {slab: tiles, emptied: 2}):
                        unit(1, tiles // 2, hidT)
                        unit(0, tiles // 2, hidT)

        @block.scalar
        def _(act):
            slab = Tally(s_used)
            for_act = Tally(s_for_act)
            rows_free = Tally(s_rows_free)

            def unit_rows(ub, nslab, width=UNIT, turned=True):
                if rows_free.count >= 2:
                    act.wait_ge(s_rows_free, rows_free.at(1))
                if turned:
                    rows_free.next()
                act.wait_ge(s_used, slab.next(nslab))
                nc.scalar.activation(rows[:, ub, :, 0:width], acc[:, ub, :, 0:width], ACT.Copy).then_inc(s_emptied, 1)

            def skip(n):
                scan.tally.next(n)

            def sbank(shared=False):
                b, free = scan.now()
                act_bank[0] = b
                if shared:
                    act.wait_ge(s_sdrained[b], free + 1)
                    scan.tally.next()
                else:
                    act.wait_ge(s_sfull, scan.tally.next())
                return psum[:, b, :]

            def sdrain(ins, n=2):
                ins.then_inc(s_sdrained[act_bank[0]], n)

            def turned_pairs(dst, bank):
                src = bank[:, 0:2 * P].rearrange("p (c n) -> p c n", c=2)
                for h in range(2):
                    for odd in range(2):
                        ins = nc.scalar.activation(dst[h * HEAD:(h + 1) * HEAD, :, odd, :],
                                                   src[odd * HEAD:(odd + 1) * HEAD, :, h * HEAD:(h + 1) * HEAD], ACT.Copy)
                sdrain(ins)

            def rms(src):
                for tok in range(TOK):
                    nc.scalar.activation(junk, src[:, tok, :], ACT.Square, accum_out=stat[:, tok:tok + 1]).then_inc(s_from_act, 1)
                    if tok == 0:
                        act.wait_ge(s_from_act, from_act.next())
                    else:
                        from_act.next()
                root(stat[:, 2:4])

            def root(v):
                act.wait_ge(s_for_act, for_act.next())
                nc.scalar.activation(v, v, ACT.Sqrt).then_inc(s_from_act, 1)
                from_act.next()

            def exps(scale):
                act.wait_ge(s_for_act, for_act.next())
                for k in range(8):
                    last = nc.scalar.activation(prob[:, k, :], work[:, k // 2, (k % 2) * SEQ:(k % 2 + 1) * SEQ], ACT.Exp,
                                                bias=stat[:, 16 + k:17 + k], scale=scale, accum_out=stat[:, 24 + k:25 + k])
                last.then_inc(s_from_act, 1)
                from_act.next()

            from_act = Tally(s_from_act)
            scan = Banks(Tally(s_sfull), s_sdrained)
            act_bank = [0]
            act.sem_inc(s_gate, 1)
            for l in range(DEPTH):
                act.wait_ge(s_mem, 16 * (l + 1))
                if l == 0:
                    act.wait_ge(s_x, 16)
                act.wait_ge(s_for_act, for_act.next())
                rms(tok_buf)
                unit_rows(0, 8)
                unit_rows(1, 8, turned=False)
                act.wait_ge(s_for_act, for_act.next())
                rms(x)
                with repeat(act, 3, {slab: 16, rows_free: 2}):
                    unit_rows(0, 8)
                    unit_rows(1, 8)
                unit_rows(0, 8, LORA_COLS)
                unit_rows(1, 8)
                unit_rows(0, 8)
                unit_rows(1, 8)
                with repeat(act, 5, {for_act: 1, from_act: 1}):
                    root(rt_tmp)
                with repeat(act, AT_KV_HEADS, {for_act: 1, from_act: 1}):
                    exps(HEAD ** -0.5)
                act.wait_ge(s_for_act, for_act.next())
                for d in range(2):
                    r = slice(d * 64, (d + 1) * 64)
                    nc.scalar.activation(lora_in[r, 0, d, :], low_in[r, 0, :], ACT.Tanh)
                nc.scalar.activation(lora_in[:, 2, 0, :], low_in[:, 2, :], ACT.Sigmoid)
                nc.scalar.activation(lora_in[0:32, 2, 1, :], low_in[0:32, 3, :], ACT.Sigmoid).then_inc(s_from_act, 1)
                from_act.next()
                if l:
                    act.wait_ge(s_x_saved, 16 * l)
                with repeat(act, PAIRS, {scan.tally: PER_PAIR, for_act: 5, from_act: 3, slab: 8}) as i:
                    start = scan.tally.count
                    act.wait_ge(s_for_act, for_act.next())
                    if l:
                        nc.scalar.activation(tmp2[:, :], tmp2[:, :], ACT.Sigmoid)
                    nc.scalar.activation(sig, sig, ACT.Sigmoid).then_inc(s_from_act, 1)
                    from_act.next()
                    skip(3 if l else 2)
                    bank = sbank()
                    sdrain(nc.scalar.activation(g_cur[:, :], bank[:, 0:SEQ], ACT.Copy))
                    bank = sbank()
                    sdrain(nc.scalar.activation(tmp[:, :], bank[:, 0:SEQ], ACT.Sqrt))
                    skip(1)
                    act.wait_ge(s_for_act, for_act.next())
                    nc.scalar.activation(p_inc, inc, ACT.Exp, scale=-DECAY)
                    nc.scalar.activation(p_inv, inc, ACT.Exp, scale=DECAY)
                    nc.scalar.activation(p_exc, exc, ACT.Exp, scale=-DECAY).then_inc(s_from_act, 1)
                    from_act.next()
                    v_bank = sbank()
                    turned_pairs(Vc[:, :, :].rearrange("p (c k) n -> p c k n", k=2), v_bank)
                    act.wait_ge(s_for_act, for_act.next())
                    for h in range(2):
                        r, o = slice(h * HEAD, (h + 1) * HEAD), slice(h * HEAD, (h + 1) * HEAD)
                        for buf, which, src in ((KB, 0, b_side), (KB, 1, E_c), (AR, 0, ar_side[:, 1]), (AR, 1, ar_side[:, 0])):
                            ins = nc.scalar.activation(buf[r, :, :, which, o], src[r], ACT.Copy)
                    ins.then_inc(s_act_pe, 1)
                    skip(5)
                    for d in range(2):
                        for c2 in range(0, NCH, 2):
                            bank = sbank()
                            sdrain(nc.scalar.activation(KBt[:, d, c2:c2 + 2].rearrange("p c w n -> p (c w n)"), bank, ACT.Copy))
                    for d in range(2):
                        bank = sbank(shared=True)
                        sdrain(nc.scalar.activation(X2_c[:, :, d], bank.rearrange("p (x c n) -> p x c n", x=2, c=NCH), ACT.Copy), 1)
                    for d in range(2):
                        bank = sbank(shared=True)
                        sdrain(nc.scalar.activation(X_c[:, d].rearrange("p c n -> p (c n)"), bank[:, 256:512], ACT.Copy), 1)
                        skip(1)
                    skip(4)
                    for n in (32, 64):
                        for d in range(2):
                            skip(1)
                            bank = sbank()
                            sdrain(nc.scalar.activation(ET[:, d].rearrange("p c n -> p (c n)"), bank, ACT.Copy))
                        skip(2)
                    for n in range(NCH):
                        bank = sbank()
                        sdrain(nc.scalar.activation(Wc[:, :, :].rearrange("p d n -> p (d n)"), bank[:, 0:P], ACT.Copy))
                        skip(3 if n < NCH - 1 else 2)
                    root(stat[:, 8:12])
                    bank = sbank()
                    turned_pairs(tmp[:, :].rearrange("p (c k n) -> p c k n", k=2, n=CHUNK), bank)
                    skip(PER_PAIR - (scan.tally.count - start))
                    act.wait_ge(s_used, slab.next(8))
                    act.wait_ge(s_for_act, for_act.next())
                    nc.scalar.activation(gates[:, i], gate_acc, ACT.Sigmoid).then_inc(s_gate, 1)
                slab.next(4 * 8)

                def product(n, nslab, ubs):
                    for j in range(n):
                        act.wait_ge(s_used, slab.next(nslab))
                        nc.scalar.activation(tok_buf[:, :, j * UNIT:(j + 1) * UNIT], acc[:, ubs[j]], ACT.Copy).then_inc(s_emptied, 1)
                product(4, 8, (0, 1, 0, 1))
                act.wait_ge(s_emptied, emptied_now(l, "wo"))
                rms(tok_buf)
                act.wait_ge(s_for_act, for_act.next())
                rms(x)
                unit_rows(0, 8)
                exps(X_HEAD ** -0.5)
                product(4, 2, (1, 0, 1, 0))
                act.wait_ge(s_emptied, emptied_now(l, "xo"))
                rms(tok_buf)
                act.wait_ge(s_for_act, for_act.next())
                rms(x)
                for tiles in FF_PARTS:
                    with repeat(act, tiles // 4, {slab: 16, rows_free: 2, from_act: 2}):
                        for ub in (1, 0):
                            act.wait_ge(s_rows_free, rows_free.at(1))
                            rows_free.next()
                            act.wait_ge(s_used, slab.next(8))
                            nc.scalar.activation(rows[:, ub, :, 0:256], acc[:, ub, :, 0:256], ACT.Silu).then_inc(s_from_act, 1)
                            from_act.next()
                    slab.next(2 * tiles)
                act.wait_ge(s_for_act, for_act.next())
                rms(tok_buf)

        @block.vector
        def _(dve):
            V = nc.vector
            slab = Tally(s_used)
            full = Tally(s_full)
            drained = Tally(s_drained)
            step = Tally(s_dve)
            for_pe = Tally(s_for_pe)
            for_act = Tally(s_for_act)
            from_act = Tally(s_from_act)
            gain = Tally(s_gain, 16)
            scan = Banks(Tally(s_sfull), s_sdrained)
            branch = Tally(s_branch)
            dve.sem_inc(s_branch, 2)
            branch.next(2)
            dve_bank = [0]
            for b in range(SCAN_BANKS):
                dve.sem_inc(s_sdrained[b], 2)

            def own(ins):
                ins.then_inc(s_dve, 1)
                dve.wait_ge(s_dve, step.next())

            def to_pe(ins):
                ins.then_inc(s_for_pe, 1)
                for_pe.next()

            def to_act(ins):
                ins.then_inc(s_for_act, 1)
                for_act.next()

            def act_result():
                dve.wait_ge(s_from_act, from_act.next())

            def bank():
                b = full.count % 4
                dve.wait_ge(s_full, full.next())
                return work[:, b, :]

            def drain(ins, n=1, wait=False, aligned=False):
                if aligned:
                    pad = -full.count % 4
                    full.next(pad)
                    n += pad
                ins.then_inc(s_drained, n)
                drained.next(n)
                if wait:
                    dve.wait_ge(s_drained, drained.at())

            def sbank():
                b, _ = scan.now()
                dve_bank[0] = b
                dve.wait_ge(s_sfull, scan.tally.next())
                return psum[:, b, :]

            def sdrain(ins, n=2, wait=False):
                b = dve_bank[0]
                ins.then_inc(s_sdrained[b], n)
                if wait:
                    own(V.tensor_copy(stat[:, 48:49], stat[:, 0:1]))

            def skipped():
                b, free = scan.now()
                scan.tally.next()
                return b, free + 2

            def shave(q):
                dve.wait_ge(s_sdrained[q[0]], q[1])

            def bc(ap, n):
                return ap.unsqueeze(2).to_broadcast([ap.shape[0], ap.shape[1], n])

            def rms_scale():
                act_result()
                act_result()
                to_act(V.tensor_scalar(stat[:, 2:4], stat[:, 0:2], 1.0 / D_MODEL, EPS, ALU.mult, ALU.add))
                act_result()
                own(V.reciprocal(stat[:, 4:6], stat[:, 2:4]))

            def norm_rows(src):
                rms_scale()
                for tok in range(TOK):
                    to_pe(V.tensor_scalar(tok_buf[:, tok, :], src[:, tok, :], stat[:, 4 + tok:5 + tok], None, ALU.mult))

            def turned_rows(gains=None):
                for tok in range(TOK):
                    for g in range(KD // 4):
                        src = bank().rearrange("p (j n) -> p j n", j=4)
                        dst = opT[:, 4 * g:4 * g + 4, tok * P:(tok + 1) * P]
                        if gains is None:
                            drain(V.tensor_copy(dst, src))
                        else:
                            drain(V.tensor_tensor(dst, src, bc(gains[:, 4 * g:4 * g + 4], P), ALU.mult))

            def post_norm(name):
                rms_scale()
                if name == "n_mix_post":
                    dve.wait_ge(s_x_back, 16 * (l + 1))
                dve.wait_ge(s_gain, gain.next())
                for tok in range(TOK):
                    own(V.scalar_tensor_tensor(tok_buf[:, tok, :], tok_buf[:, tok, :], stat[:, 4 + tok:5 + tok], gain_row, ALU.mult, ALU.mult))
                    own(V.tensor_tensor(x[:, tok, :], x[:, tok, :], tok_buf[:, tok, :], ALU.add))

            def nudge_act():
                dve.sem_inc(s_for_act, 1)
                for_act.next()

            def softmax(scale):
                for _ in range(4):
                    bank()
                scores = work[:, :, :].rearrange("p b (q s) -> p (b q) s", q=2)
                own(V.reduce_max(stat[:, 32:40], scores, AX_X))
                to_act(V.tensor_scalar(stat[:, 16:24], stat[:, 32:40], -scale, None, ALU.mult))
                act_result()
                own(V.reciprocal(stat[:, 40:48], stat[:, 24:32]))
                drain(V.tensor_tensor(prob, prob, bc(stat[:, 40:48], SEQ), ALU.mult), 4)
                for _ in range(4):
                    bank()
                drain(V.tensor_copy(probT, work[:, :, :]), 4)

            own(V.memset(prow, 0.0))
            dve.sem_inc(s_rows_zero, 1)
            own(V.memset(lora_in[:, :, :, :], 0.0))
            dve.wait_ge(s_const, 16)
            for l in range(DEPTH):
                for g in range(2):
                    n, o = GROUP_ROWS[g], GROUP_ROWS[0] * g
                    drain(V.tensor_copy(cols[:, l, o:o + n], bank()[:, 0:n]), wait=True)
                own(V.tensor_tensor(cols_mix[:, l, :], colv(l, "rw_mu_prev", 28), colv(l, "rw_mu_next", 28), ALU.add))
                own(V.tensor_scalar(cols_mix[:, l, :], cols_mix[:, l, :], -1.0, 1.0, ALU.mult, ALU.add))
                own(V.tensor_scalar(cols_ka[:, l, :], colv(l, "rw_k_a", PAIRS), -1.0, 1.0, ALU.mult, ALU.add))
            carry = cst("carry")
            for l in range(DEPTH):
                dve.sem_inc(s_mem_free, 1)
                dve.wait_ge(s_mem, 16 * (l + 1))
                if l == 0:
                    dve.wait_ge(s_x, 16)
                nudge_act()
                norm_rows(tok_buf)
                turned_rows(colv(l, "n_mem", KD))
                for b in range(2):
                    src = bank().rearrange("p (j n) -> p j n", j=2)
                    if b:
                        V.tensor_copy(memk[:, 2 * b:2 * b + 1, :], src[:, 0:1, :]).then_inc(s_rows_free, 1)
                        drain(V.tensor_copy(memk[:, 2 * b + 1:2 * b + 2, :], src[:, 1:2, :]))
                    else:
                        drain(V.tensor_copy(memk[:, 0:2, :], src))
                dve.wait_ge(s_emptied, emptied_now(l, "memv"))
                to_act(V.tensor_copy(memv[:, :, :], rows[:, 1, :, :]))

                norm_rows(x)
                dve.wait_ge(s_for_pe, for_pe.at())
                dve.sem_inc(s_x_idle, 1)
                turned_rows(colv(l, "n_mix_pre", KD))

                def shifted(src, t, w, mix, prev, nxt):
                    dst = t
                    own(V.tensor_scalar(dst, src, mix, None, ALU.mult))
                    own(V.scalar_tensor_tensor(dst[:, 1:SEQ], src[:, 0:SEQ - 1], prev, dst[:, 1:SEQ], ALU.mult, ALU.add))
                    return V.scalar_tensor_tensor(dst[:, 0:SEQ - 1], src[:, 1:SEQ], nxt, dst[:, 0:SEQ - 1], ALU.mult, ALU.add)

                with repeat(dve, 3, {full: 4, drained: 4, step: 16}) as i:
                    for u in range(2):
                        for b in range(2):
                            src = bank()
                            for j in range(2):
                                k = u * 4 + b * 2 + j
                                zt = streams[:, 0:5:2, k * SEQ:(k + 1) * SEQ]
                                pv = colv(l, "rw_mu_prev", 24).rearrange("p (i k) -> p k i", k=8)[:, k]
                                nx = colv(l, "rw_mu_next", 24).rearrange("p (i k) -> p k i", k=8)[:, k]
                                mx = cols_mix[:, l, 0:24].rearrange("p (i k) -> p k i", k=8)[:, k]
                                ins = shifted(src[:, j * SEQ:(j + 1) * SEQ], zt[:, i, :], P, mx[:, bass.ts(i, 1)], pv[:, bass.ts(i, 1)], nx[:, bass.ts(i, 1)])
                                if j:
                                    drain(ins)
                                elif b:
                                    ins.then_inc(s_rows_free, 1)
                for b in range(2):
                    src = bank()
                    for j in range(2):
                        k = 24 + 2 * b + j
                        w = LORA_W[2 * b + j]
                        ins = shifted(src[0:w, j * SEQ:(j + 1) * SEQ], low_in[0:w, k - 24, :], w, cols_mix[0:w, l, k:k + 1],
                                      col(l, "rw_mu_prev", k)[0:w], col(l, "rw_mu_next", k)[0:w])
                        if j:
                            drain(ins, wait=True)
                        elif b:
                            ins.then_inc(s_rows_free, 1)
                for u in range(3):
                    for b in range(2 if u < 2 else 1):
                        src = bank()
                        dst = qk[:, 2 * u + b]
                        if b or u == 2:
                            V.tensor_copy(dst[:, 0:1, :], src[:, 0:SEQ].rearrange("p (j n) -> p j n", j=1)).then_inc(s_rows_free, 1)
                            drain(V.tensor_copy(dst[:, 1:2, :], src[:, SEQ:2 * SEQ].rearrange("p (j n) -> p j n", j=1)), wait=True, aligned=u == 2)
                        else:
                            drain(V.tensor_copy(dst, src.rearrange("p (j n) -> p j n", j=2)), wait=True)
                own(V.tensor_copy(v_at, rows[:, 1, :, AT_KV:2 * AT_KV]))
                with repeat(dve, 5, {full: 4, drained: 4, for_pe: 2, for_act: 1, from_act: 1, step: 3}) as i:
                    qi = qk[:, i].rearrange("p a b -> p (a b)")
                    flat = lambda t: t.rearrange("p a b -> p (a b)")
                    to_pe(V.tensor_tensor(flat(sq_tmp), qi, qi, ALU.mult))
                    src = bank()
                    ins = V.tensor_scalar(flat(rt_tmp), src, 1.0 / HEAD, EPS, ALU.mult, ALU.add)
                    to_act(ins)
                    act_result()
                    own(V.reciprocal(flat(rt_tmp), flat(rt_tmp)))
                    dve.sem_inc(s_drained, 1)
                    drained.next()
                    gcol = colv(l, "qk_norm", 5)[:, bass.ts(i, 1)]
                    to_pe(V.scalar_tensor_tensor(flat(qn_tmp), qi, gcol, flat(rt_tmp), ALU.mult, ALU.mult))
                    dve.wait_ge(s_for_pe, for_pe.at())
                    b2 = lambda t: t.unsqueeze(1).to_broadcast([P, 2, SEQ])
                    own(V.tensor_tensor(qk[:, i], qn_tmp, b2(cst("cos")), ALU.mult))
                    src = bank().rearrange("p (j n) -> p j n", j=2)
                    drain(V.tensor_tensor(sq_tmp, src, b2(cst("sin")), ALU.mult), wait=True, aligned=True)
                    own(V.tensor_tensor(qk[:, i], qk[:, i], sq_tmp, ALU.add))
                for g in range(AT_KV_HEADS):
                    for half in range(2):
                        s0 = (g % 2) * HEAD
                        ins = V.tensor_copy(k_both[half * HEAD:(half + 1) * HEAD, g, :], qk[s0:s0 + HEAD, 4, g // 2, :])
                own(ins)
                with repeat(dve, AT_KV_HEADS, {full: 12, drained: 12, for_pe: 1, for_act: 1, from_act: 1, step: 2}) as g:
                    V.tensor_copy(q_now, qk[:, g])
                    V.tensor_copy(k_now, k_both[:, g, :])
                    to_pe(V.tensor_copy(v_now, v_at.rearrange("p t (g d) -> p g t d", g=AT_KV_HEADS)[:, g]))
                    softmax(HEAD ** -0.5)
                    drain(V.tensor_copy(y_at[:, :, :].rearrange("p (g t) n -> p g (t n)", t=2)[:, g], bank()), aligned=True)
                if l:
                    dve.sem_inc(s_for_pe, 1)
                    for_pe.next()
                    drain(V.tensor_copy(v_low, bank()[0:V_LORA, 0:SEQ]), aligned=True)
                nudge_act()
                for d in range(2):
                    r = slice(d * 64, (d + 1) * 64)
                    own(V.tensor_copy(lora_in[r, 1, d, :], low_in[r, 1, :]))
                own(V.memset(view(0, 4096), 0.0))
                act_result()
                dve.sem_inc(s_for_pe, 1)
                for_pe.next()
                dve.sem_inc(s_lw_free, 1)
                with repeat(dve, PAIRS, {scan.tally: PER_PAIR, for_pe: 4, for_act: 5, from_act: 3, step: N_STEP[l]}) as i:
                    start = scan.tally.count
                    rT, kT, vT = r_all[:, i, :], k_all[:, i, :], v_all[:, i, :]

                    def pcol(name, d=None):
                        v = colv(l, name, PAIRS) if d is None else cols[:, l, PCOL[name] + d * PAIRS:PCOL[name] + (d + 1) * PAIRS]
                        return v[:, bass.ts(i, 1)]
                    flat = lambda t: t.rearrange("p a b -> p (a b)")
                    two = lambda t: t.unsqueeze(1).to_broadcast([P, 2, SEQ])
                    ch = lambda t: t.rearrange("p (c n) -> p c n", c=NCH)
                    for kind, name in enumerate(("rw_w0", "rw_a0")):
                        src = sbank()
                        for d in range(2):
                            ins = V.tensor_scalar(sig[:, 2 * kind + d, :], src[:, d * SEQ:(d + 1) * SEQ], pcol(name, d), None, ALU.add)
                        if l or kind == 0:
                            sdrain(ins)
                        else:
                            sdrain(ins, wait=True)
                    if l:
                        sdrain(V.tensor_scalar(tmp2[:, :], sbank()[:, 0:SEQ], pcol("rw_v0"), None, ALU.add), wait=True)
                    nudge_act()
                    g_ready = skipped()
                    own(V.tensor_scalar(p_exc[:, 0, :], kT, pcol("rw_k_k"), None, ALU.mult))
                    V.tensor_tensor(tmp[:, :], p_exc[:, 0, :], p_exc[:, 0, :], ALU.mult)
                    act_result()
                    own(V.tensor_tensor_scan(inc[:, 0, :], carry, sig[:, 0, :], 0.0, ALU.mult, ALU.add))
                    own(V.tensor_tensor_scan(p_inc[:, 0, :], carry, sig[:, 1, :], 0.0, ALU.mult, ALU.add))
                    total = ch(p_inc[:, 0, :])[:, :, CHUNK - 1:CHUNK].to_broadcast([P, NCH, CHUNK])
                    own(V.tensor_tensor(ch(exc[:, 1, :]), total, ch(p_inc[:, 0, :]), ALU.subtract))
                    V.tensor_tensor(exc[:, 0, :], inc[:, 0, :], sig[:, 0, :], ALU.subtract)
                    own(V.tensor_tensor(inc[:, 1, :], exc[:, 1, :], sig[:, 1, :], ALU.add))
                    if l:
                        own(V.tensor_tensor(v_cur[:, :], v_first[:, :, :][:, i, :], vT, ALU.subtract))
                        own(V.tensor_tensor(v_cur[:, :], v_cur[:, :], tmp2[:, :], ALU.mult))
                        own(V.tensor_tensor(v_cur[:, :], v_cur[:, :], vT, ALU.add))
                    else:
                        V.tensor_copy(v_cur[:, :], vT)
                        own(V.tensor_copy(v_first[:, :, :][:, i, :], vT))
                    own(V.tensor_scalar(flat(kd), flat(sig[:, 2:4, :]), pcol("rw_k_a"), cols_ka[:, l, :][:, bass.ts(i, 1)], ALU.mult, ALU.add))
                    own(V.tensor_tensor(kd, kd, two(kT), ALU.mult))
                    own(V.tensor_tensor(tmp2[:, :], kd[:, 0, :], kd[:, 1, :], ALU.add))
                    to_pe(V.scalar_tensor_tensor(tmp2[:, :], rT, pcol("rw_r_k"), tmp2[:, :], ALU.mult, ALU.mult))
                    norms = skipped()
                    shave(norms)
                    dve.sem_inc(s_lw_free, 1)
                    own(V.tensor_scalar(tmp[:, :], tmp[:, :], 1e-12, None, ALU.max))
                    own(V.reciprocal(tmp[:, :], tmp[:, :]))
                    own(V.scalar_tensor_tensor(tmp[:, :], p_exc[:, 0, :], -1.0, tmp[:, :], ALU.mult, ALU.mult))
                    nudge_act()
                    own(V.scalar_tensor_tensor(sig[:, 2:4, :], two(tmp[:, :]), -1.0, sig[:, 2:4, :], ALU.mult, ALU.mult))
                    sdrain(V.tensor_tensor(kT, sbank()[:, 0:SEQ], v_cur[:, :], ALU.mult))
                    v_ready = skipped()
                    act_result()
                    V.tensor_tensor(sig[:, 2:4, :], sig[:, 2:4, :], p_inv, ALU.mult)
                    V.tensor_tensor(kd, kd, p_inv, ALU.mult)
                    V.tensor_tensor(p_exc, two(tmp[:, :]), p_exc, ALU.mult)
                    to_act(V.tensor_tensor(inc, two(rT), p_inc, ALU.mult))

                    pair2 = lambda t: t.unsqueeze(2).to_broadcast([P, t.shape[1], 2, HEAD])
                    halves = lambda t: t.rearrange("p c (h n) -> p c h n", h=2)
                    some = lambda m, k: m.rearrange("p (h n) -> p h n", h=2).unsqueeze(1).to_broadcast([P, k, 2, HEAD])
                    row4 = lambda t, k: t.unsqueeze(1).to_broadcast([P, k, HEAD])
                    before = cst("before").rearrange("p (d n) -> p d n", d=2)

                    def expand(dst, src, m=head_ones, k=NCH):
                        return V.tensor_tensor(halves(dst), pair2(src), some(m, k), ALU.mult)
                    for d in range(2):
                        for c2 in range(0, NCH, 2):
                            src = sbank().rearrange("p (j k n) -> p j k n", j=2, k=4)
                            for kind, g, m in ((0, 0, mask[:, d, P:2 * P]), (2, 1, mask[:, d, P:2 * P]), (3, 2, mask[:, d, 0:P])):
                                expand(GT[:, d, c2:c2 + 2, g, :], src[:, :, kind, :], m, 2)
                            sdrain(V.tensor_tensor(AT_c[:, d, c2:c2 + 2, :], src[:, :, 1, :], row4(before[:, d], 2), ALU.mult))
                    src = sbank().rearrange("p (d c n) -> p d c n", d=2, c=NCH)
                    for d in range(2):
                        ins = V.tensor_tensor(A_c[:, d], src[:, d], row4(before[:, 1 - d], NCH), ALU.mult)
                    sdrain(ins, wait=True)
                    dve.sem_inc(s_for_pool, 1)
                    skipped()
                    skipped()
                    skipped()
                    skipped()
                    eight = lambda t: t.rearrange("p d c n -> p (d c) n")
                    in16c = row4(cst("in16_head"), 2 * NCH)
                    V.tensor_tensor(eight(X_c), eight(A_c), in16c, ALU.mult)
                    own(V.tensor_tensor(eight(XT_c), eight(AT_c), in16c, ALU.mult))
                    for d in range(2):
                        expand(XA[:, d], X_c[:, d])
                        if d == 0:
                            to_pe(expand(XTA[:, d], XT_c[:, d]))
                        else:
                            expand(XTA[:, d], XT_c[:, d])
                            to_pe(V.tensor_tensor(eight(E_c), eight(XT_c), row4(cst("ident_head"), 2 * NCH), ALU.add))
                    side = lambda t, k: t[:, k * 256:(k + 1) * 256].rearrange("p (c n) -> p c n", c=NCH)
                    for d in range(2):
                        src = sbank()
                        expand(XB[:, d], side(src, 0))
                        sdrain(expand(XTB[:, d], side(src, 1)), 1)
                    for d in range(2):
                        src = sbank()
                        V.tensor_tensor(E_c[:, d], E_c[:, d], side(src, 0), ALU.add)
                        sdrain(expand(XA[:, d], side(src, 1)), 1)
                        sdrain(expand(XTA[:, d], side(sbank(), 0)))
                    for d in range(2):
                        src = sbank()
                        V.tensor_tensor(E_c[:, d], E_c[:, d], side(src, 0), ALU.add)
                        sdrain(expand(XB[:, d], side(src, 1)))
                    for d in range(2):
                        own(V.tensor_tensor(E_c[:, d], E_c[:, d], side(sbank(), 0), ALU.add))
                        sdrain(expand(EE[:, d], E_c[:, d]))
                    for n in (32, 64):
                        for d in range(2):
                            sdrain(V.tensor_copy(P_c[:, d], side(sbank(), 0)))
                            skipped()
                        for d in range(2):
                            own(V.tensor_tensor(E_c[:, d], E_c[:, d], side(sbank(), 0), ALU.add))
                            sdrain(expand(EE[:, d], E_c[:, d]))
                    for n in range(NCH):
                        at = (n, NCH - 1 - n)
                        skipped()
                        sdrain(V.tensor_copy(flat(Uc[:, :, :]), sbank()[:, 0:P]))
                        if n < NCH - 1:
                            src_s, b_s = sbank(), dve_bank[0]
                        src = sbank()
                        if n < NCH - 1:
                            if n:
                                own(V.tensor_tensor(flat(St[:, :, :]), flat(St[:, :, :]), src_s[:, 0:P], ALU.add))
                            for d, c in enumerate(at):
                                end = c * CHUNK + (CHUNK - 1 if d == 0 else 0)
                                s_d = St[:, d, :] if n else src_s[:, d * HEAD:(d + 1) * HEAD]
                                ins = V.tensor_scalar(St[:, d, :], s_d, p_inc[:, d, end:end + 1], None, ALU.mult)
                            ins.then_inc(s_sdrained[b_s], 2)
                        for d, c in enumerate(at):
                            y = src[:, d * HEAD:(d + 1) * HEAD]
                            if n < NCH // 2:
                                ins = V.tensor_copy(Yc[:, c, :], y)
                            else:
                                ins = V.tensor_tensor(Yc[:, c, :], Yc[:, c, :], y, ALU.add)
                        sdrain(ins, wait=n > 0)
                    own(V.reduce_sum(stat[:, 12:16], Yc[:, :, :], AX_X))
                    own(V.tensor_scalar(stat[:, 12:16], stat[:, 12:16], 1.0 / HEAD, None, ALU.mult))
                    own(V.tensor_tensor(Yc[:, :, :], Yc[:, :, :], bc(stat[:, 12:16], HEAD), ALU.subtract))
                    own(V.tensor_tensor(ch(p_inv[:, 0, :]), Yc[:, :, :], Yc[:, :, :], ALU.mult))
                    own(V.reduce_sum(stat[:, 12:16], ch(p_inv[:, 0, :]), AX_X))
                    to_act(V.tensor_scalar(stat[:, 8:12], stat[:, 12:16], 1.0 / HEAD, GN_EPS, ALU.mult, ALU.add))
                    act_result()
                    own(V.reciprocal(stat[:, 12:16], stat[:, 8:12]))
                    to_pe(V.tensor_tensor(Yc[:, :, :], Yc[:, :, :], bc(stat[:, 12:16], HEAD), ALU.mult))
                    shave(skipped())
                    shave(g_ready)
                    own(V.tensor_scalar(tmp[:, :], tmp[:, :], pcol("rw_ln_w"), pcol("rw_ln_b"), ALU.mult, ALU.add))
                    own(V.tensor_tensor(tmp[:, :], tmp[:, :], kT, ALU.add))
                    own(V.tensor_tensor(y_rw[:, i, :], tmp[:, :], g_cur[:, :], ALU.mult))
                    nudge_act()
                    while scan.tally.count - start < PER_PAIR:
                        b, read = scan.now()
                        dve.wait_ge(s_sdrained[b], read)
                        dve.sem_inc(s_sdrained[b], 2)
                        scan.tally.next()
                dve.sem_inc(s_for_pe, 1)
                for_pe.next()
                dve.sem_inc(s_gain_free, 1)
                slab.count = slab_now(l, "gates")
                with repeat(dve, 4, {slab: 8, branch: 2, step: 1}) as i:
                    tb_i = tok_buf[:, :, :].rearrange("p t (i n) -> p i t n", i=4)[:, i]
                    gate_a, gate_b = gates[:, 0:4][:, i], gates[:, 4:8][:, i]
                    dve.wait_ge(s_used, slab.next(4))
                    V.tensor_tensor(tb_i, acc[:, 0], gate_a, ALU.mult).then_inc(s_branch, 1)
                    branch.next()
                    dve.wait_ge(s_used, slab.next(4))
                    V.tensor_tensor(gate_b, acc[:, 1], gate_b, ALU.mult).then_inc(s_branch, 1)
                    dve.wait_ge(s_branch, branch.next())
                    own(V.tensor_tensor(tb_i, tb_i, gate_b, ALU.add))
                dve.sem_inc(s_x_idle, 1)
                for tok in range(TOK):
                    dve.sem_inc(s_for_pe, 1)
                    for_pe.next()
                turned_rows()
                post_norm("n_mix_post")
                nudge_act()
                norm_rows(x)
                turned_rows(colv(l, "n_x_pre", KD))
                for b in range(2):
                    src = bank().rearrange("p (j n) -> p j n", j=2)
                    if b:
                        V.tensor_copy(x_q[:, 2:3, :], src[:, 0:1, :]).then_inc(s_rows_free, 1)
                        drain(V.tensor_copy(x_q[:, 3:4, :], src[:, 1:2, :]), aligned=True)
                    else:
                        drain(V.tensor_copy(x_q[:, 0:2, :], src))
                dve.sem_inc(s_gain_free, 1)
                softmax(X_HEAD ** -0.5)
                for b2 in range(2):
                    drain(V.tensor_copy(x_y[:, 2 * b2:2 * b2 + 2, :], bank().rearrange("p (j n) -> p j n", j=2)), aligned=b2 == 1)
                post_norm("n_x_post")
                nudge_act()
                norm_rows(x)
                turned_rows(colv(l, "n_ffn_pre", KD))
                dve.sem_inc(s_gain_free, 1)
                slab.count = slab_now(l, "ffn")
                for part, tiles in enumerate(FF_PARTS):
                    with repeat(dve, tiles // 4, {slab: 16, full: 4, drained: 4, from_act: 2, step: 0}) as i:
                        for j, ub in enumerate((1, 0)):
                            act_result()
                            slab.next(8)
                            V.tensor_tensor(rows[:, ub, :, 0:256], acc[:, ub, :, 256:512], rows[:, ub, :, 0:256], ALU.mult).then_inc(s_emptied, 1)
                            src = bank().rearrange("p (t n) -> p t n", t=2)
                            dst = hidT.rearrange("p (i j t) n -> p j i t n", j=2, t=2)[:, j]
                            V.tensor_copy(dst[:, i, 0:1, :], src[:, 0:1, :]).then_inc(s_rows_free, 1)
                            drain(V.tensor_copy(dst[:, i, 1:2, :], src[:, 1:2, :]), aligned=j == 1)
                    with repeat(dve, 2, {slab: tiles, step: 0}) as i:
                        for j, ub in enumerate((1, 0)):
                            dve.wait_ge(s_used, slab.next(tiles // 2))
                            c = tok_buf[:, :, :].rearrange("p t (i j n) -> p j i t n", i=2, j=2)[:, j][:, i]
                            if part == 0:
                                V.tensor_copy(c, acc[:, ub]).then_inc(s_emptied, 1)
                            else:
                                V.tensor_tensor(c, c, acc[:, ub], ALU.add).then_inc(s_emptied, 1)
                dve.wait_ge(s_emptied, emptied_now(l, "end"))
                nudge_act()
                post_norm("n_ffn_post")
            dve.sem_inc(s_out, 1)


N_STEP = {0: 36, 1: 38}


def slab_now(l, where):
    before = {"gates": 16 + 48 + 8 + 24 + 64, "ffn": 16 + 48 + 8 + 24 + 96 + 32 + 8 + 8}[where]
    return l * SLABS + before


SLABS = 16 + 48 + 8 + 24 + 96 + 32 + 8 + 8 + 8 * 22 + 2 * sum(FF_PARTS)
UNITS = 2 + 10 + 4 + 1 + 4 + 22 + 4 * len(FF_PARTS)


def emptied_now(l, where):
    n = {"memv": 2, "wo": 16, "xo": 21, "end": UNITS}[where]
    return l * UNITS + n


_INS = ["x", "mem", "n_mix_pre", "n_mix_post", "n_x_pre", "n_x_post", "n_ffn_pre", "n_ffn_post", "n_mem", "w_in",
        "rw_mu_prev", "rw_mu_next", "rw_w0", "rw_w_up", "rw_a0", "rw_a_up", "rw_g_up", "rw_v0", "rw_v_down", "rw_v_up",
        "rw_k_k", "rw_k_a", "rw_r_k", "rw_ln_w", "rw_ln_b", "w_rw_out", "at_q_norm", "at_k_norm", "w_at_out", "w_o",
        "x_wq", "x_wkv", "x_wo", "ffn_wg", "ffn_wu", "ffn_wd"]


def kernel(**inputs):
    import numpy as _np
    import concourse.bacc as _bacc
    from concourse import mybir as _mybir
    from concourse.bass_utils import run_bass_kernel_spmd as _run

    nc = _bacc.Bacc("TRN2", target_bir_lowering=False, num_devices=1)
    given = {name: _np.ascontiguousarray(inputs[name]) for name in _INS}
    given["shape_constants"] = shape_constants()
    arrays, aps = {}, {}
    for name, v in given.items():
        arrays[f"in_{name}_dram"] = v
        aps[name] = nc.dram_tensor(f"in_{name}_dram", v.shape, _mybir.dt.from_np(v.dtype), kind="ExternalInput").ap()
    out = nc.dram_tensor("out_0_dram", (1, SEQ, D_MODEL), _mybir.dt.float32, kind="ExternalOutput").ap()
    encoder_kernel(nc, aps, out)
    r = _run(nc, [arrays], core_ids=[0])
    return r.results[0]["out_0_dram"]
```

```python
from contextlib import ExitStack, contextmanager

import numpy as np

import concourse.bass as bass
from concourse import mybir

F32 = mybir.dt.float32
F32R = mybir.dt.float32r
ALU = mybir.AluOpType
ACT = mybir.ActivationFunctionType
AX_X = mybir.AxisListType.X

P = 128
D_MODEL, SEQ, DEPTH, N_MEM = 2048, 256, 2, 256
GRID_W = 64
EPS = 1e-6
RW_HEADS, HEAD = 16, 64
RW_WIDTH = RW_HEADS * HEAD
W_LORA = A_LORA = 64
V_LORA, G_LORA = 32, 160
GN_EPS = 64e-5
AT_HEADS, AT_KV_HEADS = 16, 4
AT_Q, AT_KV = AT_HEADS * HEAD, AT_KV_HEADS * HEAD
ROPE_THETA = 10000.0
X_HEADS, X_HEAD = 4, 128
X_WIDTH = X_HEADS * X_HEAD
D_FF = -(-8 * D_MODEL // (3 * 256)) * 256
LORA_COLS = 2 * W_LORA + 2 * A_LORA + G_LORA
RW_COLS = 3 * RW_WIDTH + LORA_COLS
AT_COLS = AT_Q + 2 * AT_KV
DECAY = float(np.exp(-0.5))

TOK = SEQ // P
KD = D_MODEL // P
UNIT = 512
RING = 8
AHEAD = 6
PAIRS = RW_HEADS // 2
SCAN_BANKS = 6
PER_PAIR = 54
CHUNK = 64
NCH = SEQ // CHUNK
FF_PARTS = (16, 16, 12)
LORA_W = (P, P, P, LORA_COLS - 3 * P)

PARAM_ROWS = [
    [("n_mix_pre", KD), ("n_x_pre", KD), ("n_ffn_pre", KD), ("n_mem", KD), ("rw_mu_prev", 28), ("rw_mu_next", 28)],
    [("rw_w0", 2 * PAIRS), ("rw_a0", 2 * PAIRS), ("rw_k_k", PAIRS), ("rw_k_a", PAIRS), ("rw_r_k", PAIRS),
     ("rw_ln_w", PAIRS), ("rw_ln_b", PAIRS), ("rw_v0", PAIRS), ("qk_norm", 5)],
]
PCOL = {}
_n = 0
for _g in PARAM_ROWS:
    for _name, _rows in _g:
        PCOL[_name] = _n
        _n += _rows
GROUP_ROWS = [sum(r for _, r in g) for g in PARAM_ROWS]
N_COLS = sum(GROUP_ROWS)

CONST = {}
_n = 0
for _name, _w in (("ident", P), ("head_ones", P), ("rot", P), ("mask", 2 * 2 * P), ("in16", P), ("in32", P),
                  ("in64", P), ("cos", SEQ), ("sin", SEQ), ("carry", SEQ), ("before", 2 * HEAD),
                  ("in16_head", HEAD), ("ident_head", HEAD)):
    CONST[_name] = (_n, _w)
    _n += _w
N_CONST = _n


def shape_constants():
    out = np.zeros((P, N_CONST), np.float32)

    def put(name, a):
        o, w = CONST[name]
        out[:, o:o + w] = a.reshape(P, w)

    r = np.arange(P)
    put("ident", np.eye(P))
    head = r[:, None] // HEAD == r[None, :] // HEAD
    put("head_ones", head)
    rot = np.zeros((P, P))
    for m in range(P):
        if m % 32 < 16:
            rot[m + 16, m] = -1.0
        else:
            rot[m - 16, m] = 1.0
    put("rot", rot)
    s, t = r[:, None] % HEAD, r[None, :] % HEAD
    mask = np.stack([head & (s < t), head & (s <= t), head & (s > t), head & (s >= t)], axis=1)
    put("mask", mask)
    put("in16", r[:, None] // 16 == r[None, :] // 16)
    for n in (32, 64):
        put(f"in{n}", (r[:, None] // n == r[None, :] // n) & (r[:, None] // (n // 2) != r[None, :] // (n // 2)))
    row, c64 = r[:, None] % HEAD, np.arange(HEAD)[None, :]
    put("before", np.stack([row < c64, row > c64], axis=1))
    put("in16_head", row // 16 == c64 // 16)
    put("ident_head", row == c64)
    n_freq = HEAD // 4
    inv = np.float32(ROPE_THETA) ** (-np.arange(n_freq, dtype=np.float32) / np.float32(n_freq))
    tok = np.arange(SEQ)
    pos = np.stack([tok // GRID_W, tok % GRID_W]).astype(np.float32)
    ang = pos[(r % HEAD) // 32] * inv[r % 16][:, None]
    put("cos", np.cos(ang))
    put("sin", np.sin(ang))
    put("carry", np.broadcast_to((tok % CHUNK != 0).astype(np.float32), (P, SEQ)))
    return out


class Tally:

    def __init__(self, sem, scale=1):
        self.sem, self.count, self.loop, self.scale = sem, 0, None, scale

    def at(self, back=0):
        n = (self.count - back) * self.scale
        return n if self.loop is None else self.loop[0] * (self.loop[1] * self.scale) + n

    def next(self, n=1):
        self.count += n
        return self.at()


class Banks:

    def __init__(self, tally, drained):
        self.tally, self.drained = tally, drained

    def now(self):
        t = self.tally
        uses = t.count // SCAN_BANKS + 1
        if t.loop is not None:
            assert t.loop[1] % SCAN_BANKS == 0
            return t.count % SCAN_BANKS, t.loop[0] * (2 * (t.loop[1] // SCAN_BANKS)) + 2 * uses
        return t.count % SCAN_BANKS, 2 * uses


@contextmanager
def repeat(eng, times, per):
    start = {t: t.count for t in per}
    with eng.Fori(0, times) as i:
        for t, n in per.items():
            t.loop = (i, n)
        yield i
        for t, n in per.items():
            assert t.count - start[t] == n, (t.sem, t.count - start[t], n)
    for t, n in per.items():
        t.loop = None
        t.count = start[t] + times * n


def encoder_kernel(nc, a, out):
    with ExitStack() as ctx:
        def sb(name, shape):
            return ctx.enter_context(nc.sbuf_tensor("sb_" + name, shape, F32))

        def sem(name):
            return ctx.enter_context(nc.semaphore(name))

        with ExitStack() as places:
            ring_parts, opT_parts, arena_parts, streams_parts, y_at_parts = (
                places.enter_context(nc.sbuf_tensor(f"sb_{name}_parts", shape, F32R))
                for name, shape in (("ring", [P, RING, UNIT]), ("opT", [P, KD, SEQ]), ("arena", [P, 14336]),
                                    ("streams", [P, 5, D_MODEL]), ("y_at", [P, PAIRS, SEQ])))
        ring = sb("ring", [P, RING, UNIT])
        opT = sb("opT", [P, KD, SEQ])
        arena = sb("arena", [P, 14336])
        streams = sb("streams", [P, 5, D_MODEL])
        y_at = sb("y_at", [P, PAIRS, SEQ])
        x = streams[:, 1:5:2, :]
        tok_buf = sb("tok_buf", [P, TOK, D_MODEL])
        rows = sb("rows", [P, 2, TOK, UNIT])
        r_all, k_all, v_all = (streams[:, b, :].rearrange("p (i n) -> p i n", i=PAIRS) for b in (0, 2, 4))
        y_rw = r_all
        low_in = sb("low_in", [P, 4, SEQ])
        v_first = sb("v_first", [P, PAIRS, SEQ])
        memk = sb("memk", [P, X_HEADS, N_MEM])
        memv = sb("memv", [P, TOK, X_WIDTH])
        const = sb("const", [P, N_CONST])
        cols = sb("cols", [P, DEPTH, N_COLS])
        cols_mix = sb("cols_mix", [P, DEPTH, 28])
        cols_ka = sb("cols_ka", [P, DEPTH, PAIRS])
        vdown = sb("vdown", [P, PAIRS, V_LORA])
        stat = sb("stat", [P, 64])
        lora_w = sb("lora_w", [P, 4, P])
        lora_in = sb("lora_in", [P, 3, 2, SEQ])
        v_low = lora_in[32:32 + V_LORA, 2, 1, :]

        def view(off, *shape):
            n = int(np.prod(shape))
            names = "abcd"[:len(shape)]
            v = arena[:, off:off + n]
            if len(shape) == 1:
                return v
            return v.rearrange(f"p ({' '.join(names)}) -> p {' '.join(names)}", **dict(zip(names, shape)))

        qk = view(0, 5, 2, SEQ)
        k_both = view(2560, AT_KV_HEADS, SEQ)
        v_at = view(3584, TOK, AT_KV)
        prob = view(4096, 8, SEQ)
        probT = view(6144, 4, 2 * SEQ)
        probs = [prob, view(8192, 8, SEQ)]
        sq_tmp = view(9216, 2, SEQ)
        qk_sq = view(4096, 5, 2, SEQ)
        QK_HEADS = AT_HEADS + AT_KV_HEADS
        of_head = view(6656, QK_HEADS, HEAD)
        qk_root = view(9728, TOK, QK_HEADS)
        qk_rootT = view(9984, SEQ)
        x_q = view(10752, X_HEADS, SEQ)
        x_y = view(11776, X_HEADS, SEQ)
        AR = view(0, 2, NCH, 2, P)
        KB = view(2048, 2, NCH, 2, P)
        KBt = rows[:, :, :, :].rearrange("p a b c -> p (a b c)").rearrange("p (d c w n) -> p d c w n", d=2, c=NCH, w=2)
        GT = view(4096, 2, NCH, 3, P)
        XA = view(7168, 2, NCH, P)
        XTA = view(8192, 2, NCH, P)
        XB = view(9216, 2, NCH, P)
        XTB = view(10240, 2, NCH, P)
        ET = view(11264, 2, NCH, P)
        EE = view(12288, 2, NCH, P)
        OFF = {32: view(13312, 2, NCH, P),
               64: low_in[:, :, :].rearrange("p a b -> p (a b)").rearrange("p (d c n) -> p d c n", d=2, c=NCH)}
        tb = tok_buf[:, :, :].rearrange("p a b -> p (a b)")

        def tview(off, *shape):
            n = int(np.prod(shape))
            names = "abcd"[:len(shape)]
            v = tb[:, off:off + n]
            if len(shape) == 1:
                return v
            return v.rearrange(f"p ({' '.join(names)}) -> p {' '.join(names)}", **dict(zip(names, shape)))

        sig = tview(0, 4, SEQ)
        inc = tview(1024, 2, SEQ)
        exc = tview(1536, 2, SEQ)
        p_inc = tview(2048, 2, SEQ)
        p_inv = tview(2560, 2, SEQ)
        p_exc = tview(3072, 2, SEQ)
        kd = tview(3584, 2, SEQ)
        ar_side = tb[:, 1024:1024 + 4096 - 1024].rearrange("p (x d c n) -> p x d c n", x=6, d=2, c=NCH)[:, 0:5:4]
        b_side = tview(512, 2, NCH, HEAD)
        AT_c = tview(0, 2, NCH, HEAD)
        A_c = tview(1536, 2, NCH, HEAD)
        XT_c = tview(2560, 2, NCH, HEAD)
        X_c = tview(512, 2, NCH, HEAD)
        E_c = tview(3584, 2, NCH, HEAD)
        X2_c = tb[:, 1024:4096].rearrange("p (x d c n) -> p x d c n", x=6, d=2, c=NCH)[:, 0:5:4]
        P_c = X_c
        v_cur = sb("v_cur", [P, SEQ])
        tmp = sb("tmp", [P, SEQ])
        tmp2 = sb("tmp2", [P, SEQ])
        g_cur = sb("g_cur", [P, SEQ])
        Vc = sb("Vc", [P, NCH, HEAD])
        Yc = sb("Yc", [P, NCH, HEAD])
        Wc = sb("Wc", [P, 2, HEAD])
        Uc = sb("Uc", [P, 2, HEAD])
        St = sb("St", [P, 2, HEAD])
        prow = view(12288, DEPTH, 2, P)
        junk = view(0, D_MODEL)
        gain_row = view(2048, D_MODEL)
        tiles8 = lambda t: t.rearrange("p (k n) -> p k n", n=SEQ)
        ring_high = arena_parts[:, 4096:8192].rearrange("p (s n) -> p s n", s=RING)
        ring_high_f32 = ring_high.bitcast(F32)
        op_high = tiles8(arena_parts[:, 8192:12288])
        op_high_f32 = op_high.bitcast(F32)
        xy_low = tiles8(arena_parts[:, 11776:12800])
        hid_high = [tiles8(streams_parts[:, 0, :]), tiles8(streams_parts[:, 2, :])]
        hid_high_f32 = [t.bitcast(F32) for t in hid_high]
        hid_low = [tiles8(streams_parts[:, 4, :]), y_at_parts[:, :, :]]

        def operand(k):
            return op_high[:, k, :], opT_parts[:, k, :]

        def y_rw_operand(k):
            return op_high[:, k, :], tiles8(streams_parts[:, 0, :])[:, k, :]

        def y_at_operand(k):
            return op_high[:, PAIRS + k, :], y_at_parts[:, k, :]

        def x_y_operand(k):
            return op_high[:, k, :], xy_low[:, k, :]

        def hidden(k):
            return hid_high[k // 8][:, k % 8, :], hid_low[k // 8][:, k % 8, :]

        psum = ctx.enter_context(nc.psum_tensor("psum", [P, 8, 512], F32))
        gates = streams[:, 1:5, :].rearrange("p (t b) d -> p t (b d)", t=TOK).rearrange("p t (u n) -> p u t n", n=UNIT)
        acc = psum[:, 0:4, :].rearrange("p (u t) n -> p u t n", t=TOK)
        work = psum[:, 4:8, :]
        gate_acc = psum[:, 6:8, :]
        mem_saved = nc.dram_tensor("mem_saved", [P, 2, D_MODEL], F32, kind="Internal").ap()
        x_saved = nc.dram_tensor("x_saved", [P, TOK, D_MODEL], F32, kind="Internal").ap()

        def cst(name):
            o, w = CONST[name]
            return const[:, o:o + w]

        ident, head_ones, rot = cst("ident"), cst("head_ones"), cst("rot")
        mask = cst("mask").rearrange("p (d n) -> p d n", d=2)

        def col(l, name, j=0, n=1):
            return cols[:, l, PCOL[name] + j:PCOL[name] + j + n]

        def colv(l, name, n):
            return cols[:, l, PCOL[name]:PCOL[name] + n]

        s_const = sem("constants_landed")
        s_rows_zero = sem("param_rows_zeroed")
        s_rows = sem("param_rows_landed")
        s_rows_hw = sem("param_rows_landed_by_hardware_queues")
        s_x = sem("x_landed")
        s_mem = sem("mem_landed")
        s_gain = sem("gain_row_landed")
        s_gain_free = sem("gain_row_free")
        s_lw = sem("lora_weights_landed")
        s_lw_free = sem("lora_weights_free")
        s_land = [sem(f"slab_landed{i}") for i in range(RING)]
        s_used = sem("slab_used")
        s_high = sem("slab_high_part_ready")
        s_split = sem("slab_split")
        s_operand = sem("operand_split")
        s_asked = sem("branch_weights_asked_for")
        s_emptied = sem("unit_emptied")
        s_branch = sem("branch_unit_emptied")
        s_gate = sem("gate_unit_emptied")
        s_x_idle = sem("x_idle_from_vector")
        s_mem_normed = sem("mem_rows_normed")
        s_mem_saved = sem("mem_rows_saved_in_dram")
        s_mem_back = sem("mem_rows_back")
        s_opT_free = sem("operand_place_free")
        s_x_saved = sem("x_saved_in_dram")
        s_x_back = sem("x_back_in_place")
        s_rows_free = sem("unit_rows_transposed")
        s_full = sem("work_bank_full")
        s_drained = sem("work_bank_drained")
        s_sfull = sem("scan_bank_full")
        s_sdrained = [sem(f"scan_bank{b}_drained") for b in range(SCAN_BANKS)]
        s_pool = sem("pool_result")
        s_for_pool = sem("vector_result_for_pool")
        s_act_pe = sem("scalar_result_for_tensor")
        s_scores = sem("group_scores_full")
        s_exps = sem("group_scores_exponentiated")
        s_squared = sem("unit_squared")
        s_x_tile = sem("x_tile_updated")
        s_act = sem("scalar_step")
        s_dve = sem("vector_step")
        s_for_pe = sem("vector_result_for_tensor")
        s_for_act = sem("vector_result_for_scalar")
        s_from_act = sem("scalar_result_for_vector")
        s_out = sem("output_stored")

        w_in = a["w_in"]
        C_LORA, C_Q = 3 * RW_WIDTH, RW_COLS
        C_KV, C_G = RW_COLS + AT_Q, RW_COLS + AT_COLS

        def slabs_of(w2d, ncols):
            return w2d.rearrange("(s p) (u n) -> u s p n", p=P, n=ncols)

        rows_landed = Tally(s_rows, 16)

        def param_loads():
            loads = []
            for l in range(DEPTH):
                for g, group in enumerate(PARAM_ROWS):
                    r0 = 0
                    for name, n in group:
                        if name == "qk_norm":
                            for j in range(n):
                                g_src = a["at_q_norm" if j < 4 else "at_k_norm"][l:l + 1, :]
                                for h in range(2):
                                    loads.append((prow[r0 + j:r0 + j + 1, l, g, h * HEAD:(h + 1) * HEAD], g_src))
                        elif name != "rw_v0" or l:
                            if name == "rw_v0":
                                src = a[name][l - 1]
                            elif name in ("rw_w0", "rw_a0"):
                                src = a[name][l].rearrange("d c -> (d c)")
                            elif name == "rw_r_k":
                                src = a[name][l].rearrange("h c -> (h c)")
                            else:
                                src = a[name][l]
                            full = src.shape[0] // P
                            loads.append((prow[r0:r0 + full, l, g, :], src[0:full * P].rearrange("(r c) -> r c", c=P)))
                            rest = src.shape[0] - full * P
                            if rest:
                                loads.append((prow[r0 + full:r0 + full + 1, l, g, 0:rest],
                                              src[full * P:].rearrange("(r c) -> r c", r=1)))
                        r0 += n
            return loads

        def hw_loads(eng, part):
            eng.wait_ge(s_rows_zero, 1)
            for dst, src in param_loads()[part::3]:
                eng.dma_start(dst, src).then_inc(s_rows_hw, 16)

        block = ctx.enter_context(nc.Block())

        @block.sync
        def _(sp):
            slab = Tally(s_used)
            sp.dma_start(const[:, :], a["shape_constants"]).then_inc(s_const, 16)
            sp.dma_start(x, a["x"].rearrange("b (t p) d -> p (b t) d", p=P)).then_inc(s_x, 16)
            hw_loads(sp, 0)

            def load(src, note=False):
                slot = slab.count % RING
                if slab.count >= RING:
                    sp.wait_ge(s_used, slab.at(RING - 1))
                    if note:
                        sp.sem_inc(s_asked, 1)
                slab.next()
                for dst, part in src(ring[:, slot]):
                    sp.dma_start(dst, part).then_inc(s_land[slot], 32 // len(src(ring[:, slot])))

            def whole(part):
                w = part.shape[-1]
                return lambda r: [(r[:, 0:w], part)]

            for l in range(DEPTH):
                mem_w = slabs_of(a["x_wkv"][l], UNIT)
                for u in range(2):
                    for s in range(16):
                        load(whole(mem_w[u, s]))
                rkv = slabs_of(w_in[l][:, 0:3 * RW_WIDTH], UNIT)
                with repeat(sp, 3, {slab: 32}) as i:
                    for j in range(2):
                        v = rkv.rearrange("(i j) s p n -> j i s p n", j=2)[j]
                        for s in range(16):
                            load(whole(v[i, s]))
                lora = slabs_of(w_in[l][:, C_LORA:C_LORA + UNIT], UNIT)
                for s in range(16):
                    load(whole(lora[0, s]))
                qkv = slabs_of(w_in[l][:, C_Q:C_Q + AT_COLS], UNIT)
                for u in range(3):
                    for s in range(16):
                        load(whole(qkv[u, s]))
                gate_w = slabs_of(w_in[l][:, C_G:C_G + 2 * D_MODEL], UNIT)
                wr, wa = slabs_of(a["w_rw_out"][l], UNIT), slabs_of(a["w_at_out"][l], UNIT)
                with repeat(sp, PAIRS, {slab: 16}) as i:
                    for s in range(16):
                        load(whole(gate_w[i, s]))
                with repeat(sp, 4, {slab: 16}) as i:
                    for s in range(8):
                        load(whole(wr[i, s]), note=s == 0)
                    for s in range(8):
                        load(whole(wa[i, s]))
                wo = slabs_of(a["w_o"][l], UNIT)
                with repeat(sp, 4, {slab: 16}) as i:
                    for s in range(16):
                        load(whole(wo[i, s]))
                xq = slabs_of(a["x_wq"][l], UNIT)
                for s in range(16):
                    load(whole(xq[0, s]))
                xo = slabs_of(a["x_wo"][l], UNIT)
                for u in range(4):
                    for s in range(4):
                        load(whole(xo[u, s]))
                wg, wu = slabs_of(a["ffn_wg"][l], 256), slabs_of(a["ffn_wu"][l], 256)
                t0 = 0
                for tiles in FF_PARTS:
                    n = tiles // 2
                    g_v = wg[t0 // 2:t0 // 2 + n].rearrange("(i j) s p n -> j i s p n", j=2)
                    u_v = wu[t0 // 2:t0 // 2 + n].rearrange("(i j) s p n -> j i s p n", j=2)
                    with repeat(sp, n // 2, {slab: 32}) as i:
                        for j in range(2):
                            for s in range(16):
                                load(lambda r, j=j, s=s: [(r[:, 0:256], g_v[j][i, s]), (r[:, 256:512], u_v[j][i, s])])
                    wd = slabs_of(a["ffn_wd"][l][t0 * P:(t0 + tiles) * P, :], UNIT)
                    wd_v = wd.rearrange("(i j) s p n -> j i s p n", j=2)
                    with repeat(sp, 2, {slab: 2 * tiles}) as i:
                        for j in range(2):
                            for s in range(tiles):
                                load(whole(wd_v[j][i, s]))
                    t0 += tiles
            sp.wait_ge(s_out, 1)
            sp.dma_start(out.rearrange("b (t p) d -> p (b t) d", p=P), x).then_inc(s_x, 16)
            sp.wait_ge(s_x, 32)

        @block.gpsimd
        def _(pool):
            pool.dma_start(tok_buf[:, :, :], a["mem"].rearrange("b (t p) d -> p (b t) d", p=P)).then_inc(s_mem, 16)
            pool.wait_ge(s_rows_zero, 1)
            for dst, src in param_loads()[2::3]:
                pool.dma_start(dst, src).then_inc(s_rows, 16)
                rows_landed.next()
            pool.dma_start(vdown[:, :, :], a["rw_v_down"][0].rearrange("(t p) n -> p t n", p=P)).then_inc(s_rows, 16)
            rows_landed.next()
            landed = Tally(s_lw, 16)
            for_pool = Tally(s_for_pool)
            gain = Tally(s_gain_free)
            for l in range(DEPTH):
                if l == 0:
                    pool.wait_ge(s_mem_normed, 1)
                    pool.dma_start(mem_saved, streams[:, 0:3:2, :]).then_inc(s_mem_saved, 16)
                n_lw = 7 if l else 6
                if l:
                    pool.wait_ge(s_x_idle, 2 * l + 1)
                    pool.dma_start(x_saved, x).then_inc(s_x_saved, 16)
                with repeat(pool, PAIRS, {landed: n_lw, for_pool: 1}) as i:
                    pool.wait_ge(s_lw_free, i + (l * (PAIRS + 1) + 1))
                    for d in range(2):
                        w_v = a["rw_w_up"][l, d].rearrange("r (i c) -> i r c", c=P)
                        a_v = a["rw_a_up"][l, d].rearrange("r (i c) -> i r c", c=P)
                        pool.dma_start(lora_w[d * 64:(d + 1) * 64, 0, :], w_v[i]).then_inc(s_lw, 16)
                        pool.dma_start(lora_w[d * 64:(d + 1) * 64, 1, :], a_v[i]).then_inc(s_lw, 16)
                        landed.next(2)
                    g_v = a["rw_g_up"][l].rearrange("r (i c) -> i r c", c=P)
                    pool.dma_start(lora_w[:, 2, :], g_v[i, 0:P]).then_inc(s_lw, 16)
                    pool.dma_start(lora_w[0:32, 3, :], g_v[i, P:G_LORA]).then_inc(s_lw, 16)
                    landed.next(2)
                    if l:
                        v_v = a["rw_v_up"][l - 1].rearrange("r (i c) -> i r c", c=P)
                        pool.dma_start(lora_w[32:32 + V_LORA, 3, :], v_v[i]).then_inc(s_lw, 16)
                        landed.next()
                    pool.wait_ge(s_for_pool, for_pool.next())
                    for d in range(2):
                        for n in (32, 64):
                            in_n = cst(f"in{n}").rearrange("p (h n) -> p h n", h=2).unsqueeze(1).to_broadcast([P, NCH, 2, HEAD])
                            ins = nc.gpsimd.tensor_tensor(OFF[n][:, d].rearrange("p c (h n) -> p c h n", h=2),
                                                          A_c[:, d].unsqueeze(2).to_broadcast([P, NCH, 2, HEAD]), in_n, ALU.mult)
                    ins.then_inc(s_pool, 1)
                for name in ("n_mix_post", "n_x_post", "n_ffn_post"):
                    if name == "n_x_post":
                        if l:
                            pool.wait_ge(s_x_saved, 16 * l)
                        pool.wait_ge(s_x_idle, 2 * l + 2)
                        pool.dma_start(x, x_saved if l else a["x"].rearrange("b (t p) d -> p (b t) d", p=P)).then_inc(s_x_back, 16)
                    pool.wait_ge(s_gain_free, gain.next())
                    pool.dma_start(gain_row, a[name][l].partition_broadcast(P)).then_inc(s_gain, 16)
                if l < DEPTH - 1:
                    pool.wait_ge(s_mem_saved, 16)
                    pool.wait_ge(s_opT_free, l + 1)
                    pool.dma_start(opT[:, :, :], mem_saved.rearrange("p b (k n) -> p (b k) n", n=SEQ)).then_inc(s_mem_back, 16)

        @block.tensor
        def _(pe):
            slab = Tally(s_used)
            split = Tally(s_split)
            ready = Tally(s_operand)
            emptied = Tally(s_emptied)
            branch = Tally(s_branch)
            branch.next(2)
            gate = Tally(s_gate)
            gate.next()
            full = Tally(s_full)
            for_pe = Tally(s_for_pe)
            lw = Tally(s_lw, 16)
            scan = Banks(Tally(s_sfull), s_sdrained)
            scan_before, scan_last, scan_start = None, [None], [0]
            from_act = Tally(s_act_pe)
            exps = Tally(s_exps)
            from_pool = Tally(s_pool)

            def unit(ub, nslab, operand, width=UNIT, wait=True, between=None):
                if wait:
                    if emptied.count >= 2:
                        pe.wait_ge(s_emptied, emptied.at(1))
                    emptied.next()
                for k in range(nslab):
                    slot = slab.count % RING
                    slab.next()
                    pe.wait_ge(s_split, split.next())
                    high, low = operand(k)
                    w_high, w_low = ring_high[:, slot, 0:width], ring_parts[:, slot, 0:width]
                    for tok in range(TOK):
                        c = slice(tok * P, (tok + 1) * P)
                        nc.tensor.matmul(acc[:, ub, tok, 0:width], high[:, c], w_high, start=k == 0, stop=False)
                        nc.tensor.matmul(acc[:, ub, tok, 0:width], high[:, c], w_low, start=False, stop=False)
                        last = nc.tensor.matmul(acc[:, ub, tok, 0:width], low[:, c], w_high, start=False, stop=k == nslab - 1)
                    last.then_inc(s_used, 1)
                    if between and k == nslab // 2 - 1:
                        between()

            def gate_unit():
                pe.wait_ge(s_gate, gate.at())
                gate.next()
                for k in range(KD):
                    slot, use = slab.count % RING, slab.count // RING + 1
                    pe.wait_ge(s_land[slot], slab.loop[0] * (slab.loop[1] // RING * 32) + 32 * use)
                    slab.next()
                    for tok in range(TOK):
                        last = nc.tensor.matmul(gate_acc[:, tok, :], opT[:, k, tok * P:(tok + 1) * P], ring[:, slot, :],
                                                start=k == 0, stop=k == KD - 1)
                        if tok == TOK - 1:
                            last.then_inc(s_used, 1)
                        yield

            def settle():
                if emptied.count:
                    pe.wait_ge(s_emptied, emptied.at())

            def fill(products, aligned=False):
                b = full.count % 4
                if full.count >= 4:
                    pe.wait_ge(s_drained, full.at(3))
                last = products(work[:, b, :])
                n = 1 + (-(full.count + 1) % 4 if aligned else 0)
                last.then_inc(s_full, n)
                full.next(n)
                return full.at()

            def have(n):
                pe.wait_ge(s_drained, n)

            def transpose_unit(ub, tiles, lag, aligned=False):
                pe.wait_ge(s_emptied, emptied.at(lag))
                for b0 in range(0, len(tiles), 2):
                    def go(bank):
                        for j, w in enumerate(tiles[b0:b0 + 2]):
                            for tok in range(TOK):
                                c0 = (b0 + j) * P
                                last = nc.tensor.transpose(bank[0:w, j * SEQ + tok * P:j * SEQ + (tok + 1) * P],
                                                           rows[:, ub, tok, c0:c0 + w], ident)
                        return last
                    fill(go, aligned and b0 + 2 >= len(tiles))

            def transpose_tok(n_src=TOK):
                for tok in range(TOK):
                    pe.wait_ge(s_for_pe, for_pe.next())
                    for g in range(KD // 4):
                        def go(bank):
                            for j in range(4):
                                k = 4 * g + j
                                last = nc.tensor.transpose(bank[:, j * P:(j + 1) * P], tok_buf[:, tok, k * P:(k + 1) * P], ident)
                            return last
                        fill(go)
                settle()
                pe.wait_ge(s_operand, ready.next())

            def sfill(products, pad=0):
                nonlocal scan_before
                b, free = scan.now()
                pe.wait_ge(s_sdrained[b], free)
                scan_before = scan_last[0]
                last = products(psum[:, b, :])
                n = 1 if not pad else pad - (scan.tally.count - scan_start[0])
                last.then_inc(s_sfull, n)
                scan.tally.next(n)
                scan_last[0] = (b, free + 2)
                return scan_last[0]

            def shave(q):
                pe.wait_ge(s_sdrained[q[0]], q[1])

            def softmax_turn(prob, wait=False):
                for b in range(4):
                    def go(bank):
                        for st in range(2):
                            for qt in range(2):
                                last = nc.tensor.transpose(bank[:, st * SEQ + qt * P:st * SEQ + (qt + 1) * P],
                                                           prob[:, 2 * b + qt, st * P:(st + 1) * P], ident)
                        return last
                    if b == 0 and wait:
                        have(full.at())
                    n = fill(go)
                have(n)

            pe.wait_ge(s_const, 16)
            pe.wait_ge(s_rows, rows_landed.at())
            pe.wait_ge(s_rows_hw, 16 * (len(param_loads()[0::3]) + len(param_loads()[1::3])))
            for l in range(DEPTH):
                for g in range(2):
                    n = GROUP_ROWS[g]
                    fill(lambda bank: nc.tensor.transpose(bank[:, 0:n], prow[0:n, l, g, :], ident[0:n, 0:n]))
            for l in range(DEPTH):
                if l == 0:
                    transpose_tok()
                else:
                    pe.wait_ge(s_operand, ready.next())
                keys, values_in = MEM_UNITS[l]
                unit(keys, 16, operand)
                unit(values_in, 16, operand)
                transpose_unit(keys, [P] * 4, 1)
                transpose_tok()
                with repeat(pe, 3, {slab: 32, split: 32, emptied: 2, full: 4}):
                    unit(0, 16, operand)
                    unit(1, 16, operand, between=lambda: transpose_unit(0, [P] * 4, 1))
                    transpose_unit(1, [P] * 4, 0)
                unit(0, 16, operand, width=LORA_COLS)
                unit(1, 16, operand, between=lambda: transpose_unit(0, LORA_W, 1))
                unit(0, 16, operand, between=lambda: transpose_unit(1, [P] * 4, 1))
                unit(1, 16, operand, between=lambda: transpose_unit(0, [P] * 4, 1))
                transpose_unit(1, [P] * 2, 0, aligned=True)
                def sums(bank):
                    for tok in range(TOK):
                        for t in range(QK_HEADS // 2):
                            o = tok * QK_HEADS + 2 * t
                            last = nc.tensor.matmul(bank[:, o:o + 2], qk_sq[:, t // 2, t % 2, tok * P:(tok + 1) * P],
                                                    head_ones[:, 0:P:HEAD], start=True, stop=True)
                    return last

                def roots_turn(bank):
                    for tok in range(TOK):
                        last = nc.tensor.transpose(bank[0:QK_HEADS, tok * P:(tok + 1) * P], qk_root[:, tok, :], ident)
                    return last

                def spread(i):
                    def go(bank):
                        for t in range(2):
                            w = of_head[0:QK_HEADS, 4 * i + 2 * t:4 * i + 2 * t + 2, :].rearrange("p h n -> p (h n)")
                            last = nc.tensor.matmul(bank[:, t * SEQ:(t + 1) * SEQ], w, qk_rootT[0:QK_HEADS, :], start=True, stop=True)
                        return last
                    return go

                def turn_pairs(i):
                    pe.wait_ge(s_for_pe, for_pe.next())
                    fill(lambda bank: nc.tensor.matmul(bank, rot, qk_sq[:, i], start=True, stop=True))
                pe.wait_ge(s_for_pe, for_pe.next())
                fill(sums)
                pe.wait_ge(s_for_pe, for_pe.next())
                have(fill(roots_turn))
                fill(spread(0))
                for i in range(1, 5):
                    fill(spread(i))
                    turn_pairs(i - 1)
                turn_pairs(4)
                def scores(g):
                    if g:
                        pe.wait_ge(s_exps, exps.next())
                    for tile in range(2):
                        for h in range(2):
                            r = slice(h * HEAD, (h + 1) * HEAD)
                            for qt in range(2):
                                last = nc.tensor.matmul(psum[:, 2 * tile + h, qt * SEQ:(qt + 1) * SEQ],
                                                        qk[r, g, tile, qt * P:(qt + 1) * P], k_both[r, g, :], start=True, stop=True)
                    last.then_inc(s_scores, 1)

                def values(bank):
                    for tile in range(2):
                        for h in range(2):
                            for st in range(2):
                                last = nc.tensor.matmul(bank[h * HEAD:(h + 1) * HEAD, tile * SEQ:(tile + 1) * SEQ],
                                                        v_at[:, st, g * HEAD:(g + 1) * HEAD],
                                                        probT[:, 2 * tile + h, st * SEQ:(st + 1) * SEQ],
                                                        start=st == 0, stop=st == 1)
                    return last
                pe.wait_ge(s_for_pe, for_pe.next())
                settle()
                scores(0)
                for g in range(AT_KV_HEADS):
                    if g < AT_KV_HEADS - 1:
                        scores(g + 1)
                    pe.wait_ge(s_for_pe, for_pe.next())
                    softmax_turn(probs[g % 2])
                    fill(values, aligned=g == AT_KV_HEADS - 1)
                exps.next()
                if l:
                    pe.wait_ge(s_for_pe, for_pe.next())
                    def low(bank):
                        for j in range(PAIRS):
                            last = nc.tensor.matmul(bank[0:V_LORA, 0:SEQ], vdown[:, j, :], v_all[:, j, :],
                                                    start=j == 0, stop=j == PAIRS - 1)
                        return last
                    fill(low, aligned=True)
                pe.wait_ge(s_for_pe, for_pe.next())
                settle()
                with repeat(pe, PAIRS, {scan.tally: PER_PAIR, for_pe: 4, from_act: 2, from_pool: 1, slab: 16, gate: 1, lw: 7 if l else 6}):
                    scan_start[0] = scan.tally.count
                    beside = gate_unit()

                    def step(n=1):
                        for _ in range(n):
                            next(beside, None)
                    pe.wait_ge(s_lw, lw.next(7 if l else 6))
                    sfill(lambda bank: nc.tensor.matmul(bank, lora_w[:, 0, :], lora_in[:, 0], start=True, stop=True))
                    sfill(lambda bank: nc.tensor.matmul(bank, lora_w[:, 1, :], lora_in[:, 1], start=True, stop=True))
                    if l:
                        sfill(lambda bank: nc.tensor.matmul(bank[:, 0:SEQ], lora_w[32:32 + V_LORA, 3, :], v_low, start=True, stop=True))

                    def gate_low(bank):
                        nc.tensor.matmul(bank[:, 0:SEQ], lora_w[:, 2, :], lora_in[:, 2, 0, :], start=True, stop=False)
                        return nc.tensor.matmul(bank[:, 0:SEQ], lora_w[0:32, 3, :], lora_in[0:32, 2, 1, :], start=False, stop=True)
                    sfill(gate_low)
                    step(6)
                    pe.wait_ge(s_for_pe, for_pe.next())
                    sfill(lambda bank: nc.tensor.matmul(bank[:, 0:SEQ], head_ones, tmp[:, :], start=True, stop=True))
                    sfill(lambda bank: nc.tensor.matmul(bank[:, 0:SEQ], head_ones, tmp2[:, :], start=True, stop=True))

                    def v_turn(bank):
                        for c2 in range(NCH // 2):
                            last = nc.tensor.transpose(bank[:, c2 * P:(c2 + 1) * P], v_cur[:, c2 * P:(c2 + 1) * P], ident)
                        return last
                    sfill(v_turn)
                    step(10)
                    pe.wait_ge(s_act_pe, from_act.next())
                    for d in range(2):
                        for c2 in range(0, NCH, 2):
                            def go(bank):
                                for j in range(2):
                                    for w in range(2):
                                        o = bank[:, (2 * j + w) * P:(2 * j + w + 1) * P].rearrange("p (x n) -> p x n", x=2)
                                        last = nc.tensor.matmul(o, KB[:, d, c2 + j, w, :], ar_side[:, :, d, c2 + j, :], start=True, stop=True)
                                return last
                            sfill(go)

                    def natural(bank):
                        for d in range(2):
                            for c in range(NCH):
                                o = bank[:, (d * NCH + c) * HEAD:(d * NCH + c + 1) * HEAD]
                                last = nc.tensor.matmul(o, AR[:, d, c, 0, :], b_side[:, d, c, :], start=True, stop=True)
                        return last
                    pe.wait_ge(s_act_pe, from_act.next())
                    sfill(natural)
                    for d in range(2):
                        for c2 in range(0, NCH, 2):
                            def go(bank):
                                for j in range(4):
                                    last = nc.tensor.transpose(bank[:, j * P:(j + 1) * P], KB[:, d, c2 + j // 2, j % 2, :], ident)
                                return last
                            sfill(go)

                    def blocks(*products):
                        def go(bank):
                            for k, (lhs, rhs) in enumerate(products):
                                for c in range(NCH):
                                    o = bank[:, (k * NCH + c) * HEAD:(k * NCH + c + 1) * HEAD]
                                    last = nc.tensor.matmul(o, lhs[:, c, :], rhs[:, c, :], start=True, stop=True)
                            return last
                        return go

                    def turned(src):
                        def go(bank):
                            for c in range(NCH):
                                last = nc.tensor.transpose(bank[:, c * P:(c + 1) * P], src[:, c, :], ident)
                            return last
                        return go

                    step(4)
                    done = {}
                    for d in range(2):
                        pe.wait_ge(s_for_pe, for_pe.next())
                        done[d] = sfill(blocks((XTA[:, d], X_c[:, d]), (XA[:, d], XT_c[:, d])))
                    for d in range(2):
                        shave(done[d])
                        sfill(blocks((XB[:, d], E_c[:, d]), (XTB[:, d], X2_c[:, 0, d])))
                        done[d] = sfill(blocks((XB[:, d], X2_c[:, 1, d])))
                        done[d, 1] = scan_before
                    for d in range(2):
                        shave(done[d, 1])
                        shave(done[d])
                        done[d] = sfill(blocks((XA[:, d], E_c[:, d]), (XTA[:, d], X_c[:, d])))
                    for d in range(2):
                        shave(done[d])
                        done[d] = sfill(blocks((XB[:, d], E_c[:, d])))
                    pe.wait_ge(s_pool, from_pool.next())
                    for n in (32, 64):
                        for d in range(2):
                            shave(done[d])
                            done[d, 1] = sfill(blocks((OFF[n][:, d], E_c[:, d])))
                            done[d] = sfill(turned(EE[:, d]))
                        for d in range(2):
                            shave(done[d, 1])
                            shave(done[d])
                            done[d] = sfill(blocks((ET[:, d], P_c[:, d])))
                    shave(done[0])
                    shave(done[1])
                    for n in range(NCH):
                        at = (n, NCH - 1 - n)

                        def go_w(bank):
                            for d, c in enumerate(at):
                                o = bank[:, d * HEAD:(d + 1) * HEAD]
                                if n:
                                    nc.tensor.matmul(o, AR[:, d, c, 0, :], St[:, d, :], start=True, stop=False)
                                last = nc.tensor.matmul(o, GT[:, d, c, 2, :], Vc[:, c, :], start=n == 0, stop=True)
                            return last

                        def go_u(bank):
                            for d, c in enumerate(at):
                                last = nc.tensor.matmul(bank[:, d * HEAD:(d + 1) * HEAD], EE[:, d, c, :], Wc[:, d, :], start=True, stop=True)
                            return last

                        def go_y(bank):
                            for d, c in enumerate(at):
                                o = bank[:, d * HEAD:(d + 1) * HEAD]
                                if n:
                                    nc.tensor.matmul(o, AR[:, d, c, 1, :], St[:, d, :], start=True, stop=False)
                                nc.tensor.matmul(o, GT[:, d, c, 0, :], Uc[:, d, :], start=n == 0, stop=False)
                                last = nc.tensor.matmul(o, GT[:, d, c, 1, :], Vc[:, c, :], start=False, stop=True)
                            return last

                        def go_s(bank):
                            for d, c in enumerate(at):
                                o = bank[:, d * HEAD:(d + 1) * HEAD]
                                nc.tensor.matmul(o, KBt[:, d, c, 0, :], Uc[:, d, :], start=True, stop=False)
                                last = nc.tensor.matmul(o, KBt[:, d, c, 1, :], Vc[:, c, :], start=False, stop=True)
                            return last
                        n_w = sfill(go_w)
                        step()
                        shave(n_w)
                        n_u = sfill(go_u)
                        step()
                        shave(n_u)
                        if n < NCH - 1:
                            n_s = sfill(go_s)
                            sfill(go_y)
                            shave(n_s)
                        else:
                            sfill(go_y)
                    step(KD * TOK)
                    pe.wait_ge(s_for_pe, for_pe.next())

                    def y_turn(bank):
                        for c2 in range(NCH // 2):
                            two_chunks = Yc[:, 2 * c2:2 * c2 + 2, :].rearrange("p c n -> p (c n)")
                            last = nc.tensor.transpose(bank[:, c2 * P:(c2 + 1) * P], two_chunks, ident)
                        return last
                    sfill(y_turn, pad=PER_PAIR)
                pe.wait_ge(s_gate, gate.at())
                pe.wait_ge(s_operand, ready.next())
                with repeat(pe, 4, {slab: 16, split: 16, branch: 2}):
                    pe.wait_ge(s_branch, branch.at(1))
                    unit(0, 8, y_rw_operand, wait=False)
                    pe.wait_ge(s_branch, branch.at())
                    unit(1, 8, y_at_operand, wait=False)
                    branch.next(2)
                pe.wait_ge(s_branch, branch.at())
                transpose_tok()
                with repeat(pe, 2, {slab: 32, split: 32, emptied: 2}):
                    unit(0, 16, operand)
                    unit(1, 16, operand)
                transpose_tok()
                unit(0, 16, operand)
                transpose_unit(0, [P] * 4, 0, aligned=True)
                have(full.at())
                for b in range(X_HEADS):
                    def go(bank):
                        for qt in range(2):
                            last = nc.tensor.matmul(bank[:, qt * SEQ:(qt + 1) * SEQ], x_q[:, b, qt * P:(qt + 1) * P], memk[:, b, :],
                                                    start=True, stop=True)
                        return last
                    fill(go)
                softmax_turn(prob, wait=True)
                for b2 in range(2):
                    def go(bank):
                        for j in range(2):
                            for st in range(2):
                                b = 2 * b2 + j
                                last = nc.tensor.matmul(bank[:, j * SEQ:(j + 1) * SEQ], memv[:, st, b * X_HEAD:(b + 1) * X_HEAD],
                                                        probT[:, b, st * SEQ:(st + 1) * SEQ], start=st == 0, stop=st == 1)
                        return last
                    fill(go, aligned=b2 == 1)
                pe.wait_ge(s_operand, ready.next())
                unit(1, 4, x_y_operand)
                for u in range(1, 4):
                    unit((u + 1) % 2, 4, x_y_operand)
                transpose_tok()
                ub = 1
                for tiles in FF_PARTS:
                    settle()
                    for half in range(0, tiles, 8):
                        with repeat(pe, min(8, tiles - half) // 4, {slab: 32, split: 32, emptied: 2, full: 4}):
                            unit(1, 16, operand)
                            unit(0, 16, operand, between=lambda: transpose_unit(1, [P] * 2, 1))
                            transpose_unit(0, [P] * 2, 0, aligned=True)
                    have(full.at())
                    with repeat(pe, 2, {slab: 2 * tiles, split: 2 * tiles, emptied: 2}):
                        unit(1, tiles, hidden)
                        unit(0, tiles, hidden)

        @block.scalar
        def _(act):
            slab = Tally(s_used)
            to_split = Tally(None)
            for_act = Tally(s_for_act)
            rows_free = Tally(s_rows_free)

            def high(n):
                for _ in range(n):
                    slot, use = to_split.count % RING, to_split.count // RING + 1
                    loop = to_split.loop
                    act.wait_ge(s_land[slot], 32 * use if loop is None else loop[0] * (loop[1] // RING * 32) + 32 * use)
                    nc.scalar.activation(ring_high[:, slot, :], ring[:, slot, :], ACT.Copy).then_inc(s_high, 1)
                    to_split.next()

            def operand_high():
                for tok in range(TOK):
                    c = slice(tok * P, (tok + 1) * P)
                    act.wait_ge(s_for_act, for_act.next())
                    nc.scalar.activation(op_high[:, :, c], opT[:, :, c], ACT.Copy).then_inc(s_from_act, 1)
                    from_act.next()

            def unit_rows(ub, nslab, width=UNIT, turned=True, split=None):
                high(nslab if split is None else split)
                if rows_free.count >= 2:
                    act.wait_ge(s_rows_free, rows_free.at(1))
                if turned:
                    rows_free.next()
                act.wait_ge(s_used, slab.next(nslab))
                nc.scalar.activation(rows[:, ub, :, 0:width], acc[:, ub, :, 0:width], ACT.Copy).then_inc(s_emptied, 1)

            def skip(n):
                scan.tally.next(n)

            def sbank(shared=False):
                b, free = scan.now()
                act_bank[0] = b
                if shared:
                    act.wait_ge(s_sdrained[b], free + 1)
                    scan.tally.next()
                else:
                    act.wait_ge(s_sfull, scan.tally.next())
                return psum[:, b, :]

            def sdrain(ins, n=2):
                ins.then_inc(s_sdrained[act_bank[0]], n)

            def turned_pairs(dst, bank):
                src = bank[:, 0:2 * P].rearrange("p (c n) -> p c n", c=2)
                for h in range(2):
                    for odd in range(2):
                        ins = nc.scalar.activation(dst[h * HEAD:(h + 1) * HEAD, :, odd, :],
                                                   src[odd * HEAD:(odd + 1) * HEAD, :, h * HEAD:(h + 1) * HEAD], ACT.Copy)
                sdrain(ins)

            def square(src, tok):
                nc.scalar.activation(junk, src[:, tok, :], ACT.Square, accum_out=stat[:, tok:tok + 1]).then_inc(s_from_act, 1)
                from_act.next()

            def rms(src, updated=False):
                for tok in range(TOK):
                    if updated:
                        act.wait_ge(s_x_tile, x_tile.next())
                    square(src, tok)
                    root(stat[:, 2 + tok:3 + tok])

            def root(v):
                act.wait_ge(s_for_act, for_act.next())
                nc.scalar.activation(v, v, ACT.Sqrt).then_inc(s_from_act, 1)
                from_act.next()

            def exps(scale, banks, prob):
                act.wait_ge(s_for_act, for_act.next())
                for k in range(8):
                    last = nc.scalar.activation(prob[:, k, :], banks[:, k // 2, (k % 2) * SEQ:(k % 2 + 1) * SEQ], ACT.Exp,
                                                bias=stat[:, 16 + k:17 + k], scale=scale, accum_out=stat[:, 24 + k:25 + k])
                return last

            from_act = Tally(s_from_act)
            x_tile = Tally(s_x_tile)
            scan = Banks(Tally(s_sfull), s_sdrained)
            act_bank = [0]
            hw_loads(act, 1)
            act.sem_inc(s_gate, 1)
            for l in range(DEPTH):
                keys, values_in = MEM_UNITS[l]
                if l == 0:
                    act.wait_ge(s_mem, 16)
                    act.wait_ge(s_x, 16)
                    act.wait_ge(s_for_act, for_act.next())
                    high(AHEAD)
                    rms(tok_buf)
                    operand_high()
                    unit_rows(keys, 16)
                    unit_rows(values_in, 16, turned=False)
                    act.wait_ge(s_for_act, for_act.next())
                    rms(x)
                else:
                    unit_rows(keys, 16, split=16 - 8)
                    rms(x, updated=True)
                    unit_rows(values_in, 16, turned=False)
                    act.wait_ge(s_for_act, for_act.next())
                operand_high()
                with repeat(act, 3, {slab: 32, to_split: 32, rows_free: 2}):
                    unit_rows(0, 16)
                    unit_rows(1, 16)
                unit_rows(0, 16, LORA_COLS)
                unit_rows(1, 16)
                unit_rows(0, 16)
                unit_rows(1, 16, split=16 - AHEAD)
                root(qk_root)
                for g in range(AT_KV_HEADS):
                    exps(HEAD ** -0.5, psum[:, 0:4, :], probs[g % 2]).then_inc(s_exps, 1)
                act.wait_ge(s_for_act, for_act.next())
                for d in range(2):
                    r = slice(d * 64, (d + 1) * 64)
                    nc.scalar.activation(lora_in[r, 0, d, :], low_in[r, 0, :], ACT.Tanh)
                nc.scalar.activation(lora_in[:, 2, 0, :], low_in[:, 2, :], ACT.Sigmoid)
                nc.scalar.activation(lora_in[0:32, 2, 1, :], low_in[0:32, 3, :], ACT.Sigmoid).then_inc(s_from_act, 1)
                from_act.next()
                if l:
                    act.wait_ge(s_x_saved, 16 * l)
                with repeat(act, PAIRS, {scan.tally: PER_PAIR, for_act: 8, from_act: 3, slab: 16}) as i:
                    start = scan.tally.count
                    act.wait_ge(s_for_act, for_act.next())
                    if l:
                        nc.scalar.activation(tmp2[:, :], tmp2[:, :], ACT.Sigmoid)
                    nc.scalar.activation(sig, sig, ACT.Sigmoid).then_inc(s_from_act, 1)
                    from_act.next()
                    skip(3 if l else 2)
                    bank = sbank()
                    sdrain(nc.scalar.activation(g_cur[:, :], bank[:, 0:SEQ], ACT.Copy))
                    act.wait_ge(s_for_act, for_act.next())
                    nc.scalar.activation(p_inc, inc, ACT.Exp, scale=-DECAY)
                    nc.scalar.activation(p_inv, inc, ACT.Exp, scale=DECAY)
                    nc.scalar.activation(p_exc, exc, ACT.Exp, scale=-DECAY).then_inc(s_from_act, 1)
                    from_act.next()
                    bank = sbank()
                    sdrain(nc.scalar.activation(tmp[:, :], bank[:, 0:SEQ], ACT.Sqrt))
                    skip(1)
                    v_bank = sbank()
                    turned_pairs(Vc[:, :, :].rearrange("p (c k) n -> p c k n", k=2), v_bank)
                    for n, (buf, which, src) in enumerate(((KB, 0, b_side), (KB, 1, E_c), (AR, 0, ar_side[:, 1]), (AR, 1, ar_side[:, 0]))):
                        if n < 2:
                            act.wait_ge(s_for_act, for_act.next())
                        for h in range(2):
                            if (n, h) == (1, 1):
                                act.wait_ge(s_for_act, for_act.next(2))
                            r = slice(h * HEAD, (h + 1) * HEAD)
                            ins = nc.scalar.activation(buf[r, :, :, which, r], src[r], ACT.Copy)
                        if n in (1, 3):
                            ins.then_inc(s_act_pe, 1)
                    skip(5)
                    for d in range(2):
                        for c2 in range(0, NCH, 2):
                            bank = sbank()
                            sdrain(nc.scalar.activation(KBt[:, d, c2:c2 + 2].rearrange("p c w n -> p (c w n)"), bank, ACT.Copy))
                    for d in range(2):
                        bank = sbank(shared=True)
                        sdrain(nc.scalar.activation(X2_c[:, :, d], bank.rearrange("p (x c n) -> p x c n", x=2, c=NCH), ACT.Copy), 1)
                    for d in range(2):
                        bank = sbank(shared=True)
                        sdrain(nc.scalar.activation(X_c[:, d].rearrange("p c n -> p (c n)"), bank[:, 256:512], ACT.Copy), 1)
                        skip(1)
                    skip(4)
                    for n in (32, 64):
                        for d in range(2):
                            skip(1)
                            bank = sbank()
                            sdrain(nc.scalar.activation(ET[:, d].rearrange("p c n -> p (c n)"), bank, ACT.Copy))
                        skip(2)
                    for n in range(NCH):
                        bank = sbank()
                        sdrain(nc.scalar.activation(Wc[:, :, :].rearrange("p d n -> p (d n)"), bank[:, 0:P], ACT.Copy))
                        skip(3 if n < NCH - 1 else 2)
                    root(stat[:, 8:12])
                    bank = sbank()
                    turned_pairs(tmp[:, :].rearrange("p (c k n) -> p c k n", k=2, n=CHUNK), bank)
                    skip(PER_PAIR - (scan.tally.count - start))
                    act.wait_ge(s_used, slab.next(16))
                    act.wait_ge(s_for_act, for_act.next())
                    nc.scalar.activation(gates[:, i], gate_acc, ACT.Sigmoid).then_inc(s_gate, 1)
                nc.scalar.activation(op_high[:, 0:PAIRS, :], y_rw, ACT.Copy)
                nc.scalar.activation(op_high[:, PAIRS:2 * PAIRS, :], y_at[:, :, :], ACT.Copy).then_inc(s_from_act, 1)
                from_act.next()
                to_split.next(PAIRS * 16)
                high(AHEAD)
                with repeat(act, 4, {slab: 16, to_split: 16}):
                    high(16)
                    slab.next(16)

                def product(n, nslab, ubs):
                    for j in range(n):
                        high(nslab)
                        act.wait_ge(s_used, slab.next(nslab))
                        for tok in range(TOK):
                            ins = nc.scalar.activation(junk[:, (2 * j + tok) % 4 * UNIT:((2 * j + tok) % 4 + 1) * UNIT], acc[:, ubs[j], tok], ACT.Square,
                                                       accum_out=stat[:, 52 + 4 * tok + j:53 + 4 * tok + j])
                        ins.then_inc(s_squared, 1)
                operand_high()
                product(4, 16, (0, 1, 0, 1))
                root(stat[:, 2:4])
                rms(x, updated=True)
                operand_high()
                unit_rows(0, 16, split=16 - AHEAD)
                exps(X_HEAD ** -0.5, work, prob).then_inc(s_from_act, 1)
                from_act.next()
                act.wait_ge(s_for_act, for_act.next())
                nc.scalar.activation(op_high[:, 0:X_HEADS, :], x_y, ACT.Copy).then_inc(s_from_act, 1)
                from_act.next()
                high(AHEAD)
                product(4, 4, (1, 0, 1, 0))
                root(stat[:, 2:4])
                rms(x, updated=True)
                operand_high()
                for part, tiles in enumerate(FF_PARTS):
                    for half in range(0, tiles, 8):
                        with repeat(act, min(8, tiles - half) // 4, {slab: 32, to_split: 32, rows_free: 2, from_act: 2}):
                            for ub in (1, 0):
                                high(16)
                                act.wait_ge(s_rows_free, rows_free.at(1))
                                rows_free.next()
                                act.wait_ge(s_used, slab.next(16))
                                nc.scalar.activation(rows[:, ub, :, 0:256], acc[:, ub, :, 0:256], ACT.Silu).then_inc(s_from_act, 1)
                                from_act.next()
                    if part == len(FF_PARTS) - 1:
                        high(2 * tiles)
                        if l < DEPTH - 1:
                            operand_high()
                            high(2 * tiles)
                        else:
                            high(2 * tiles - AHEAD)
                    else:
                        with repeat(act, 2, {to_split: 2 * tiles}):
                            high(2 * tiles)
                    slab.next(4 * tiles)
                act.wait_ge(s_for_act, for_act.next())
                if l < DEPTH - 1:
                    for tok in range(TOK):
                        square(tok_buf, tok)
                        high(4)
                        root(stat[:, 2 + tok:3 + tok])
                else:
                    rms(tok_buf)

        @block.vector
        def _(dve):
            V = nc.vector
            slab = Tally(s_used)
            split = Tally(s_high)
            full = Tally(s_full)
            drained = Tally(s_drained)
            step = Tally(s_dve)
            for_pe = Tally(s_for_pe)
            for_act = Tally(s_for_act)
            from_act = Tally(s_from_act)
            gain = Tally(s_gain, 16)
            scored = Tally(s_scores)
            squared = Tally(s_squared)
            exps = Tally(s_exps)
            scan = Banks(Tally(s_sfull), s_sdrained)
            branch = Tally(s_branch)
            dve.sem_inc(s_branch, 2)
            branch.next(2)
            dve_bank = [0, 0]
            for b in range(SCAN_BANKS):
                dve.sem_inc(s_sdrained[b], 2)

            def own(ins):
                ins.then_inc(s_dve, 1)
                dve.wait_ge(s_dve, step.next())

            def to_pe(ins):
                ins.then_inc(s_for_pe, 1)
                for_pe.next()

            def to_act(ins):
                ins.then_inc(s_for_act, 1)
                for_act.next()

            def act_result():
                dve.wait_ge(s_from_act, from_act.next())

            def bank():
                b = full.count % 4
                dve.wait_ge(s_full, full.next())
                return work[:, b, :]

            def drain(ins, n=1, wait=False, aligned=False):
                if aligned:
                    pad = -full.count % 4
                    full.next(pad)
                    n += pad
                ins.then_inc(s_drained, n)
                drained.next(n)
                if wait:
                    dve.wait_ge(s_drained, drained.at())

            def sbank():
                b, free = scan.now()
                dve_bank[:] = b, free
                dve.wait_ge(s_sfull, scan.tally.next())
                return psum[:, b, :]

            def sdrain(ins, n=2, wait=False):
                b = dve_bank[0]
                ins.then_inc(s_sdrained[b], n)
                if wait:
                    dve.wait_ge(s_sdrained[b], dve_bank[1] + n)

            def skipped():
                b, free = scan.now()
                scan.tally.next()
                return b, free + 2

            def shave(q):
                dve.wait_ge(s_sdrained[q[0]], q[1])

            def low(n):
                for _ in range(n):
                    slot = split.count % RING
                    dve.wait_ge(s_high, split.next())
                    V.tensor_tensor(ring_parts[:, slot, :], ring[:, slot, :], ring_high_f32[:, slot, :], ALU.subtract).then_inc(s_split, 1)

            def bc(ap, n):
                return ap.unsqueeze(2).to_broadcast([ap.shape[0], ap.shape[1], n])

            def rms_scale(tok, n=1, squared=True):
                v = lambda c: stat[:, c + tok:c + tok + n]
                if squared:
                    act_result()
                to_act(V.tensor_scalar(v(2), v(0), 1.0 / D_MODEL, EPS, ALU.mult, ALU.add))
                act_result()
                own(V.reciprocal(v(4), v(2)))

            def norm_rows(src):
                for tok in range(TOK):
                    rms_scale(tok)
                    to_pe(V.tensor_scalar(tok_buf[:, tok, :], src[:, tok, :], stat[:, 4 + tok:5 + tok], None, ALU.mult))

            def split_operand():
                for tok in range(TOK):
                    c = slice(tok * P, (tok + 1) * P)
                    act_result()
                    ins = V.tensor_tensor(opT_parts[:, :, c], opT[:, :, c], op_high_f32[:, :, c], ALU.subtract)
                ins.then_inc(s_operand, 1)

            def turned_rows(gains=None, keep=False):
                for tok in range(TOK):
                    for g in range(KD // 4):
                        src = bank().rearrange("p (j n) -> p j n", j=4)
                        dst = opT[:, 4 * g:4 * g + 4, tok * P:(tok + 1) * P]
                        if keep:
                            own(V.tensor_copy(tiles8(streams[:, 2 * (g // 2), :])[:, g % 2 * 4:g % 2 * 4 + 4, tok * P:(tok + 1) * P], src))
                        if gains is None:
                            ins = V.tensor_copy(dst, src)
                        else:
                            ins = V.tensor_tensor(dst, src, bc(gains[:, 4 * g:4 * g + 4], P), ALU.mult)
                        drain(ins, wait=g == KD // 4 - 1)
                    nudge_act()
                if keep:
                    dve.sem_inc(s_mem_normed, 1)
                split_operand()

            def units_by_gains(nslab, ubs):
                dve.wait_ge(s_gain, gain.next())
                for j in range(4):
                    low(nslab)
                    dve.wait_ge(s_squared, squared.next())
                    c = slice(j * UNIT, (j + 1) * UNIT)
                    V.tensor_tensor(tok_buf[:, :, c], acc[:, ubs[j]], gain_row[:, c].unsqueeze(1).to_broadcast([P, TOK, UNIT]),
                                    ALU.mult).then_inc(s_emptied, 1)

            def post_norm():
                own(V.reduce_sum(stat[:, 0:2], stat[:, 52:60].rearrange("p (t j) -> p t j", t=TOK), AX_X))
                rms_scale(0, TOK, squared=False)
                for tok in range(TOK):
                    V.scalar_tensor_tensor(x[:, tok, :], tok_buf[:, tok, :], stat[:, 4 + tok:5 + tok], x[:, tok, :],
                                           ALU.mult, ALU.add).then_inc(s_x_tile, 1)

            def post_norm_rows(beside):
                dve.wait_ge(s_gain, gain.next())
                for tok in range(TOK):
                    low(beside)
                    rms_scale(tok)
                    own(V.scalar_tensor_tensor(tok_buf[:, tok, :], tok_buf[:, tok, :], stat[:, 4 + tok:5 + tok], gain_row, ALU.mult, ALU.mult))
                    ins = V.tensor_tensor(x[:, tok, :], x[:, tok, :], tok_buf[:, tok, :], ALU.add)
                    ins.then_inc(s_x_tile, 1)

            def nudge_act():
                dve.sem_inc(s_for_act, 1)
                for_act.next()

            def softmax(scale):
                for _ in range(4):
                    bank()
                scores = work[:, :, :].rearrange("p b (q s) -> p (b q) s", q=2)
                own(V.reduce_max(stat[:, 32:40], scores, AX_X))
                to_act(V.tensor_scalar(stat[:, 16:24], stat[:, 32:40], -scale, None, ALU.mult))
                act_result()
                own(V.reciprocal(stat[:, 40:48], stat[:, 24:32]))
                drain(V.tensor_tensor(prob, prob, bc(stat[:, 40:48], SEQ), ALU.mult), 4)
                for _ in range(4):
                    bank()
                drain(V.tensor_copy(probT, work[:, :, :]), 4)

            own(V.memset(prow, 0.0))
            dve.sem_inc(s_rows_zero, 1)
            own(V.memset(lora_in[:, :, :, :], 0.0))

            def parameter_columns():
                dve.wait_ge(s_const, 16)
                for l in range(DEPTH):
                    for g in range(2):
                        n, o = GROUP_ROWS[g], GROUP_ROWS[0] * g
                        drain(V.tensor_copy(cols[:, l, o:o + n], bank()[:, 0:n]), wait=True)
                    own(V.tensor_tensor(cols_mix[:, l, :], colv(l, "rw_mu_prev", 28), colv(l, "rw_mu_next", 28), ALU.add))
                    own(V.tensor_scalar(cols_mix[:, l, :], cols_mix[:, l, :], -1.0, 1.0, ALU.mult, ALU.add))
                    own(V.tensor_scalar(cols_ka[:, l, :], colv(l, "rw_k_a", PAIRS), -1.0, 1.0, ALU.mult, ALU.add))

            carry = cst("carry")
            for l in range(DEPTH):
                keys, values_in = MEM_UNITS[l]
                if l == 0:
                    dve.wait_ge(s_mem, 16)
                    dve.wait_ge(s_x, 16)
                    nudge_act()
                    low(AHEAD)
                    norm_rows(tok_buf)
                    parameter_columns()
                    turned_rows(colv(l, "n_mem", KD), keep=True)
                    low(32)
                else:
                    low(16 - 8)
                    norm_rows(x)
                    low(16)
                for b in range(2):
                    src = bank().rearrange("p (j n) -> p j n", j=2)
                    if b:
                        V.tensor_copy(memk[:, 2 * b:2 * b + 1, :], src[:, 0:1, :]).then_inc(s_rows_free, 1)
                        drain(V.tensor_copy(memk[:, 2 * b + 1:2 * b + 2, :], src[:, 1:2, :]))
                    else:
                        drain(V.tensor_copy(memk[:, 0:2, :], src))
                dve.wait_ge(s_emptied, emptied_now(l, "memv"))
                to_act(V.tensor_copy(memv[:, :, :], rows[:, values_in, :, :]))

                if l == 0:
                    norm_rows(x)
                    dve.wait_ge(s_mem_saved, 16)
                dve.wait_ge(s_for_pe, for_pe.at())
                dve.sem_inc(s_x_idle, 1)
                turned_rows(colv(l, "n_mix_pre", KD))

                def shifted(src, t, w, mix, prev, nxt):
                    dst = t
                    own(V.tensor_scalar(dst, src, mix, None, ALU.mult))
                    own(V.scalar_tensor_tensor(dst[:, 1:SEQ], src[:, 0:SEQ - 1], prev, dst[:, 1:SEQ], ALU.mult, ALU.add))
                    return V.scalar_tensor_tensor(dst[:, 0:SEQ - 1], src[:, 1:SEQ], nxt, dst[:, 0:SEQ - 1], ALU.mult, ALU.add)

                with repeat(dve, 3, {full: 4, drained: 4, step: 16, split: 32}) as i:
                    for u in range(2):
                        low((22, 10)[u])
                        for b in range(2):
                            src = bank()
                            for j in range(2):
                                k = u * 4 + b * 2 + j
                                zt = streams[:, 0:5:2, k * SEQ:(k + 1) * SEQ]
                                pv = colv(l, "rw_mu_prev", 24).rearrange("p (i k) -> p k i", k=8)[:, k]
                                nx = colv(l, "rw_mu_next", 24).rearrange("p (i k) -> p k i", k=8)[:, k]
                                mx = cols_mix[:, l, 0:24].rearrange("p (i k) -> p k i", k=8)[:, k]
                                ins = shifted(src[:, j * SEQ:(j + 1) * SEQ], zt[:, i, :], P, mx[:, bass.ts(i, 1)], pv[:, bass.ts(i, 1)], nx[:, bass.ts(i, 1)])
                                if j:
                                    drain(ins)
                                elif b:
                                    ins.then_inc(s_rows_free, 1)
                low(22)
                for b in range(2):
                    src = bank()
                    for j in range(2):
                        k = 24 + 2 * b + j
                        w = LORA_W[2 * b + j]
                        ins = shifted(src[0:w, j * SEQ:(j + 1) * SEQ], low_in[0:w, k - 24, :], w, cols_mix[0:w, l, k:k + 1],
                                      col(l, "rw_mu_prev", k)[0:w], col(l, "rw_mu_next", k)[0:w])
                        if j:
                            drain(ins, wait=True)
                        elif b:
                            ins.then_inc(s_rows_free, 1)
                for u in range(3):
                    low((16, 16, 4)[u])
                    for b in range(2 if u < 2 else 1):
                        src = bank()
                        dst = qk[:, 2 * u + b]
                        if b or u == 2:
                            V.tensor_copy(dst[:, 0:1, :], src[:, 0:SEQ].rearrange("p (j n) -> p j n", j=1)).then_inc(s_rows_free, 1)
                            drain(V.tensor_copy(dst[:, 1:2, :], src[:, SEQ:2 * SEQ].rearrange("p (j n) -> p j n", j=1)), wait=True, aligned=u == 2)
                        else:
                            drain(V.tensor_copy(dst, src.rearrange("p (j n) -> p j n", j=2)), wait=True)
                own(V.tensor_copy(v_at, rows[:, 1, :, AT_KV:2 * AT_KV]))
                dve.wait_ge(s_used, slab_now(l, "z"))
                own(V.tensor_tensor(opT[:, :, :], opT_parts[:, :, :].bitcast(F32), op_high_f32, ALU.add))
                V.tensor_copy(of_head[0:QK_HEADS], ident[0:QK_HEADS, 0:QK_HEADS].unsqueeze(2).to_broadcast([QK_HEADS, QK_HEADS, HEAD]))
                to_pe(V.tensor_tensor(qk_sq, qk, qk, ALU.mult))
                roots = qk_root.rearrange("p t h -> p (t h)")
                src = bank()
                ins = V.tensor_scalar(roots, src[:, 0:TOK * QK_HEADS], 1.0 / HEAD, EPS, ALU.mult, ALU.add)
                drain(ins, wait=True)
                nudge_act()
                act_result()
                to_pe(V.reciprocal(roots, roots))
                drain(V.tensor_copy(qk_rootT[0:QK_HEADS, :], bank()[0:QK_HEADS, 0:SEQ]))

                def normed(i):
                    src = bank().rearrange("p (j n) -> p j n", j=2)
                    ins = V.scalar_tensor_tensor(qk_sq[:, i], qk[:, i], col(l, "qk_norm", i), src, ALU.mult, ALU.mult)
                    drain(ins, wait=True)
                    dve.sem_inc(s_for_pe, 1)
                    for_pe.next()

                def rotated(i):
                    b2 = lambda t: t.unsqueeze(1).to_broadcast([P, 2, SEQ])
                    own(V.tensor_tensor(qk[:, i], qk_sq[:, i], b2(cst("cos")), ALU.mult))
                    src = bank().rearrange("p (j n) -> p j n", j=2)
                    drain(V.tensor_tensor(sq_tmp, src, b2(cst("sin")), ALU.mult), wait=True)
                    own(V.tensor_tensor(qk[:, i], qk[:, i], sq_tmp, ALU.add))
                normed(0)
                for i in range(1, 5):
                    normed(i)
                    rotated(i - 1)
                rotated(4)
                for g in range(AT_KV_HEADS):
                    for half in range(2):
                        s0 = (g % 2) * HEAD
                        ins = V.tensor_copy(k_both[half * HEAD:(half + 1) * HEAD, g, :], qk[s0:s0 + HEAD, 4, g // 2, :])
                own(ins)
                dve.sem_inc(s_for_pe, 1)
                for_pe.next()

                def maxima():
                    dve.wait_ge(s_scores, scored.next())
                    own(V.reduce_max(stat[:, 32:40], psum[:, 0:4, :].rearrange("p b (q s) -> p (b q) s", q=2), AX_X))
                    to_act(V.tensor_scalar(stat[:, 16:24], stat[:, 32:40], -HEAD ** -0.5, None, ALU.mult))
                maxima()
                for g in range(AT_KV_HEADS):
                    dve.wait_ge(s_exps, exps.next())
                    own(V.reciprocal(stat[:, 40:48], stat[:, 24:32]))
                    to_pe(V.tensor_tensor(probs[g % 2], probs[g % 2], bc(stat[:, 40:48], SEQ), ALU.mult))
                    if g < AT_KV_HEADS - 1:
                        maxima()
                    for b in range(4):
                        drain(V.tensor_copy(probT[:, b, :], bank()))
                    drain(V.tensor_copy(y_at[:, 2 * g:2 * g + 2, :].rearrange("p t n -> p (t n)"), bank()),
                          aligned=g == AT_KV_HEADS - 1)
                if l:
                    dve.sem_inc(s_for_pe, 1)
                    for_pe.next()
                    drain(V.tensor_copy(v_low, bank()[0:V_LORA, 0:SEQ]), aligned=True)
                nudge_act()
                for d in range(2):
                    r = slice(d * 64, (d + 1) * 64)
                    own(V.tensor_copy(lora_in[r, 1, d, :], low_in[r, 1, :]))
                own(V.memset(view(0, 4096), 0.0))
                act_result()
                dve.sem_inc(s_for_pe, 1)
                for_pe.next()
                dve.sem_inc(s_lw_free, 1)
                with repeat(dve, PAIRS, {scan.tally: PER_PAIR, for_pe: 4, for_act: 8, from_act: 3, step: N_STEP[l]}) as i:
                    start = scan.tally.count
                    rT, kT, vT = r_all[:, i, :], k_all[:, i, :], v_all[:, i, :]

                    def pcol(name, d=None):
                        v = colv(l, name, PAIRS) if d is None else cols[:, l, PCOL[name] + d * PAIRS:PCOL[name] + (d + 1) * PAIRS]
                        return v[:, bass.ts(i, 1)]
                    flat = lambda t: t.rearrange("p a b -> p (a b)")
                    two = lambda t: t.unsqueeze(1).to_broadcast([P, 2, SEQ])
                    ch = lambda t: t.rearrange("p (c n) -> p c n", c=NCH)
                    for kind, name in enumerate(("rw_w0", "rw_a0")):
                        src = sbank()
                        for d in range(2):
                            ins = V.tensor_scalar(sig[:, 2 * kind + d, :], src[:, d * SEQ:(d + 1) * SEQ], pcol(name, d), None, ALU.add)
                        if l or kind == 0:
                            sdrain(ins)
                        else:
                            sdrain(ins, wait=True)
                    if l:
                        sdrain(V.tensor_scalar(tmp2[:, :], sbank()[:, 0:SEQ], pcol("rw_v0"), None, ALU.add), wait=True)
                    nudge_act()
                    g_ready = skipped()
                    kk = flat(Yc[:, :, :])
                    own(V.tensor_scalar(kk, kT, pcol("rw_k_k"), None, ALU.mult))
                    V.tensor_tensor(tmp[:, :], kk, kk, ALU.mult)
                    act_result()
                    own(V.tensor_tensor_scan(inc[:, 0, :], carry, sig[:, 0, :], 0.0, ALU.mult, ALU.add))
                    own(V.tensor_tensor_scan(p_inc[:, 0, :], carry, sig[:, 1, :], 0.0, ALU.mult, ALU.add))
                    total = ch(p_inc[:, 0, :])[:, :, CHUNK - 1:CHUNK].to_broadcast([P, NCH, CHUNK])
                    own(V.tensor_tensor(ch(exc[:, 1, :]), total, ch(p_inc[:, 0, :]), ALU.subtract))
                    V.tensor_tensor(exc[:, 0, :], inc[:, 0, :], sig[:, 0, :], ALU.subtract)
                    to_act(V.tensor_tensor(inc[:, 1, :], exc[:, 1, :], sig[:, 1, :], ALU.add))
                    if l:
                        own(V.tensor_tensor(v_cur[:, :], v_first[:, :, :][:, i, :], vT, ALU.subtract))
                        own(V.tensor_tensor(v_cur[:, :], v_cur[:, :], tmp2[:, :], ALU.mult))
                        own(V.tensor_tensor(v_cur[:, :], v_cur[:, :], vT, ALU.add))
                    else:
                        V.tensor_copy(v_cur[:, :], vT)
                        own(V.tensor_copy(v_first[:, :, :][:, i, :], vT))
                    own(V.tensor_scalar(flat(kd), flat(sig[:, 2:4, :]), pcol("rw_k_a"), cols_ka[:, l, :][:, bass.ts(i, 1)], ALU.mult, ALU.add))
                    own(V.tensor_tensor(kd, kd, two(kT), ALU.mult))
                    own(V.tensor_tensor(tmp2[:, :], kd[:, 0, :], kd[:, 1, :], ALU.add))
                    to_pe(V.scalar_tensor_tensor(tmp2[:, :], rT, pcol("rw_r_k"), tmp2[:, :], ALU.mult, ALU.mult))
                    norms = skipped()
                    shave(norms)
                    dve.sem_inc(s_lw_free, 1)
                    own(V.tensor_scalar(tmp[:, :], tmp[:, :], 1e-12, None, ALU.max))
                    own(V.reciprocal(tmp[:, :], tmp[:, :]))
                    own(V.scalar_tensor_tensor(tmp[:, :], kk, -1.0, tmp[:, :], ALU.mult, ALU.mult))
                    own(V.scalar_tensor_tensor(sig[:, 2:4, :], two(tmp[:, :]), -1.0, sig[:, 2:4, :], ALU.mult, ALU.mult))
                    sdrain(V.tensor_tensor(kT, sbank()[:, 0:SEQ], v_cur[:, :], ALU.mult))
                    v_ready = skipped()
                    act_result()
                    to_act(V.tensor_tensor(sig[:, 2:4, :], sig[:, 2:4, :], p_inv, ALU.mult))
                    to_act(V.tensor_tensor(kd, kd, p_inv, ALU.mult))
                    to_act(V.tensor_tensor(p_exc, two(tmp[:, :]), p_exc, ALU.mult))
                    to_act(V.tensor_tensor(inc, two(rT), p_inc, ALU.mult))

                    pair2 = lambda t: t.unsqueeze(2).to_broadcast([P, t.shape[1], 2, HEAD])
                    halves = lambda t: t.rearrange("p c (h n) -> p c h n", h=2)
                    some = lambda m, k: m.rearrange("p (h n) -> p h n", h=2).unsqueeze(1).to_broadcast([P, k, 2, HEAD])
                    row4 = lambda t, k: t.unsqueeze(1).to_broadcast([P, k, HEAD])
                    before = cst("before").rearrange("p (d n) -> p d n", d=2)

                    def expand(dst, src, m=head_ones, k=NCH):
                        return V.tensor_tensor(halves(dst), pair2(src), some(m, k), ALU.mult)
                    for d in range(2):
                        for c2 in range(0, NCH, 2):
                            src = sbank().rearrange("p (j k n) -> p j k n", j=2, k=4)
                            for kind, g, m in ((0, 0, mask[:, d, P:2 * P]), (2, 1, mask[:, d, P:2 * P]), (3, 2, mask[:, d, 0:P])):
                                expand(GT[:, d, c2:c2 + 2, g, :], src[:, :, kind, :], m, 2)
                            sdrain(V.tensor_tensor(AT_c[:, d, c2:c2 + 2, :], src[:, :, 1, :], row4(before[:, d], 2), ALU.mult))
                    src = sbank().rearrange("p (d c n) -> p d c n", d=2, c=NCH)
                    for d in range(2):
                        ins = V.tensor_tensor(A_c[:, d], src[:, d], row4(before[:, 1 - d], NCH), ALU.mult)
                    sdrain(ins, wait=True)
                    dve.sem_inc(s_for_pool, 1)
                    skipped()
                    skipped()
                    skipped()
                    skipped()
                    eight = lambda t: t.rearrange("p d c n -> p (d c) n")
                    in16c = row4(cst("in16_head"), 2 * NCH)
                    V.tensor_tensor(eight(X_c), eight(A_c), in16c, ALU.mult)
                    own(V.tensor_tensor(eight(XT_c), eight(AT_c), in16c, ALU.mult))
                    for d in range(2):
                        expand(XA[:, d], X_c[:, d])
                        if d == 0:
                            to_pe(expand(XTA[:, d], XT_c[:, d]))
                        else:
                            expand(XTA[:, d], XT_c[:, d])
                            to_pe(V.tensor_tensor(eight(E_c), eight(XT_c), row4(cst("ident_head"), 2 * NCH), ALU.add))
                    side = lambda t, k: t[:, k * 256:(k + 1) * 256].rearrange("p (c n) -> p c n", c=NCH)
                    for d in range(2):
                        src = sbank()
                        expand(XB[:, d], side(src, 0))
                        sdrain(expand(XTB[:, d], side(src, 1)), 1)
                    for d in range(2):
                        src = sbank()
                        V.tensor_tensor(E_c[:, d], E_c[:, d], side(src, 0), ALU.add)
                        sdrain(expand(XA[:, d], side(src, 1)), 1)
                        sdrain(expand(XTA[:, d], side(sbank(), 0)))
                    for d in range(2):
                        src = sbank()
                        V.tensor_tensor(E_c[:, d], E_c[:, d], side(src, 0), ALU.add)
                        sdrain(expand(XB[:, d], side(src, 1)))
                    for d in range(2):
                        own(V.tensor_tensor(E_c[:, d], E_c[:, d], side(sbank(), 0), ALU.add))
                        sdrain(expand(EE[:, d], E_c[:, d]))
                    for n in (32, 64):
                        for d in range(2):
                            sdrain(V.tensor_copy(P_c[:, d], side(sbank(), 0)))
                            skipped()
                        for d in range(2):
                            own(V.tensor_tensor(E_c[:, d], E_c[:, d], side(sbank(), 0), ALU.add))
                            sdrain(expand(EE[:, d], E_c[:, d]))
                    for n in range(NCH):
                        at = (n, NCH - 1 - n)
                        skipped()
                        sdrain(V.tensor_copy(flat(Uc[:, :, :]), sbank()[:, 0:P]))
                        if n < NCH - 1:
                            src_s, b_s = sbank(), dve_bank[0]
                        src = sbank()
                        if n < NCH - 1:
                            if n:
                                own(V.tensor_tensor(flat(St[:, :, :]), flat(St[:, :, :]), src_s[:, 0:P], ALU.add))
                            for d, c in enumerate(at):
                                end = c * CHUNK + (CHUNK - 1 if d == 0 else 0)
                                s_d = St[:, d, :] if n else src_s[:, d * HEAD:(d + 1) * HEAD]
                                ins = V.tensor_scalar(St[:, d, :], s_d, p_inc[:, d, end:end + 1], None, ALU.mult)
                            ins.then_inc(s_sdrained[b_s], 2)
                        for d, c in enumerate(at):
                            y = src[:, d * HEAD:(d + 1) * HEAD]
                            if n < NCH // 2:
                                ins = V.tensor_copy(Yc[:, c, :], y)
                            else:
                                ins = V.tensor_tensor(Yc[:, c, :], Yc[:, c, :], y, ALU.add)
                        sdrain(ins, wait=n > 0)
                    own(V.reduce_sum(stat[:, 12:16], Yc[:, :, :], AX_X))
                    own(V.tensor_scalar(stat[:, 12:16], stat[:, 12:16], 1.0 / HEAD, None, ALU.mult))
                    own(V.tensor_tensor(Yc[:, :, :], Yc[:, :, :], bc(stat[:, 12:16], HEAD), ALU.subtract))
                    own(V.tensor_tensor(ch(p_inv[:, 0, :]), Yc[:, :, :], Yc[:, :, :], ALU.mult))
                    own(V.reduce_sum(stat[:, 12:16], ch(p_inv[:, 0, :]), AX_X))
                    to_act(V.tensor_scalar(stat[:, 8:12], stat[:, 12:16], 1.0 / HEAD, GN_EPS, ALU.mult, ALU.add))
                    act_result()
                    own(V.reciprocal(stat[:, 12:16], stat[:, 8:12]))
                    to_pe(V.tensor_tensor(Yc[:, :, :], Yc[:, :, :], bc(stat[:, 12:16], HEAD), ALU.mult))
                    shave(skipped())
                    shave(g_ready)
                    own(V.tensor_scalar(tmp[:, :], tmp[:, :], pcol("rw_ln_w"), pcol("rw_ln_b"), ALU.mult, ALU.add))
                    own(V.tensor_tensor(tmp[:, :], tmp[:, :], kT, ALU.add))
                    own(V.tensor_tensor(y_rw[:, i, :], tmp[:, :], g_cur[:, :], ALU.mult))
                    nudge_act()
                    while scan.tally.count - start < PER_PAIR:
                        b, read = scan.now()
                        dve.wait_ge(s_sdrained[b], read)
                        dve.sem_inc(s_sdrained[b], 2)
                        scan.tally.next()
                dve.sem_inc(s_gain_free, 1)
                act_result()
                V.tensor_tensor(tiles8(streams_parts[:, 0, :]), y_rw, op_high_f32[:, 0:PAIRS, :], ALU.subtract)
                V.tensor_tensor(y_at_parts[:, :, :], y_at[:, :, :], op_high_f32[:, PAIRS:2 * PAIRS, :], ALU.subtract).then_inc(s_operand, 1)
                low(AHEAD)
                slab.count = slab_now(l, "gates")
                with repeat(dve, 4, {slab: 16, split: 16, branch: 2, step: 1}) as i:
                    tb_i = tok_buf[:, :, :].rearrange("p t (i n) -> p i t n", i=4)[:, i]
                    gate_a, gate_b = gates[:, 0:4][:, i], gates[:, 4:8][:, i]
                    low(8)
                    dve.wait_ge(s_used, slab.next(8))
                    V.tensor_tensor(tb_i, acc[:, 0], gate_a, ALU.mult).then_inc(s_branch, 1)
                    branch.next()
                    low(8)
                    dve.wait_ge(s_used, slab.next(8))
                    V.tensor_tensor(gate_b, acc[:, 1], gate_b, ALU.mult).then_inc(s_branch, 1)
                    dve.wait_ge(s_branch, branch.next())
                    own(V.tensor_tensor(tb_i, tb_i, gate_b, ALU.add))
                dve.sem_inc(s_x_idle, 1)
                for tok in range(TOK):
                    dve.sem_inc(s_for_pe, 1)
                    for_pe.next()
                turned_rows()
                units_by_gains(16, (0, 1, 0, 1))
                dve.wait_ge(s_x_back, 16 * (l + 1))
                post_norm()
                norm_rows(x)
                turned_rows(colv(l, "n_x_pre", KD))
                low(16 - AHEAD)
                for b in range(2):
                    src = bank().rearrange("p (j n) -> p j n", j=2)
                    if b:
                        V.tensor_copy(x_q[:, 2:3, :], src[:, 0:1, :]).then_inc(s_rows_free, 1)
                        drain(V.tensor_copy(x_q[:, 3:4, :], src[:, 1:2, :]), aligned=True)
                    else:
                        drain(V.tensor_copy(x_q[:, 0:2, :], src))
                dve.sem_inc(s_gain_free, 1)
                softmax(X_HEAD ** -0.5)
                for b2 in range(2):
                    drain(V.tensor_copy(x_y[:, 2 * b2:2 * b2 + 2, :], bank().rearrange("p (j n) -> p j n", j=2)), aligned=b2 == 1, wait=b2 == 1)
                nudge_act()
                act_result()
                V.tensor_tensor(xy_low, x_y, op_high_f32[:, 0:X_HEADS, :], ALU.subtract).then_inc(s_operand, 1)
                low(AHEAD)
                units_by_gains(4, (1, 0, 1, 0))
                post_norm()
                norm_rows(x)
                turned_rows(colv(l, "n_ffn_pre", KD))
                dve.sem_inc(s_gain_free, 1)
                slab.count = slab_now(l, "ffn")
                for part, tiles in enumerate(FF_PARTS):
                    for half in range(0, tiles, 8):
                        b = half // 8
                        quads = lambda t: t.rearrange("p (i j t) n -> p j i t n", j=2, t=2)
                        with repeat(dve, min(8, tiles - half) // 4, {slab: 32, split: 32, full: 4, drained: 4, from_act: 2, step: 2}) as i:
                            for j, ub in enumerate((1, 0)):
                                low((16, 10)[j])
                                act_result()
                                slab.next(16)
                                V.tensor_tensor(rows[:, ub, :, 0:256], acc[:, ub, :, 256:512], rows[:, ub, :, 0:256], ALU.mult).then_inc(s_emptied, 1)
                                if j == 0:
                                    low(6)
                                src = bank().rearrange("p (t n) -> p t n", t=2)
                                own(V.tensor_copy(quads(hid_high[b])[:, j][:, i], src))
                                dve.sem_inc(s_rows_free, 1)
                                drain(V.tensor_tensor(quads(hid_low[b])[:, j][:, i], src, quads(hid_high_f32[b])[:, j][:, i], ALU.subtract), aligned=j == 1)

                    def down(i, ahead=0, between=None):
                        for j, ub in enumerate((1, 0)):
                            low(tiles - (ahead if j else 0))
                            if j and between:
                                between()
                            dve.wait_ge(s_used, slab.next(tiles))
                            c = tok_buf[:, :, :].rearrange("p t (i j n) -> p j i t n", i=2, j=2)[:, j][:, i]
                            if part == 0:
                                V.tensor_copy(c, acc[:, ub]).then_inc(s_emptied, 1)
                            else:
                                V.tensor_tensor(c, c, acc[:, ub], ALU.add).then_inc(s_emptied, 1)
                    if part == len(FF_PARTS) - 1:
                        if l < DEPTH - 1:
                            dve.sem_inc(s_opT_free, 1)
                            down(0)
                            dve.wait_ge(s_mem_back, 16 * (l + 1))
                            own(V.tensor_tensor(opT[:, :, :], opT[:, :, :], bc(colv(l + 1, "n_mem", KD), SEQ), ALU.mult))
                            for tok in range(TOK):
                                nudge_act()
                            down(1, between=split_operand)
                        else:
                            down(0)
                            down(1, AHEAD)
                    else:
                        with repeat(dve, 2, {slab: 2 * tiles, split: 2 * tiles, step: 0}) as i:
                            down(i)
                dve.wait_ge(s_emptied, emptied_now(l, "end"))
                nudge_act()
                post_norm_rows(beside=4 if l < DEPTH - 1 else 0)
                dve.wait_ge(s_x_tile, 6 * (l + 1))
            dve.sem_inc(s_out, 1)


MEM_UNITS = [(0, 1)] + [(1, 0)] * (DEPTH - 1)
N_STEP = {0: 30, 1: 32}


def slab_now(l, where):
    before = {"z": 192, "gates": 192 + 128, "ffn": 192 + 128 + 64 + 64 + 16 + 16}[where]
    return l * SLABS + before


SLABS = 192 + 128 + 64 + 64 + 16 + 16 + 16 * 22 + 4 * sum(FF_PARTS)
UNITS = 2 + 10 + 4 + 1 + 4 + 22 + 4 * len(FF_PARTS)


def emptied_now(l, where):
    n = {"memv": 2, "wo": 16, "xo": 21, "end": UNITS}[where]
    return l * UNITS + n


_INS = ["x", "mem", "n_mix_pre", "n_mix_post", "n_x_pre", "n_x_post", "n_ffn_pre", "n_ffn_post", "n_mem", "w_in",
        "rw_mu_prev", "rw_mu_next", "rw_w0", "rw_w_up", "rw_a0", "rw_a_up", "rw_g_up", "rw_v0", "rw_v_down", "rw_v_up",
        "rw_k_k", "rw_k_a", "rw_r_k", "rw_ln_w", "rw_ln_b", "w_rw_out", "at_q_norm", "at_k_norm", "w_at_out", "w_o",
        "x_wq", "x_wkv", "x_wo", "ffn_wg", "ffn_wu", "ffn_wd"]


def kernel(**inputs):
    import numpy as _np
    import concourse.bacc as _bacc
    from concourse import mybir as _mybir
    from concourse.bass_utils import run_bass_kernel_spmd as _run

    nc = _bacc.Bacc("TRN2", target_bir_lowering=False, num_devices=1)
    given = {name: _np.ascontiguousarray(inputs[name]) for name in _INS}
    given["shape_constants"] = shape_constants()
    arrays, aps = {}, {}
    for name, v in given.items():
        arrays[f"in_{name}_dram"] = v
        aps[name] = nc.dram_tensor(f"in_{name}_dram", v.shape, _mybir.dt.from_np(v.dtype), kind="ExternalInput").ap()
    out = nc.dram_tensor("out_0_dram", (1, SEQ, D_MODEL), _mybir.dt.float32, kind="ExternalOutput").ap()
    encoder_kernel(nc, aps, out)
    r = _run(nc, [arrays], core_ids=[0])
    return r.results[0]["out_0_dram"]
```
